# Optimizing a Trainium2 kernel written in Bass

```python
import jax, jax.numpy as jnp
from jax import lax
import numpy as np

D_MODEL = 1024
BATCH = 1
SEQ = 256
DEPTH = 1

CTX_LEN = 256
GRID_W = 64
D_MIX = 1024
HEAD_DIM = 64
N_Q_HEADS = 8
N_KV_HEADS = 2
Q_PER_KV = N_Q_HEADS // N_KV_HEADS
D_ATTN = N_Q_HEADS * HEAD_DIM
D_KV = N_KV_HEADS * HEAD_DIM
N_GM_GROUPS = 8
GM_GROUP_DIM = 64
D_GM = N_GM_GROUPS * GM_GROUP_DIM
CHUNK = 128
Q_BLOCK = 128
D_IN = D_ATTN + 2 * D_KV + 2 * D_GM
ROPE_THETA = 10000.0
N_EXPERTS = 16
CAPACITY_FACTOR = 2
EXPERT_FF = 2048
EPS = 1e-6


def rmsnorm(x, g):
    xf = x.astype(jnp.float32)
    y = xf * lax.rsqrt(jnp.mean(xf * xf, axis=-1, keepdims=True) + EPS)
    return (y * g.astype(jnp.float32)).astype(x.dtype)

def adaln(cvec, w_mod, b_mod):
    m = jax.nn.silu(cvec) @ w_mod + b_mod
    return jnp.split(m, 6, axis=-1)

def axial_rope(row, col):
    n_freq = HEAD_DIM // 4
    inv = ROPE_THETA ** (-jnp.arange(n_freq, dtype=jnp.float32) / n_freq)
    ang = jnp.concatenate([row[:, None].astype(jnp.float32) * inv,
                           col[:, None].astype(jnp.float32) * inv], axis=-1)
    return jnp.cos(ang), jnp.sin(ang)

def apply_rope(x, cos, sin):
    shape = (cos.shape[0],) + (1,) * (x.ndim - 3) + (cos.shape[-1],)
    cos = cos.reshape(shape).astype(x.dtype)
    sin = sin.reshape(shape).astype(x.dtype)
    x1, x2 = jnp.split(x, 2, axis=-1)
    return jnp.concatenate([x1 * cos - x2 * sin, x1 * sin + x2 * cos], axis=-1)

def modulate(x, g, shift, scale):
    return rmsnorm(x, g) * (1 + scale) + shift

def split_in_proj(w_in):
    return jnp.split(w_in, [D_ATTN, D_ATTN + 2 * D_KV], axis=1)

def queries(h, w_q, q_gain):
    b, n = h.shape[:2]
    return rmsnorm((h @ w_q).reshape(b, n, N_KV_HEADS, Q_PER_KV, HEAD_DIM), q_gain)

def keys_values(h, w_kv, k_gain):
    b, n = h.shape[:2]
    k, v = jnp.split(h @ w_kv, 2, axis=-1)
    k = rmsnorm(k.reshape(b, n, N_KV_HEADS, HEAD_DIM), k_gain)
    return k, v.reshape(b, n, N_KV_HEADS, HEAD_DIM)

def gqa_attend(q, k, v):
    b, nq = q.shape[:2]
    scale = HEAD_DIM ** -0.5

    def block(qb):
        s = jnp.einsum('bqkgd,bskd->bkgqs', qb, k).astype(jnp.float32) * scale
        p = jax.nn.softmax(s, axis=-1).astype(v.dtype)
        return jnp.einsum('bkgqs,bskd->bqkgd', p, v)

    nb = nq // Q_BLOCK
    qb = jnp.moveaxis(q.reshape(b, nb, Q_BLOCK, N_KV_HEADS, Q_PER_KV, HEAD_DIM), 1, 0)
    o = lax.map(block, qb)
    return jnp.moveaxis(o, 0, 1).reshape(b, nq, D_ATTN)

def spatial_gating(h, w_gm, v_gain, w_s, b_s):
    b, n = h.shape[:2]
    u, vv = jnp.split(jax.nn.gelu(h @ w_gm, approximate=False), 2, axis=-1)
    vv = rmsnorm(vv, v_gain).reshape(b, n // CHUNK, CHUNK, N_GM_GROUPS, GM_GROUP_DIM)
    mixed = jnp.einsum('gij,bcjgd->bcigd', w_s, vv) + b_s.T[:, :, None]
    return u * mixed.reshape(b, n, D_GM)

def expert_choice_ffn(h, w_router, w1, w3, w2):
    n, d = h.shape[1], h.shape[2]
    cap = CAPACITY_FACTOR * n // N_EXPERTS
    aff = jax.nn.softmax((h @ w_router).astype(jnp.float32), axis=-1)
    gate, idx = lax.top_k(jnp.swapaxes(aff, 1, 2), cap)
    xe = jax.vmap(lambda hb, ib: hb[ib])(h, idx)
    hid = jax.nn.silu(jnp.einsum('becd,edf->becf', xe, w1)) * jnp.einsum('becd,edf->becf', xe, w3)
    ye = jnp.einsum('becf,efd->becd', hid, w2) * gate[..., None].astype(h.dtype)

    def scatter(yb, ib):
        return jnp.zeros((n, d), h.dtype).at[ib.reshape(-1)].add(yb.reshape(-1, d))

    return jax.vmap(scatter)(ye, idx)

def hybrid_layer(xl, xc, c, c_ctx, cos, sin, w_mod, b_mod, g_mix, g_ffn, w_in, q_gain, k_gain,
                 v_gain, w_s, b_s, w_out, w_router, w1, w3, w2, update_ctx):
    sh1, sc1, gt1, sh2, sc2, gt2 = [m[:, None, :] for m in adaln(c, w_mod, b_mod)]
    csh1, csc1, cgt1, csh2, csc2, cgt2 = adaln(c_ctx, w_mod, b_mod)
    w_q, w_kv, w_gm = split_in_proj(w_in)

    hl = modulate(xl, g_mix, sh1, sc1)
    hc = modulate(xc, g_mix, csh1, csc1)
    kc, vc = keys_values(hc, w_kv, k_gain)
    ql = apply_rope(queries(hl, w_q, q_gain), cos, sin)
    kl, vl = keys_values(hl, w_kv, k_gain)
    kl = apply_rope(kl, cos, sin)
    k_all = jnp.concatenate([kl, kc], axis=1)
    v_all = jnp.concatenate([vl, vc], axis=1)
    mix_l = jnp.concatenate([gqa_attend(ql, k_all, v_all),
                             spatial_gating(hl, w_gm, v_gain, w_s, b_s)], axis=-1)
    xl_new = xl + gt1 * (mix_l @ w_out)

    xl_new = xl_new + gt2 * expert_choice_ffn(modulate(xl_new, g_ffn, sh2, sc2), w_router, w1, w3, w2)

    if update_ctx:
        qc = queries(hc, w_q, q_gain)
        mix_c = jnp.concatenate([gqa_attend(qc, kc, vc),
                                 spatial_gating(hc, w_gm, v_gain, w_s, b_s)], axis=-1)
        xc = xc + cgt1 * (mix_c @ w_out)
        xc = xc + cgt2 * expert_choice_ffn(modulate(xc, g_ffn, csh2, csc2), w_router, w1, w3, w2)
    return xl_new, xc

def first_inputs(seed: int = 0) -> dict:
    key = jax.random.key(seed)
    ks = jax.random.split(key, 21)
    f32 = jnp.float32
    L = DEPTH

    def nrm(k, shape, s):
        return jax.random.normal(k, shape, f32) * s

    return {
        "x": nrm(ks[0], (BATCH, SEQ, D_MODEL), 1.0),
        "c": nrm(ks[1], (BATCH, D_MODEL), 1.0),
        "ctx": nrm(ks[2], (BATCH, CTX_LEN, D_MODEL), 1.0),
        "c_ctx": nrm(ks[3], (D_MODEL,), 1.0),
        "w_mod": nrm(ks[4], (L, D_MODEL, 6 * D_MODEL), D_MODEL ** -0.5),
        "b_mod": nrm(ks[5], (L, 6 * D_MODEL), 0.02),
        "g_mix": 1.0 + nrm(ks[6], (L, D_MODEL), 0.02),
        "g_ffn": 1.0 + nrm(ks[7], (L, D_MODEL), 0.02),
        "w_in": nrm(ks[8], (L, D_MODEL, D_IN), D_MODEL ** -0.5),
        "q_gain": 1.0 + nrm(ks[9], (L, HEAD_DIM), 0.02),
        "k_gain": 1.0 + nrm(ks[10], (L, HEAD_DIM), 0.02),
        "v_gain": 1.0 + nrm(ks[11], (L, D_GM), 0.02),
        "w_s": nrm(ks[12], (L, N_GM_GROUPS, CHUNK, CHUNK), CHUNK ** -0.5),
        "b_s": 1.0 + nrm(ks[13], (L, N_GM_GROUPS, CHUNK), 0.02),
        "w_out": nrm(ks[14], (L, D_MIX, D_MODEL), D_MIX ** -0.5),
        "w_router": nrm(ks[15], (L, D_MODEL, N_EXPERTS), D_MODEL ** -0.5),
        "w1": nrm(ks[16], (L, N_EXPERTS, D_MODEL, EXPERT_FF), D_MODEL ** -0.5),
        "w3": nrm(ks[17], (L, N_EXPERTS, D_MODEL, EXPERT_FF), D_MODEL ** -0.5),
        "w2": nrm(ks[18], (L, N_EXPERTS, EXPERT_FF, D_MODEL), EXPERT_FF ** -0.5),
        "g_final": 1.0 + nrm(ks[19], (D_MODEL,), 0.02),
    }

def first_block(x, c, ctx, c_ctx, w_mod, b_mod, g_mix, g_ffn, w_in, q_gain, k_gain, v_gain,
              w_s, b_s, w_out, w_router, w1, w3, w2, g_final):
    n_lat = x.shape[1]
    rows = n_lat // GRID_W
    row = jnp.repeat(jnp.arange(rows), GRID_W)
    col = jnp.tile(jnp.arange(GRID_W), rows)
    cos, sin = axial_rope(row, col)
    xl, xc = x, ctx
    for layer in range(DEPTH):
        xl, xc = hybrid_layer(xl, xc, c, c_ctx, cos, sin, w_mod[layer], b_mod[layer], g_mix[layer],
                              g_ffn[layer], w_in[layer], q_gain[layer], k_gain[layer], v_gain[layer],
                              w_s[layer], b_s[layer], w_out[layer], w_router[layer], w1[layer],
                              w3[layer], w2[layer], update_ctx=layer + 1 < DEPTH)
    return rmsnorm(xl, g_final)


FF_HALF = 2816
F_GROUPS = 4
F_GROUP_DIM = 128
F_WIDTH = F_GROUPS * F_GROUP_DIM
M_HEADS = 4
M_HEAD_DIM = 256
M_WIDTH = M_HEADS * M_HEAD_DIM
CONV_K = 3
N_ADA = 9

COL_F = 0
COL_Q = COL_F + F_WIDTH
COL_K = COL_Q + M_WIDTH
COL_V = COL_K + M_WIDTH
COL_O = COL_V + M_WIDTH
COL_GATES = COL_O + M_WIDTH
COL_BR = COL_GATES + 4 * M_HEADS
IN_WIDTH = COL_BR + 2 * D_MODEL


def rmsnorm_2(x, g):
    xf = x.astype(jnp.float32)
    y = xf * lax.rsqrt(jnp.mean(xf * xf, axis=-1, keepdims=True) + EPS)
    return (y * g.astype(jnp.float32)).astype(x.dtype)

def modulate_2(x, shift, scale):
    return x * (1 + scale) + shift

def ada_params(cvec, w, b):
    m = jax.nn.silu(cvec) @ w + b
    return m.reshape(cvec.shape[0], N_ADA, 1, D_MODEL)

def swiglu(u, w13, w2):
    a, b = jnp.split(u @ w13, 2, axis=-1)
    return (jax.nn.silu(a) * b) @ w2

def half_ffn(h, shift, scale, gate, g_pre, g_post, w13, w2):
    u = modulate_2(rmsnorm_2(h, g_pre), shift, scale)
    return h + 0.5 * gate * rmsnorm_2(swiglu(u, w13, w2), g_post)

def dwconv(x, w, b):
    y = lax.conv_general_dilated(
        x, w[:, None, :].astype(x.dtype), window_strides=(1,),
        padding=[(CONV_K // 2, CONV_K // 2)],
        dimension_numbers=("NWC", "WIO", "NWC"),
        feature_group_count=x.shape[-1])
    return y + b

def to_heads(x):
    B, T, _ = x.shape
    return x.reshape(B, T, M_HEADS, M_HEAD_DIM).transpose(0, 2, 1, 3)

def fourier_latent(xf):
    B, T, _ = xf.shape
    rows = T // GRID_W
    z = xf.astype(jnp.float32).reshape(B, rows, GRID_W, F_GROUPS, F_GROUP_DIM)
    y = jnp.fft.fftn(z, axes=(1, 2, 4), norm="ortho").real
    return y.reshape(B, T, F_WIDTH).astype(xf.dtype)

def fourier_context(xf):
    B, T, _ = xf.shape
    z = xf.astype(jnp.float32).reshape(B, T, F_GROUPS, F_GROUP_DIM)
    y = jnp.fft.fftn(z, axes=(1, 3), norm="ortho").real
    return y.reshape(B, T, F_WIDTH).astype(xf.dtype)

def project(u, w_in, b_in, conv_w, conv_b):
    B, T, _ = u.shape
    p = u @ w_in + b_in
    xf = p[..., COL_F:COL_Q]
    qk = jax.nn.silu(dwconv(p[..., COL_Q:COL_V], conv_w, conv_b))
    q = to_heads(qk[..., :M_WIDTH])
    k = to_heads(qk[..., M_WIDTH:])
    v = to_heads(p[..., COL_V:COL_O])
    o = p[..., COL_O:COL_GATES]
    gates = p[..., COL_GATES:COL_BR].astype(jnp.float32)
    gates = gates.reshape(B, T, 4, M_HEADS).transpose(2, 0, 3, 1)
    gate_pre = (gates[0], jax.nn.log_sigmoid(gates[1]), gates[2], jax.nn.log_sigmoid(gates[3]))
    g_f = p[..., COL_BR:COL_BR + D_MODEL]
    g_m = p[..., COL_BR + D_MODEL:]
    return xf, q, k, v, o, gate_pre, g_f, g_m

def mlstm_scan(q, k, v, li, lf, state):
    B, H, T, DK = q.shape
    NC = T // CHUNK

    def chunks(a):
        a = a.astype(jnp.float32).reshape(B, H, NC, CHUNK, *a.shape[3:])
        return jnp.moveaxis(a, 2, 0)

    qc, kc, vc, lic, lfc = map(chunks, (q, k * (DK ** -0.5), v, li, lf))
    lower = jnp.tril(jnp.ones((CHUNK, CHUNK), dtype=bool))

    def step(carry, inp):
        C, n, m = carry
        qx, kx, vx, lix, lfx = inp
        b = jnp.cumsum(lfx, axis=-1)
        dmat = b[..., :, None] - b[..., None, :] + lix[..., None, :]
        dmat = jnp.where(lower, dmat, -jnp.inf)
        inter = b + m[..., None]
        m_t = jnp.maximum(inter, jnp.max(dmat, axis=-1))
        w = jnp.exp(dmat - m_t[..., None])
        a = jnp.exp(inter - m_t)
        s = jnp.einsum("bhtd,bhsd->bhts", qx, kx) * w
        num = a[..., None] * jnp.einsum("bhtd,bhde->bhte", qx, C) + jnp.einsum("bhts,bhse->bhte", s, vx)
        den = a * jnp.einsum("bhtd,bhd->bht", qx, n) + jnp.sum(s, axis=-1)
        h = num / jnp.maximum(jnp.abs(den), jnp.exp(-m_t))[..., None]
        bL = b[..., -1]
        g = bL[..., None] - b + lix
        m_new = jnp.maximum(bL + m, jnp.max(g, axis=-1))
        decay = jnp.exp(bL + m - m_new)
        wk = jnp.exp(g - m_new[..., None])
        C_new = decay[..., None, None] * C + jnp.einsum("bhsd,bhse->bhde", kx * wk[..., None], vx)
        n_new = decay[..., None] * n + jnp.einsum("bhs,bhsd->bhd", wk, kx)
        return (C_new, n_new, m_new), h

    state_out, hs = lax.scan(step, state, (qc, kc, vc, lic, lfc))
    h = jnp.moveaxis(hs, 0, 2).reshape(B, H, T, -1)
    return h.astype(q.dtype), state_out

def bidir_mlstm(q, k, v, gate_pre, state_f, state_b):
    li_f, lf_f, li_b, lf_b = gate_pre
    h_f, s_f = mlstm_scan(q, k, v, li_f, lf_f, state_f)
    flip = lambda a: jnp.flip(a, axis=2)
    h_b, s_b = mlstm_scan(flip(q), flip(k), flip(v), flip(li_b), flip(lf_b), state_b)
    return h_f + flip(h_b), s_f, s_b

def merge(y_fourier, h, o, g_f, g_m, head_g, w_four, w_mproj, w_out):
    B, H, T, dh = h.shape
    hn = rmsnorm_2(h.transpose(0, 2, 1, 3), head_g.reshape(M_HEADS, M_HEAD_DIM)).reshape(B, T, M_WIDTH)
    hm = jax.nn.sigmoid(o) * hn
    y = jax.nn.sigmoid(g_f) * (y_fourier @ w_four) + jax.nn.sigmoid(g_m) * (hm @ w_mproj)
    return y @ w_out

def token_mixing(h_lat, h_ctx, mod_l, mod_c, g_pre, g_post, w_in, b_in, conv_w, conv_b,
                 head_g, w_four, w_mproj, w_out, update_ctx):
    sh_l, sc_l, gt_l = mod_l
    sh_c, sc_c, gt_c = mod_c
    pl = project(modulate_2(rmsnorm_2(h_lat, g_pre), sh_l, sc_l), w_in, b_in, conv_w, conv_b)
    pc = project(modulate_2(rmsnorm_2(h_ctx, g_pre), sh_c, sc_c), w_in, b_in, conv_w, conv_b)
    B = h_ctx.shape[0]
    zero = (jnp.zeros((B, M_HEADS, M_HEAD_DIM, M_HEAD_DIM), jnp.float32),
            jnp.zeros((B, M_HEADS, M_HEAD_DIM), jnp.float32),
            jnp.zeros((B, M_HEADS), jnp.float32))
    h_c, s_f, s_b = bidir_mlstm(pc[1], pc[2], pc[3], pc[5], zero, zero)
    h_l, _, _ = bidir_mlstm(pl[1], pl[2], pl[3], pl[5], s_f, s_b)
    out_l = merge(fourier_latent(pl[0]), h_l, pl[4], pl[6], pl[7], head_g, w_four, w_mproj, w_out)
    new_lat = h_lat + gt_l * rmsnorm_2(out_l, g_post)
    new_ctx = None
    if update_ctx:
        out_c = merge(fourier_context(pc[0]), h_c, pc[4], pc[6], pc[7], head_g, w_four, w_mproj, w_out)
        new_ctx = h_ctx + gt_c * rmsnorm_2(out_c, g_post)
    return new_lat, new_ctx

def second_inputs(seed: int = 0) -> dict:
    key = jax.random.key(seed)
    ks = jax.random.split(key, 20)
    nrm = lambda k, shape, s: jax.random.normal(k, shape, jnp.float32) * s
    D = D_MODEL
    b_in = nrm(ks[10], (DEPTH, IN_WIDTH), 0.02)
    f_bias = jnp.linspace(3.0, 6.0, M_HEADS, dtype=jnp.float32)
    b_in = b_in.at[:, COL_GATES + M_HEADS:COL_GATES + 2 * M_HEADS].add(f_bias)
    b_in = b_in.at[:, COL_GATES + 3 * M_HEADS:COL_GATES + 4 * M_HEADS].add(f_bias)
    return {
        "x": nrm(ks[0], (BATCH, SEQ, D), 1.0),
        "c": nrm(ks[1], (BATCH, D), 1.0),
        "ctx": nrm(ks[2], (BATCH, CTX_LEN, D), 1.0),
        "c_ctx": nrm(ks[3], (D,), 1.0),
        "w_ada": nrm(ks[4], (DEPTH, D, N_ADA * D), D ** -0.5),
        "b_ada": nrm(ks[5], (DEPTH, N_ADA * D), 0.02),
        "norm_g": 1.0 + nrm(ks[6], (DEPTH, 6, D), 0.05),
        "w13_a": nrm(ks[7], (DEPTH, D, 2 * FF_HALF), D ** -0.5),
        "w2_a": nrm(ks[8], (DEPTH, FF_HALF, D), FF_HALF ** -0.5),
        "w_in": nrm(ks[9], (DEPTH, D, IN_WIDTH), D ** -0.5),
        "b_in": b_in,
        "conv_w": nrm(ks[11], (DEPTH, CONV_K, 2 * M_WIDTH), CONV_K ** -0.5),
        "conv_b": nrm(ks[12], (DEPTH, 2 * M_WIDTH), 0.02),
        "head_g": 1.0 + nrm(ks[13], (DEPTH, M_WIDTH), 0.05),
        "w_four": nrm(ks[14], (DEPTH, F_WIDTH, D), F_WIDTH ** -0.5),
        "w_mproj": nrm(ks[15], (DEPTH, M_WIDTH, D), M_WIDTH ** -0.5),
        "w_out": nrm(ks[16], (DEPTH, D, D), D ** -0.5),
        "w13_b": nrm(ks[17], (DEPTH, D, 2 * FF_HALF), D ** -0.5),
        "w2_b": nrm(ks[18], (DEPTH, FF_HALF, D), FF_HALF ** -0.5),
    }

def second_block(x, c, ctx, c_ctx, w_ada, b_ada, norm_g, w13_a, w2_a, w_in, b_in, conv_w, conv_b,
              head_g, w_four, w_mproj, w_out, w13_b, w2_b):
    h_lat = x
    h_ctx = ctx
    for l in range(DEPTH):
        last = l == DEPTH - 1
        ml = ada_params(c, w_ada[l], b_ada[l])
        mc = ada_params(c_ctx[None], w_ada[l], b_ada[l])
        g = norm_g[l]
        h_lat = half_ffn(h_lat, ml[:, 0], ml[:, 1], ml[:, 2], g[0], g[1], w13_a[l], w2_a[l])
        h_ctx = half_ffn(h_ctx, mc[:, 0], mc[:, 1], mc[:, 2], g[0], g[1], w13_a[l], w2_a[l])
        h_lat, h_ctx_new = token_mixing(
            h_lat, h_ctx, (ml[:, 3], ml[:, 4], ml[:, 5]), (mc[:, 3], mc[:, 4], mc[:, 5]),
            g[2], g[3], w_in[l], b_in[l], conv_w[l], conv_b[l], head_g[l],
            w_four[l], w_mproj[l], w_out[l], not last)
        h_lat = half_ffn(h_lat, ml[:, 6], ml[:, 7], ml[:, 8], g[4], g[5], w13_b[l], w2_b[l])
        if not last:
            h_ctx = half_ffn(h_ctx_new, mc[:, 6], mc[:, 7], mc[:, 8], g[4], g[5], w13_b[l], w2_b[l])
    return h_lat


DEPTH_3 = 2

N_META = 16
N_MIXERS = 2
RMS_EPS = 1e-6

MLA_HEADS = 8
QK_NOPE = 128
QK_ROPE = 64
V_HEAD = 128
Q_LORA = 384
KV_LORA = 256
MLA_WIDTH = MLA_HEADS * V_HEAD
ROPE_BASE = 10000.0
MASK_VALUE = -1e30

LRU_WIDTH = 1024
LRU_BLOCKS = 4
LRU_BLOCK = LRU_WIDTH // LRU_BLOCKS
CONV_WIDTH = 4
LRU_C = 8.0


def rmsnorm_3(x, g):
    xf = x.astype(jnp.float32)
    y = xf * lax.rsqrt(jnp.mean(xf * xf, axis=-1, keepdims=True) + RMS_EPS)
    return (y * g.astype(jnp.float32)).astype(x.dtype)

def rotate_half_split(x, cos, sin):
    x1, x2 = jnp.split(x, 2, axis=-1)
    return jnp.concatenate([x1 * cos - x2 * sin, x1 * sin + x2 * cos], axis=-1).astype(x.dtype)

def block_causal_attention(q_nope, q_rope, k_nope, k_rope, v):
    B, T, H, _ = q_nope.shape
    pad = (-T) % Q_BLOCK
    Tp = T + pad
    nb = Tp // Q_BLOCK

    def padt(a):
        return jnp.pad(a, [(0, 0), (pad, 0)] + [(0, 0)] * (a.ndim - 2))

    q_nope, q_rope, k_nope, k_rope, v = (padt(a) for a in (q_nope, q_rope, k_nope, k_rope, v))
    scale = (QK_NOPE + QK_ROPE) ** -0.5
    key_idx = jnp.arange(Tp)

    def to_blocks(a):
        return jnp.moveaxis(a.reshape(B, nb, Q_BLOCK, *a.shape[2:]), 1, 0)

    def one_block(args):
        blk, qn, qr = args
        s = (jnp.einsum('bqhd,bkhd->bhqk', qn, k_nope, preferred_element_type=jnp.float32)
             + jnp.einsum('bqhr,bkr->bhqk', qr, k_rope, preferred_element_type=jnp.float32)) * scale
        q_idx = blk * Q_BLOCK + jnp.arange(Q_BLOCK)
        mask = (key_idx[None, :] <= q_idx[:, None]) & (key_idx[None, :] >= pad)
        s = jnp.where(mask[None, None], s, MASK_VALUE)
        p = jax.nn.softmax(s, axis=-1)
        return jnp.einsum('bhqk,bkhd->bqhd', p.astype(v.dtype), v)

    out = lax.map(one_block, (jnp.arange(nb), to_blocks(q_nope), to_blocks(q_rope)))
    out = jnp.moveaxis(out, 0, 1).reshape(B, Tp, H, V_HEAD)
    return out[:, pad:]

def mla_mixer(h, w_in, q_norm_g, kv_norm_g, w_uq, w_ukv, w_out):
    B, T, _ = h.shape
    proj = h @ w_in
    q_lat, kv_lat, k_rope, gate = jnp.split(
        proj, [Q_LORA, Q_LORA + KV_LORA, Q_LORA + KV_LORA + QK_ROPE], axis=-1)
    q = (rmsnorm_3(q_lat, q_norm_g) @ w_uq).reshape(B, T, MLA_HEADS, QK_NOPE + QK_ROPE)
    q_nope, q_rope = q[..., :QK_NOPE], q[..., QK_NOPE:]
    kv = (rmsnorm_3(kv_lat, kv_norm_g) @ w_ukv).reshape(B, T, MLA_HEADS, QK_NOPE + V_HEAD)
    k_nope, v = kv[..., :QK_NOPE], kv[..., QK_NOPE:]
    pos = jnp.arange(T, dtype=jnp.float32)
    inv_freq = ROPE_BASE ** (-jnp.arange(0, QK_ROPE, 2, dtype=jnp.float32) / QK_ROPE)
    ang = pos[:, None] * inv_freq[None, :]
    cos, sin = jnp.cos(ang), jnp.sin(ang)
    q_rope = rotate_half_split(q_rope, cos[:, None, :], sin[:, None, :])
    k_rope = rotate_half_split(k_rope, cos, sin)
    attn = block_causal_attention(q_nope, q_rope, k_nope, k_rope, v)
    y = attn.reshape(B, T, MLA_WIDTH) * jax.nn.silu(gate)
    return y @ w_out

def rglru_mixer(h, w_in, conv_w, conv_b, w_rg, b_rg, w_ig, b_ig, lam, w_out):
    B, T, _ = h.shape
    proj = h @ w_in
    u, gate = jnp.split(proj, [LRU_WIDTH], axis=-1)
    up = jnp.pad(u, ((0, 0), (CONV_WIDTH - 1, 0), (0, 0)))
    uc = conv_b + up[:, 0:T] * conv_w[0]
    for j in range(1, CONV_WIDTH):
        uc = uc + up[:, j:j + T] * conv_w[j]
    ub = uc.reshape(B, T, LRU_BLOCKS, LRU_BLOCK)
    r = jax.nn.sigmoid(jnp.einsum('btgi,gij->btgj', ub, w_rg).reshape(B, T, LRU_WIDTH) + b_rg)
    i = jax.nn.sigmoid(jnp.einsum('btgi,gij->btgj', ub, w_ig).reshape(B, T, LRU_WIDTH) + b_ig)
    log_a = -LRU_C * r.astype(jnp.float32) * jax.nn.softplus(-lam.astype(jnp.float32))
    a = jnp.exp(log_a)
    mult = jnp.sqrt(-jnp.expm1(2.0 * log_a))
    mult = jnp.where(jnp.arange(T)[None, :, None] == 0, 1.0, mult)
    b = mult * (i * uc).astype(jnp.float32)

    def combine(left, right):
        a1, b1 = left
        a2, b2 = right
        return a1 * a2, a2 * b1 + b2

    _, hs = lax.associative_scan(combine, (a, b), axis=1)
    y = hs.astype(h.dtype) * jax.nn.silu(gate)
    return y @ w_out

def third_inputs(seed: int = 0) -> dict:
    key = jax.random.key(seed)
    ks = jax.random.split(key, 24)
    n_a = (DEPTH_3 + 1) // 2
    n_b = DEPTH_3 // 2
    d = D_MODEL
    f32 = jnp.float32

    def nrm(k, shape, fan_in):
        return jax.random.normal(k, shape, f32) * (fan_in ** -0.5)

    def gain(k, shape):
        return 1.0 + 0.01 * jax.random.normal(k, shape, f32)

    a_in_cols = Q_LORA + KV_LORA + QK_ROPE + MLA_WIDTH
    u0 = jax.random.uniform(ks[17], (n_b, LRU_WIDTH), f32, minval=0.9, maxval=0.999)
    s0 = u0 ** (1.0 / LRU_C)
    lam = jnp.log(s0) - jnp.log1p(-s0)
    return {
        'x': jax.random.normal(ks[0], (BATCH, SEQ, d), f32),
        'meta_tokens': jax.random.normal(ks[1], (N_META, d), f32),
        'a_norm_g': gain(ks[2], (n_a, d)),
        'a_w_in': nrm(ks[3], (n_a, d, a_in_cols), d),
        'a_q_norm_g': gain(ks[4], (n_a, Q_LORA)),
        'a_kv_norm_g': gain(ks[5], (n_a, KV_LORA)),
        'a_w_uq': nrm(ks[6], (n_a, Q_LORA, MLA_HEADS * (QK_NOPE + QK_ROPE)), Q_LORA),
        'a_w_ukv': nrm(ks[7], (n_a, KV_LORA, MLA_HEADS * (QK_NOPE + V_HEAD)), KV_LORA),
        'a_w_out': nrm(ks[8], (n_a, MLA_WIDTH, d), MLA_WIDTH),
        'b_norm_g': gain(ks[9], (n_b, d)),
        'b_w_in': nrm(ks[10], (n_b, d, 2 * LRU_WIDTH), d),
        'b_conv_w': nrm(ks[11], (n_b, CONV_WIDTH, LRU_WIDTH), CONV_WIDTH),
        'b_conv_b': 0.01 * jax.random.normal(ks[12], (n_b, LRU_WIDTH), f32),
        'b_w_rg': nrm(ks[13], (n_b, LRU_BLOCKS, LRU_BLOCK, LRU_BLOCK), LRU_BLOCK),
        'b_b_rg': 0.01 * jax.random.normal(ks[14], (n_b, LRU_WIDTH), f32),
        'b_w_ig': nrm(ks[15], (n_b, LRU_BLOCKS, LRU_BLOCK, LRU_BLOCK), LRU_BLOCK),
        'b_b_ig': 0.01 * jax.random.normal(ks[16], (n_b, LRU_WIDTH), f32),
        'b_lam': lam,
        'b_w_out': nrm(ks[18], (n_b, LRU_WIDTH, d), LRU_WIDTH),
        'final_norm_g': gain(ks[19], (d,)),
    }

def third_block(x, meta_tokens, a_norm_g, a_w_in, a_q_norm_g, a_kv_norm_g, a_w_uq, a_w_ukv,
              a_w_out, b_norm_g, b_w_in, b_conv_w, b_conv_b, b_w_rg, b_b_rg, b_w_ig, b_b_ig,
              b_lam, b_w_out, final_norm_g):
    B = x.shape[0]
    meta = jnp.broadcast_to(meta_tokens[None].astype(x.dtype), (B, N_META, x.shape[-1]))
    h = jnp.concatenate([meta, x], axis=1)
    for layer in range(DEPTH_3):
        j = layer // N_MIXERS
        if layer % N_MIXERS == 0:
            h = h + mla_mixer(rmsnorm_3(h, a_norm_g[j]), a_w_in[j], a_q_norm_g[j], a_kv_norm_g[j],
                              a_w_uq[j], a_w_ukv[j], a_w_out[j])
        else:
            h = h + rglru_mixer(rmsnorm_3(h, b_norm_g[j]), b_w_in[j], b_conv_w[j], b_conv_b[j],
                                b_w_rg[j], b_b_rg[j], b_w_ig[j], b_b_ig[j], b_lam[j], b_w_out[j])
    h = rmsnorm_3(h, final_norm_g)
    return h[:, N_META:]


def setup_inputs(seed=0):
    out = dict(first_inputs(seed))
    for name, value in second_inputs(seed + 1).items():
        if name != "x":
            out[name + "_2"] = value
    for name, value in third_inputs(seed + 2).items():
        if name != "x":
            out[name + "_3"] = value
    return out


def reference(
    x, c, ctx, c_ctx, w_mod, b_mod, g_mix, g_ffn, w_in, q_gain, k_gain, v_gain, w_s, b_s, w_out,
    w_router, w1, w3, w2, g_final, c_2, ctx_2, c_ctx_2, w_ada_2, b_ada_2, norm_g_2, w13_a_2,
    w2_a_2, w_in_2, b_in_2, conv_w_2, conv_b_2, head_g_2, w_four_2, w_mproj_2, w_out_2, w13_b_2,
    w2_b_2, meta_tokens_3, a_norm_g_3, a_w_in_3, a_q_norm_g_3, a_kv_norm_g_3, a_w_uq_3,
    a_w_ukv_3, a_w_out_3, b_norm_g_3, b_w_in_3, b_conv_w_3, b_conv_b_3, b_w_rg_3, b_b_rg_3,
    b_w_ig_3, b_b_ig_3, b_lam_3, b_w_out_3, final_norm_g_3,
):
    x = first_block(
        x, c, ctx, c_ctx, w_mod, b_mod, g_mix, g_ffn, w_in, q_gain, k_gain, v_gain, w_s, b_s,
        w_out, w_router, w1, w3, w2, g_final,
    )
    x = second_block(
        x, c_2, ctx_2, c_ctx_2, w_ada_2, b_ada_2, norm_g_2, w13_a_2, w2_a_2, w_in_2, b_in_2,
        conv_w_2, conv_b_2, head_g_2, w_four_2, w_mproj_2, w_out_2, w13_b_2, w2_b_2,
    )
    return third_block(
        x, meta_tokens_3, a_norm_g_3, a_w_in_3, a_q_norm_g_3, a_kv_norm_g_3, a_w_uq_3,
        a_w_ukv_3, a_w_out_3, b_norm_g_3, b_w_in_3, b_conv_w_3, b_conv_b_3, b_w_rg_3, b_b_rg_3,
        b_w_ig_3, b_b_ig_3, b_lam_3, b_w_out_3, final_norm_g_3,
    )


_drawn_inputs = setup_inputs


def setup_inputs(seed=0):
    import zlib

    import numpy as np

    out = dict(_drawn_inputs(seed))
    spreads = {}
    factors = {'q_gain': 8.0,
     'k_gain': 8.0,
     'v_gain': 3.889,
     'b_s': 4.027,
     'conv_b_2': 8.0,
     'a_norm_g_3': 8.0,
     'a_q_norm_g_3': 8.0,
     'a_kv_norm_g_3': 8.0,
     'b_norm_g_3': 41.22,
     'b_conv_b_3': 55.306,
     'b_b_rg_3': 64.0,
     'b_b_ig_3': 64.0,
     'final_norm_g_3': 169.095}
    for name, (base, spread) in spreads.items():
        noise = np.random.default_rng([zlib.crc32(name.encode()), seed]).standard_normal(out[name].shape)
        drawn = base * np.exp(spread * noise) if base else spread * noise
        out[name] = __import__('jax').numpy.asarray(drawn.astype(out[name].dtype))
    for name, factor in factors.items():
        out[name] = (out[name] * factor).astype(out[name].dtype)
    return out
```

```python
from contextlib import ExitStack

import numpy as np
import concourse.bass as bass
from concourse import mybir

F32 = mybir.dt.float32
ALU = mybir.AluOpType
ACT = mybir.ActivationFunctionType
AX = mybir.AxisListType.X
D = 1024
NSLOT = 10
NEG = -1e30

COLS = [("c", 8), ("c_ctx", 8), ("b_mod", 48), ("g_mix", 8), ("g_ffn", 8),
        ("c_2", 8), ("c_ctx_2", 8), ("b_ada_2", 72), ("norm_g_2", 48), ("b_q", 8), ("b_k", 8), ("b_gf", 8),
        ("b_gm", 8), ("conv_w_2", 48), ("conv_b_2", 16), ("b_s", 8),
        ("a_norm", 8), ("a_qn", 3), ("a_kvn", 2), ("b_norm", 8), ("conv_w_3", 32), ("conv_b_3", 8),
        ("b_rg", 8), ("b_ig", 8), ("lam", 8), ("b_gate", 2)]
CO, _n = {}, 0
for _name, _w in COLS:
    CO[_name] = _n
    _n += _w
NCOL = _n
ROWS = [("q_gain", 512), ("k_gain", 128), ("v_gain", 512), ("g_final", 1024), ("b_f", 512), ("b_v", 1024),
        ("b_o", 1024), ("head_g", 1024), ("final_g", 1024)]
RO, _n = {}, 0
for _name, _w in ROWS:
    RO[_name] = _n
    _n += _w
NROW = _n
CONSTS = [("ident", 128), ("ones", 128), ("sel", 256), ("rope1", 128), ("rope3", 192), ("slot", 32), ("tri", 256),
          ("selg", 1024), ("m8", 8)]
KO, _n = {}, 0
for _name, _w in CONSTS:
    KO[_name] = _n
    _n += _w
NCONST = _n


def build(nc, I, out, dbg=None):
    ctx = ExitStack()
    with ctx:
        _build(nc, I, out, ctx, dbg)


def _build(nc, I, out, ctx, dbg):
    def sb(name, shape, dt=F32):
        return ctx.enter_context(nc.sbuf_tensor(name, shape, dt))

    def sem(name):
        return ctx.enter_context(nc.semaphore(name))

    ring = sb("ring", [128, NSLOT, 2048])
    X = sb("X", [128, 4, D])
    HT = sb("HT", [128, 8, 512])
    big = sb("big", [128, 16000])
    cols = sb("cols", [128, NCOL])
    K = sb("K", [128, NCONST])
    cs = sb("cs", [128, 8, 2])
    mraw = sb("mraw", [128, 5, 512])
    mcol = sb("mcol", [128, 80, 2])
    AB = sb("AB", [128, 64])
    st = sb("st", [128, 64])
    PB = [ctx.enter_context(nc.psum_tensor(f"pb{i}", [128, 512], F32)) for i in range(8)]

    eng = {"v": nc.vector, "a": nc.scalar, "g": nc.gpsimd, "t": nc.tensor, "s": nc.sync}
    esem = {e: sem("s_" + e) for e in "vagt"}
    count = {e: 0 for e in "vagt"}
    waited = {e: {} for e in "vagts"}

    def wait(e, toks):
        for t in toks:
            if t is None:
                continue
            s, n, key = t
            if waited[e].get(key, 0) < n:
                eng[e].wait_ge(s, n)
                waited[e][key] = n

    def done(e, ins):
        count[e] += 1
        ins.then_inc(esem[e], 1)
        return (esem[e], count[e], e)

    def last(e):
        return (esem[e], count[e], e) if count[e] else None

    def V(name, *args, w=(), **kw):
        wait("v", [last("v"), *w])
        return done("v", name(*args, **kw))

    def A(out_, in_, func, w=(), **kw):
        wait("a", [last("a"), *w])
        return done("a", nc.scalar.activation(out_, in_, func, **kw))

    def G(name, *args, w=(), **kw):
        wait("g", [last("g"), *w])
        return done("g", name(*args, **kw))

    def mm(o, l, r, start=True, stop=True, w=(), inc=False):
        wait("t", w)
        i = nc.tensor.matmul(o, l, r, start=start, stop=stop)
        return done("t", i) if inc else None

    def tp(o, in_, w=(), inc=False):
        n = in_.shape[0]
        wait("t", w)
        i = nc.tensor.transpose(o, in_, ident[0:n, 0:n])
        return done("t", i) if inc else None

    ve = nc.vector
    tt, ts, stt, cp = ve.tensor_tensor, ve.tensor_scalar, ve.scalar_tensor_tensor, ve.tensor_copy

    nload = [0]
    stores = []

    def store(dst, src, w):
        wait("s", w)
        s = sem(f"st{len(stores)}")
        nc.sync.dma_start(dst, src).then_inc(s, 16)
        stores.append(s)
        return (s, 16, f"st{len(stores)}")

    def dump(name, ap, w):
        if dbg is not None and name in dbg:
            t = store(dbg[name], ap, w)
            wait("v", [t])
            wait("a", [t])

    def load_once(dst, src):
        nload[0] += 1
        s = sem(f"ld{nload[0]}")
        nc.sync.dma_start(dst, src).then_inc(s, 16)
        return (s, 16, f"ld{nload[0]}")

    class Slot:
        pass

    slot_sem = [sem(f"rs{i}") for i in range(NSLOT)]
    slot_use = [0] * NSLOT
    slot_last = [None] * NSLOT
    nslot = [0]

    def load(src, n, pat=None, parts=128, **dims):
        while slot_last[nslot[0] % NSLOT] is not None and slot_last[nslot[0] % NSLOT].free is None:
            nslot[0] += 1
        i = nslot[0] % NSLOT
        nslot[0] += 1
        if slot_last[i] is not None:
            wait("s", slot_last[i].free)
        s = Slot()
        ap = ring[0:parts, i, 0:n]
        s.ap = ap.rearrange(pat, **dims) if pat else ap
        nc.sync.dma_start(s.ap, src).then_inc(slot_sem[i], 16)
        slot_use[i] += 16
        s.tok = (slot_sem[i], slot_use[i], f"rs{i}")
        s.free = None
        slot_last[i] = s
        return s

    bank = [None] * 8

    def barrier():
        return [last(e) for e in "vagt"]

    def barrier_all():
        b = barrier()
        for e in "vagt":
            wait(e, b)

    t_k = load_once(K[:], I["consts"])
    t_cols = load_once(cols[:], I["cols"])
    xv = I["x"].rearrange("a (t p) d -> p (a t) d", p=128)
    xc = I["ctx"].rearrange("a (t p) d -> p (a t) d", p=128)
    t_x = load_once(X[:, 0:2, :], xv)
    t_c = load_once(X[:, 2:4, :], xc)

    def k(name, n=None):
        w = dict(CONSTS)[name]
        return K[:, KO[name]:KO[name] + (n or w)]

    ident = k("ident")
    ones = k("ones")

    def col(name, i=0, n=1):
        return cols[:, CO[name] + i:CO[name] + i + n]

    def arena(start=0):
        at = [start]

        def take(*shape, parts=128):
            n = 1
            for s in shape:
                n *= s
            ap = big[0:parts, at[0]:at[0] + n]
            at[0] += n
            assert at[0] <= 16000, at[0]
            if len(shape) == 2:
                ap = ap.rearrange("p (a b) -> p a b", a=shape[0])
            elif len(shape) == 3:
                ap = ap.rearrange("p (a b c) -> p a b c", a=shape[0], b=shape[1])
            return ap
        return take

    for e in "vagt":
        wait(e, [t_k, t_cols])
    V(ve.memset, st[:], 1.0)

    def rstd(tiles, base, d, w=(), junk=None, eps=1e-6):
        t = None
        for i, (ap, n) in enumerate(tiles):
            t = A(junk[0:n, 0:d], ap, ACT.Square, accum_out=st[0:n, base + i:base + i + 1], w=w)
        return rstd_of(base, len(tiles), d, t, eps)

    def rstd_of(base, n, d, t, eps=1e-6, src=None, dst=None, parts=128):
        s = st[0:parts, base:base + n] if src is None else src
        t = V(ts, s, s, 1.0 / d, eps, ALU.mult, ALU.add, w=[t])
        t = A(s, s, ACT.Sqrt, w=[t])
        return V(ve.reciprocal, s, s, w=[t])

    def modulated_T(tiles, regions, xn, w):
        ready = []
        for i, (ap, n, r, c) in enumerate(tiles):
            if i % 2 == 0:
                ready.append(V(ts, xn(i)[0:n, :], ap, st[0:n, r:r + 1], None, ALU.mult, w=w))
            else:
                ready.append(A(xn(i)[0:n, :], ap, ACT.Copy, scale=st[0:n, r:r + 1], w=w))
        for kk in range(8):
            b = kk % 4
            for i, (ap, n, r, c) in enumerate(tiles):
                t = tp(PB[b][:, c:c + n], xn(i)[0:n, kk * 128:kk * 128 + 128], w=[ready[i], bank[b]], inc=True)
            for j, (c0, c1, a, s) in enumerate(regions):
                if s is None:
                    t2 = V(ts, HT[:, kk, c0:c1], PB[b][:, c0:c1], a(kk), None, ALU.mult, w=[t])
                else:
                    t2 = V(ts, HT[:, kk, c0:c1], PB[b][:, c0:c1], a(kk), s(kk), ALU.mult, ALU.add, w=[t])
            bank[b] = t2
        return t2

    def gemv(w_dram, cname, bname, cctx, nchunk):
        t = A(cs[:, :, 0], col(cname, 0, 8), ACT.Silu, w=barrier())
        t = A(cs[:, :, 1], col(cctx, 0, 8), ACT.Silu)
        for nb in range((nchunk + 3) // 4):
            q = min(4, nchunk - 4 * nb)
            for kk in range(8):
                s = load(w_dram[kk * 128:kk * 128 + 128, nb * 2048:nb * 2048 + q * 512], q * 512)
                for j in range(q):
                    e = mm(PB[nb % 2][32 * j:32 * j + 2, :], cs[:, kk, :], s.ap[:, 512 * j:512 * j + 512],
                           kk == 0, kk == 7, w=[t, s.tok, bank[nb % 2]], inc=j == q - 1)
                s.free = [e]
            for j in range(q):
                f = A(mraw[32 * j:32 * j + 2, nb, :], PB[nb % 2][32 * j:32 * j + 2, :], ACT.Copy, w=[e])
            bank[nb % 2] = f
        mv = mcol[:, :, :].rearrange("p (b q j) c -> p b q j c", q=4, j=4)
        bv = col(bname, 0, 80 if nchunk > 16 else 48).rearrange("p (b q j) -> p b q j", q=4, j=4)
        es = []
        for q in range(4):
            nb = (nchunk - q + 3) // 4
            for b in range(nb):
                for j in range(4):
                    e = mm(PB[2 + q][:, 8 * b + 2 * j:8 * b + 2 * j + 2], mraw[32 * q:32 * q + 2, b, 128 * j:128 * j + 128],
                           ident[32 * q:32 * q + 2, 32 * q:32 * q + 2], w=[f, bank[2 + q]], inc=True)
            es.append(e)
        for q in range(4):
            nb = (nchunk - q + 3) // 4
            bank[2 + q] = V(tt, mv[:, 0:nb, q], PB[2 + q][:, 0:8 * nb].rearrange("p (b j c) -> p b j c", b=nb, c=2),
                            bv[:, 0:nb, q][:, :, :, None].to_broadcast([128, nb, 4, 2]), ALU.add, w=[es[q]])
        return bank[5]

    def row_of(dst, c8, tmp, w):
        for kk in range(8):
            d = tmp[:, (kk % 2) * 128:(kk % 2) * 128 + 128]
            t = V(ts, d, ident, c8[:, kk:kk + 1], None, ALU.mult, w=[*w, last("t")])
            e = mm(PB[3][:, (kk % 4) * 128:(kk % 4) * 128 + 128], ones, d, w=[t, bank[3]], inc=True)
            if kk % 4 == 3:
                bank[3] = A(dst[:, (kk - 3) * 128:(kk + 1) * 128], PB[3][:, :], ACT.Copy, w=[e])
        return bank[3]

    def rope(dst1, dst2, x1, x2, cos, sin, t1, w):
        V(tt, t1[0], x1, cos, ALU.mult, w=w)
        V(tt, t1[1], x2, sin, ALU.mult)
        V(tt, dst1, t1[0], t1[1], ALU.subtract)
        V(tt, t1[0], x1, sin, ALU.mult)
        V(tt, t1[1], x2, cos, ALU.mult)
        return V(tt, dst2, t1[0], t1[1], ALU.add)

    only = dbg.get("only") if dbg else None

    def first():
        t_mod = gemv(I["w_mod"][0], "c", "b_mod", "c_ctx", 12)
        for i, (g, ch, which) in enumerate((("g_mix", 1, 0), ("g_mix", 1, 1), ("g_ffn", 4, 0))):
            V(stt, AB[:, 8 * i:8 * i + 8], mcol[:, 8 * ch:8 * ch + 8, which], 1.0, col(g, 0, 8), ALU.add, ALU.mult)
        take = arena()
        xn = take(4, D)
        t = rstd([(X[:, i, :], 128) for i in range(4)], 0, D, w=[t_x, t_c], junk=xn[:, 0, :])
        t_h = modulated_T([(X[:, i, :], 128, i, 128 * i) for i in range(4)],
                          [(0, 256, lambda q: AB[:, q:q + 1], lambda q: mcol[:, q, 0:1]),
                           (256, 512, lambda q: AB[:, 8 + q:9 + q], lambda q: mcol[:, q, 1:2])],
                          lambda i: xn[:, i, :], [t])
        dump("hT", HT[:], [t_h])
        barrier_all()
        take = arena()
        qkv = take(4, 768)
        gm = take(2, D)
        w_in = I["w_in"][0]
        for kk in range(8):
            s = load(w_in[kk * 128:kk * 128 + 128, 0:1792], 1792)
            for i in range(2):
                mm(PB[i][:, :], HT[:, kk, 128 * i:128 * i + 128], s.ap[:, 0:512], kk == 0, kk == 7, w=[s.tok, bank[i]])
            for i in range(4):
                e = mm(PB[2 + i][:, 0:256], HT[:, kk, 128 * i:128 * i + 128], s.ap[:, 512:768], kk == 0, kk == 7,
                       w=[bank[2 + i]], inc=True)
            s.free = [e]
        for i in range(2):
            bank[i] = A(qkv[:, i, 0:512], PB[i][:, :], ACT.Copy, w=[e])
        for i in range(4):
            bank[2 + i] = A(qkv[:, i, 512:768], PB[2 + i][:, 0:256], ACT.Copy)
        t_qkv = bank[5]
        for kk in range(8):
            s = load(w_in[kk * 128:kk * 128 + 128, 768:1792], 1024)
            for i in range(2):
                for j in range(2):
                    b = (6, 7, 0, 1)[2 * i + j]
                    e = mm(PB[b][:, :], HT[:, kk, 128 * i:128 * i + 128], s.ap[:, 512 * j:512 * j + 512],
                           kk == 0, kk == 7, w=[s.tok, bank[b]], inc=i + j == 2)
            s.free = [e]
        for i in range(2):
            for j in range(2):
                b = (6, 7, 0, 1)[2 * i + j]
                bank[b] = A(gm[:, i, 512 * j:512 * j + 512], PB[b][:, :], ACT.Gelu, w=[e])
        t_gm = bank[1]
        sq = take(512)
        nrm = take(640)
        cos = [k("rope1")[:, 64 * i:64 * i + 32] for i in range(2)]
        sin = [k("rope1")[:, 64 * i + 32:64 * i + 64] for i in range(2)]
        qT = take(4, 256)
        kT = take(512)
        qp = take(512)
        kp = take(128)
        gains = load(I["rows"][:, 0:1152], 1152)
        s1, s2 = take(256), take(256)
        t_q = None
        for i in range(4):
            n0 = 0 if i < 2 else 512
            nh = 10 if i < 2 else 2
            src = qkv[:, i, n0:640]
            dst = nrm[:, n0:640]
            ss = st[:, 16:16 + nh]
            junk = HT[:, 0:2, :].rearrange("p a b -> p (a b)")[:, 0:nh * 64]
            V(tt, junk, src, src, ALU.mult, w=[t_qkv, last("t")])
            t = V(ve.tensor_reduce, ss, junk.rearrange("p (h d) -> p h d", d=64), AX, ALU.add)
            t = rstd_of(0, 0, 64, t, src=ss)
            V(tt, dst.rearrange("p (h d) -> p h d", d=64), src.rearrange("p (h d) -> p h d", d=64),
              ss[:, :, None].to_broadcast([128, nh, 64]), ALU.mult)
            t = V(tt, dst, dst, gains.ap[:, n0:640], ALU.mult, w=[gains.tok])
            if i < 2:
                for (src, dst, h0, hn) in ((nrm[:, 0:512], qp, 0, 8), (nrm[:, 512:640], kp, 8, 2)):
                    a = src.rearrange("p (h c d) -> p c h d", c=2, d=32)
                    if hn == 8:
                        o = dst.rearrange("p (i j c d) -> p c j i d", j=2, c=2, d=32)
                        for j in range(2):
                            x1, x2 = a[:, 0, 4 * j:4 * j + 4], a[:, 1, 4 * j:4 * j + 4]
                            cc = cos[i][:, None, :].to_broadcast([128, 4, 32])
                            si = sin[i][:, None, :].to_broadcast([128, 4, 32])
                            sc = [s1[:, 0:128].rearrange("p (h d) -> p h d", h=4), s2[:, 0:128].rearrange("p (h d) -> p h d", h=4)]
                            t = rope(o[:, 0, j], o[:, 1, j], x1, x2, cc, si, sc, [last("t")])
                    else:
                        o = dst.rearrange("p (h c d) -> p c h d", c=2, d=32)
                        cc = cos[i][:, None, :].to_broadcast([128, 2, 32])
                        si = sin[i][:, None, :].to_broadcast([128, 2, 32])
                        sc = [s1[:, 0:64].rearrange("p (h d) -> p h d", h=2), s2[:, 0:64].rearrange("p (h d) -> p h d", h=2)]
                        t = rope(o[:, 0], o[:, 1], a[:, 0], a[:, 1], cc, si, sc, [last("t")])
                for c in range(4):
                    e = tp(PB[2][:, 128 * c:128 * c + 128], qp[:, 128 * c:128 * c + 128], w=[t, bank[2]], inc=True)
                bank[2] = A(qT[:, :, 128 * i:128 * i + 128], PB[2][:, :].rearrange("p (c t) -> p c t", c=4), ACT.Copy, w=[e])
                e = tp(PB[3][:, 0:128], kp, w=[t, bank[3]], inc=True)
                bank[3] = A(kT[:, 128 * i:128 * i + 128], PB[3][:, 0:128], ACT.Copy, w=[e])
            else:
                e = tp(PB[3][:, 0:128], nrm[:, 512:640], w=[t, bank[3]], inc=True)
                bank[3] = A(kT[:, 128 * i:128 * i + 128], PB[3][:, 0:128], ACT.Copy, w=[e])
                wait("v", [e])
        t_q = last("a")
        dump("kT1", kT, [t_q])
        pr = [take(512), take(512)]
        pT = [take(4, 256), take(4, 256)]
        mixT = take(8, 256)
        u = 0
        pT_free = [None, None]
        for h in range(8):
            pl, r = h % 4, 64 * (h // 4)
            for i in range(2):
                b = i
                e = mm(PB[b][:, :], qT[r:r + 64, pl, 128 * i:128 * i + 128], kT[r:r + 64, :], w=[t_q, bank[b]], inc=True)
                mx = st[:, 32 + i:33 + i]
                t = V(ve.tensor_reduce, mx, PB[b][:, :], AX, ALU.max, w=[e])
                t = V(ts, mx, mx, -0.125, None, ALU.mult)
                bank[b] = A(pr[i], PB[b][:, :], ACT.Exp, bias=mx, scale=0.125, accum_out=st[:, 34 + i:35 + i],
                            w=[t, last("t")])
                t = V(ve.reciprocal, st[:, 36 + i:37 + i], st[:, 34 + i:35 + i], w=[bank[b]])
                t = V(ts, pr[i], pr[i], st[:, 36 + i:37 + i], None, ALU.mult)
                for s_ in range(4):
                    e = tp(PB[2 + i][:, 128 * s_:128 * s_ + 128], pr[i][:, 128 * s_:128 * s_ + 128], w=[t, bank[2 + i]], inc=True)
                bank[2 + i] = A(pT[h % 2][:, :, 128 * i:128 * i + 128], PB[2 + i][:, :].rearrange("p (s t) -> p s t", s=4),
                                ACT.Copy, w=[e, pT_free[h % 2]])
            b = 4 + h % 2
            ro = 64 * (h % 2)
            for s_ in range(4):
                e = mm(PB[b][ro:ro + 64, 0:256], qkv[:, s_, 640 + 64 * (h // 4):704 + 64 * (h // 4)], pT[h % 2][:, s_, :],
                       s_ == 0, s_ == 3, w=[bank[3], bank[b]], inc=True)
            pT_free[h % 2] = e
            bank[b] = V(cp, mixT[ro:ro + 64, h // 2, :], PB[b][ro:ro + 64, 0:256], w=[e])
        ws = load(I["w_sT"], 1024, "p (g i) -> p g i", g=8)
        t = None
        for i in range(2):
            t = A(HT[:, i, :], gm[:, i, 512:1024], ACT.Square, accum_out=st[:, 40 + i:41 + i], w=[t_gm, last("v"), last("t")])
        t = rstd_of(40, 2, 512, t)
        for i in range(2):
            vv = gm[:, i, 512:1024]
            t = V(stt, vv, vv, st[:, 40 + i:41 + i], gains.ap[:, 640:1152], ALU.mult, ALU.mult)
            for g in range(8):
                e = mm(PB[6][:, 64 * g:64 * g + 64], ws.ap[:, g, :], vv[:, 64 * g:64 * g + 64], w=[t, ws.tok, bank[6]], inc=g == 7)
            V(tt, vv.rearrange("p (g d) -> p g d", g=8), PB[6][:, :].rearrange("p (g d) -> p g d", g=8),
              col("b_s", 0, 8)[:, :, None].to_broadcast([128, 8, 64]), ALU.add, w=[e])
            t = V(tt, vv, vv, gm[:, i, 0:512], ALU.mult)
            bank[6] = t
            for c in range(4):
                e = tp(PB[7][:, 128 * c:128 * c + 128], vv[:, 128 * c:128 * c + 128], w=[t, bank[7]], inc=True)
            bank[7] = V(cp, mixT[:, 4:8, 128 * i:128 * i + 128], PB[7][:, :].rearrange("p (c t) -> p c t", c=4), w=[e])
        ws.free = [e]
        gains.free = [t]
        t_mix = bank[7]
        dump("mixT", mixT, [t_mix])
        gt = take(D)
        t_g = row_of(gt, mcol[:, 16:24, 0], s1, [t_mix])
        for kk in range(0, 8, 2):
            s = load(I["w_out"][0][kk * 128:kk * 128 + 256, :].rearrange("(a p) n -> p a n", p=128), 2048,
                     "p (a n) -> p a n", a=2)
            for a in range(2):
                for i in range(2):
                    for j in range(2):
                        b = 2 * i + j + 4
                        e = mm(PB[b][:, :], mixT[:, kk + a, 128 * i:128 * i + 128], s.ap[:, a, 512 * j:512 * j + 512],
                               kk + a == 0, kk + a == 7, w=[s.tok, t_mix, bank[b]], inc=True)
            s.free = [e]
        tmp = pr[0]
        for i in range(2):
            for j in range(2):
                b = 2 * i + j + 4
                V(tt, tmp, PB[b][:, :], gt[:, 512 * j:512 * j + 512], ALU.mult, w=[e, t_g])
                bank[b] = V(tt, X[:, i, 512 * j:512 * j + 512], X[:, i, 512 * j:512 * j + 512], tmp, ALU.add)
        dump("x1", X[:, 0:2, :], [last("v")])
        barrier_all()

        take = arena()
        xn = take(2, D)
        pos = take(2, 512)
        aff = take(2, 16)
        slotT = take(2, 16)
        big_g = take(4096)
        gT = take(16, 256)
        rT = take(256, parts=16)
        rW = take(256, parts=16)
        rM = take(256, parts=16)
        m8 = take(8, parts=16)
        t = rstd([(X[:, i, :], 128) for i in range(2)], 0, D, junk=big_g[:, 0:D])
        t_h = modulated_T([(X[:, i, :], 128, i, 128 * i) for i in range(2)],
                          [(0, 256, lambda q: AB[:, 16 + q:17 + q], lambda q: mcol[:, 24 + q, 0:1])],
                          lambda i: xn[:, i, :], [t])
        s = load(I["w_router"][0].rearrange("(a p) n -> p a n", p=128), 128, "p (a n) -> p a n", a=8)
        for i in range(2):
            for kk in range(8):
                e = mm(PB[4][:, 16 * i:16 * i + 16], HT[:, kk, 128 * i:128 * i + 128], s.ap[:, kk, :],
                       kk == 0, kk == 7, w=[t_h, s.tok, bank[4]], inc=kk == 7)
        s.free = [e]
        lg = PB[4][:, 0:32].rearrange("p (i e) -> p i e", i=2)
        mx = st[:, 8:10]
        t = V(ve.tensor_reduce, mx, lg, AX, ALU.max, w=[e])
        t = V(tt, aff, lg, mx[:, :, None].to_broadcast([128, 2, 16]), ALU.subtract)
        bank[4] = t
        t = A(aff, aff, ACT.Exp, w=[t])
        t = V(ve.tensor_reduce, mx, aff, AX, ALU.add, w=[t])
        t = V(ve.reciprocal, mx, mx)
        t_aff = V(tt, aff, aff, mx[:, :, None].to_broadcast([128, 2, 16]), ALU.mult)
        dump("aff", aff, [t_aff])
        for i in range(2):
            e = tp(PB[4][0:16, 128 * i:128 * i + 128], aff[:, i, :], w=[t_aff, bank[4]], inc=True)
        t = V(cp, rT, PB[4][0:16, 0:256], w=[e])
        bank[4] = t
        cur = rT
        for r in range(4):
            V(ve.max, m8, cur)
            V(ve.match_replace, rW, m8, cur, -1.0)
            cur = rW
        V(ts, rM, rW, 0.0, None, ALU.is_lt)
        V(ve.memset, rT, 0.0)
        V(ve.tensor_tensor_scan, rW, rM, rT, 0.0, ALU.add, ALU.add)
        t = V(tt, rW, rW, rM, ALU.mult)
        for i in range(2):
            e = tp(PB[4][:, 16 * i:16 * i + 16], rW[:, 128 * i:128 * i + 128], w=[t, bank[4]], inc=True)
        t = V(cp, slotT, PB[4][:, 0:32].rearrange("p (i e) -> p i e", i=2), w=[e])
        bank[4] = t
        sl = k("slot")
        for i in range(2):
            t = V(tt, pos[:, i, :].rearrange("p (e s) -> p e s", e=16), slotT[:, i, :, None].to_broadcast([128, 16, 32]),
                  sl[:, None, :].to_broadcast([128, 16, 32]), ALU.is_equal)
        t_pos = t
        wait("t", [t_pos])
        for kk in range(8):
            b = kk % 2
            for i in range(2):
                e = mm(PB[b][:, :], xn[:, i, kk * 128:kk * 128 + 128], pos[:, i, :], i == 0, i == 1, w=[bank[b]], inc=i == 1)
            bank[b] = V(ts, HT[:, kk, :], PB[b][:, :], AB[:, 16 + kk:17 + kk], mcol[:, 24 + kk, 0:1], ALU.mult, ALU.add, w=[e])
        t_xe = bank[1]
        gg = big_g[:, 0:2048].rearrange("p (e c s) -> p e c s", e=16, c=4)
        for i in range(2):
            V(tt, pos[:, i, :].rearrange("p (e s) -> p e s", e=16), pos[:, i, :].rearrange("p (e s) -> p e s", e=16),
              aff[:, i, :, None].to_broadcast([128, 16, 32]), ALU.mult, w=[e])
            for c in range(4):
                t = V(cp, gg[:, :, c, :], pos[:, i, :].rearrange("p (e s) -> p e s", e=16), w=[last("t")])
            for q in range(4):
                for r in range(4):
                    ex = 4 * q + r
                    e = tp(PB[2 + q % 2][:, 128 * r:128 * r + 128], gg[:, ex].rearrange("p c s -> p (c s)"),
                           w=[t, bank[2 + q % 2]], inc=True)
                bank[2 + q % 2] = A(gT[:, 4 * q:4 * q + 4, 128 * i:128 * i + 128],
                                    PB[2 + q % 2][:, :].rearrange("p (r t) -> p r t", r=4), ACT.Copy, w=[e])
        t_gT = bank[3]
        barrier_all()
        sil = [big_g[:, 0:512], big_g[:, 512:1024]]
        hidT = [big_g[:, 1024:1536].rearrange("p (c m) -> p c m", c=4), big_g[:, 1536:2048].rearrange("p (c m) -> p c m", c=4)]
        ye = [big_g[:, 2048:3072], big_g[:, 3072:4096]]
        sil_free = [None, None]
        ye_free = [None, None]
        w1, w3, w2 = I["w1"][0], I["w3"][0], I["w2"][0]

        def scatter(x, t):
            for i in range(2):
                for j in range(2):
                    e = mm(PB[4 + 2 * i + j][:, :], gT[:, x, 128 * i:128 * i + 128], ye[x % 2][:, 512 * j:512 * j + 512],
                           x == 0, x == 15, w=[t, bank[4 + 2 * i + j]], inc=True)
            ye_free[x % 2] = e
            return e

        t_ye = None
        for x in range(16):
            z = x % 2
            for half, w_ in ((0, w1), (1, w3)):
                for kk in range(8):
                    s = load(w_[x, kk * 128:kk * 128 + 128, :], 2048)
                    for j in range(4):
                        e = mm(PB[half][32 * j:32 * j + 32, :], HT[:, kk, 32 * x:32 * x + 32], s.ap[:, 512 * j:512 * j + 512],
                               kk == 0, kk == 7, w=[s.tok, bank[half]], inc=j == 3)
                    s.free = [e]
                if half == 0:
                    t_s = A(sil[z], PB[0][:, :], ACT.Silu, w=[e, sil_free[z]])
                    bank[0] = t_s
                    if x:
                        scatter(x - 1, t_ye)
            t = V(tt, sil[z], sil[z], PB[1][:, :], ALU.mult, w=[e, t_s])
            bank[1] = t
            for c in range(4):
                e = tp(PB[2][:, 128 * c:128 * c + 128], sil[z][:, 128 * c:128 * c + 128], w=[t, bank[2]], inc=True)
            sil_free[z] = e
            t = V(cp, hidT[z], PB[2][:, :].rearrange("p (c m) -> p c m", c=4), w=[e])
            bank[2] = t
            for c in range(4):
                sl_ = []
                for hf in range(2):
                    s = load(w2[x].rearrange("(j c p) n -> c p j n", j=4, c=4)[c][:, 2 * hf:2 * hf + 2, :], 2048,
                             "p (j n) -> p j n", j=2)
                    sl_.append(s)
                for n in range(2):
                    for j in range(4):
                        s = sl_[j // 2]
                        e = mm(PB[2 + n][32 * j:32 * j + 32, :], hidT[z][:, c, 32 * j:32 * j + 32],
                               s.ap[:, j % 2, 512 * n:512 * n + 512], c == 0, c == 3,
                               w=[s.tok, t, bank[2 + n]], inc=True)
                        if n == 1:
                            s.free = [e]
            A(ye[z][:, 0:512], PB[2][:, :], ACT.Copy, w=[e, ye_free[z]])
            t_ye = A(ye[z][:, 512:1024], PB[3][:, :], ACT.Copy)
            bank[2] = bank[3] = t_ye
        e = scatter(15, t_ye)
        wait("v", [e])
        wait("a", [e])
        gt = xn[:, 0, :]
        t_g = row_of(gt, mcol[:, 40:48, 0], sil[0], [])
        gf = load(I["rows"][:, RO["g_final"]:RO["g_final"] + 1024], 1024)
        for i in range(2):
            for j in range(2):
                b = 4 + 2 * i + j
                V(tt, sil[1], PB[b][:, :], gt[:, 512 * j:512 * j + 512], ALU.mult, w=[e, t_g])
                bank[b] = V(tt, X[:, i, 512 * j:512 * j + 512], X[:, i, 512 * j:512 * j + 512], sil[1], ALU.add)
        dump("x2", X[:, 0:2, :], [last("v")])
        t = rstd([(X[:, i, :], 128) for i in range(2)], 0, D, junk=ye[0], w=[last("v")])
        for i in range(2):
            t = V(stt, X[:, i, :], X[:, i, :], st[:, i:i + 1], gf.ap, ALU.mult, ALU.mult, w=[gf.tok])
        gf.free = [t]
        dump("xf", X[:, 0:2, :], [t])
        barrier_all()

    def second():
        wait("s", [last("v"), last("a"), last("t"), t_c])
        t_c2 = load_once(X[:, 2:4, :], I["ctx_2"].rearrange("a (t p) d -> p (a t) d", p=128))
        for e in "va":
            wait(e, [t_c2, t_x])
        gemv(I["w_ada_2"][0], "c_2", "b_ada_2", "c_ctx_2", 18)

        def ng(i):
            return col("norm_g_2", 8 * i, 8)

        for i, (g, ch, which) in enumerate(((0, 1, 0), (0, 1, 1), (2, 4, 0), (2, 4, 1), (4, 7, 0))):
            V(stt, AB[:, 8 * i:8 * i + 8], mcol[:, 8 * ch:8 * ch + 8, which], 1.0, ng(g), ALU.add, ALU.mult)
        V(stt, AB[:, 40:48], mcol[:, 16:24, 0], 0.5, ng(1), ALU.mult, ALU.mult)
        V(stt, AB[:, 48:56], mcol[:, 16:24, 1], 0.5, ng(1), ALU.mult, ALU.mult)
        barrier_all()

        def post(nt, G_, banks, tmp, e, t_g):
            for i in range(nt):
                for j in range(2):
                    t = A(tmp, PB[banks[2 * i + j]][:, :], ACT.Square, accum_out=st[:, 8 + 2 * i + j:9 + 2 * i + j], w=[e, last("v")])
            sv = st[:, 8:8 + 2 * nt].rearrange("p (i j) -> p i j", j=2)
            t = V(tt, st[:, 0:nt], sv[:, :, 0], sv[:, :, 1], ALU.add, w=[t])
            t = rstd_of(0, nt, D, t)
            for i in range(nt):
                for j in range(2):
                    b = banks[2 * i + j]
                    V(stt, tmp, PB[b][:, :], st[:, i:i + 1], G_[i // 2][:, 512 * j:512 * j + 512], ALU.mult, ALU.mult, w=[t_g])
                    bank[b] = V(tt, X[:, i, 512 * j:512 * j + 512], X[:, i, 512 * j:512 * j + 512], tmp, ALU.add)

        def half_ffn(nt, pre, sh, gates, w13, w2):
            take = arena()
            hid = take(22, 128 * nt)
            T = 128 * nt
            xn = hid.rearrange("p a b -> p (a b)")
            Gr = [take(D) for _ in gates]
            tmp = take(512)
            sl = [take(512), take(512)]
            t_g = None
            for g_, c8 in zip(Gr, gates):
                t_g = row_of(g_, c8, sl[0], [last("v")])
            t = rstd([(X[:, i, :], 128) for i in range(nt)], 0, D, junk=xn[:, 0:D], w=[last("v"), last("t")])
            reg = []
            for z, p in enumerate(pre):
                reg.append((256 * z, 256 * z + 256, (lambda q, p=p: AB[:, 8 * p + q:8 * p + q + 1]),
                            (lambda q, z=z: mcol[:, sh * 8 + q, z:z + 1])))
            t_h = modulated_T([(X[:, i, :], 128, i, 128 * i) for i in range(nt)], reg,
                              lambda i: xn[:, D * i:D * i + D], [t])
            wait("t", [t_h])
            for b in range(8):
                bank[b] = t_h
            wait("v", [last("t")])
            sfree = [last("v")] * 2
            for p in range(11):
                ss = [load(w13[:, c0 + 256 * p:c0 + 256 * p + 256].rearrange("(a p) n -> p a n", p=128), 2048,
                           "p (a n) -> p a n", a=8) for c0 in (0, 2816)]
                for f in range(2):
                    n = 2 * p + f
                    ba, bb = (n % 4) * 2, (n % 4) * 2 + 1
                    for kk in range(8):
                        e = mm(PB[ba][:, 0:T], ss[0].ap[:, kk, 128 * f:128 * f + 128], HT[:, kk, 0:T], kk == 0, kk == 7,
                               w=[ss[0].tok, bank[ba]], inc=kk == 7)
                    t = A(sl[n % 2][:, 0:T], PB[ba][:, 0:T], ACT.Silu, w=[e, sfree[n % 2]])
                    for kk in range(8):
                        e2 = mm(PB[bb][:, 0:T], ss[1].ap[:, kk, 128 * f:128 * f + 128], HT[:, kk, 0:T], kk == 0, kk == 7,
                                w=[ss[1].tok, bank[bb]], inc=kk == 7)
                    t2 = V(tt, hid[:, n, :], sl[n % 2][:, 0:T], PB[bb][:, 0:T], ALU.mult, w=[e2, t])
                    sfree[n % 2] = t2
                    bank[ba], bank[bb] = t, t2
                ss[0].free, ss[1].free = [e], [e2]
            wait("t", [t2])
            for p in range(11):
                s = load(w2[256 * p:256 * p + 256, :].rearrange("(a p) n -> p a n", p=128), 2048, "p (a n) -> p a n", a=2)
                for a in range(2):
                    n = 2 * p + a
                    for i in range(nt):
                        for j in range(2):
                            b = 2 * i + j
                            e = mm(PB[b][:, :], hid[:, n, 128 * i:128 * i + 128], s.ap[:, a, 512 * j:512 * j + 512],
                                   n == 0, n == 21, w=[s.tok, bank[b]], inc=True)
                s.free = [e]
            post(nt, Gr, list(range(8)), tmp, e, t_g)
            barrier_all()

        half_ffn(4, (0, 1), 0, (AB[:, 40:48], AB[:, 48:56]), I["w13_a_2"][0], I["w2_a_2"][0])
        dump("ffa", X[:], [last("v")])
        mixer(post)
        dump("mix2", X[:, 0:2, :], [last("v")])
        V(stt, AB[:, 40:48], mcol[:, 64:72, 0], 0.5, ng(5), ALU.mult, ALU.mult)
        half_ffn(2, (4,), 6, (AB[:, 40:48],), I["w13_b_2"][0], I["w2_b_2"][0])
        dump("ffb", X[:, 0:2, :], [last("v")])

    CF, CQ, CK, CV, CO_, CG, CB = 0, 512, 1536, 2560, 3584, 4608, 4624

    def mixer(post):
        w_in = I["w_in_2"][0]
        take = arena()
        xn = big[:, 0:4096].rearrange("p (a b) -> p a b", a=4)
        t = rstd([(X[:, i, :], 128) for i in range(4)], 0, D, junk=xn[:, 0, :])
        t_h = modulated_T([(X[:, i, :], 128, i, 128 * i) for i in range(4)],
                          [(0, 256, lambda q: AB[:, 16 + q:17 + q], lambda q: mcol[:, 24 + q, 0:1]),
                           (256, 512, lambda q: AB[:, 24 + q:25 + q], lambda q: mcol[:, 24 + q, 1:2])],
                          lambda i: xn[:, i, :], [t])
        barrier_all()
        yfT = take(4, 256)
        hmT = take(8, 256)
        yT = take(8, 256)
        gr = 512
        MM = take(gr, parts=36)
        dec = take(8, 4)
        gc = take(4, 4, 8)
        kept = 3072 + 2048 + 512 + 32 + 128
        li = take(gr, parts=36)
        lf = take(gr, parts=36)
        bb = take(gr, parts=36)
        rr = take(gr, parts=36)
        q_a = take(gr, parts=36)
        q_f = take(gr, parts=36)
        q_w = take(gr, parts=36)
        zz = take(gr, parts=36)
        small = take(32, parts=36)
        sg = load(w_in[:, CG:CG + 16].rearrange("(a p) n -> p a n", p=128), 128, "p (a n) -> p a n", a=8)
        V(ve.memset, PB[0][0:36, :], 0.0, w=[last("t")])
        V(ve.memset, PB[1][0:36, :], 0.0)
        t = V(ve.memset, zz, 0.0)
        for d in range(2):
            for q in range(2):
                for kk in range(8):
                    e = mm(PB[q][32 * d:32 * d + 4, :], sg.ap[:, kk, 8 * d + 4 * q:8 * d + 4 * q + 4], HT[:, kk, :],
                           kk == 0, kk == 7, w=[t, sg.tok], inc=True)
        sg.free = [e]
        bg = col("b_gate", 0, 2)
        V(ts, li, PB[0][0:36, :], bg[0:36, 0:1], None, ALU.add, w=[e])
        t = V(ts, lf, PB[1][0:36, :], bg[0:36, 1:2], None, ALU.add)
        bank[0] = bank[1] = t
        V(ts, bb, lf, 0.0, None, ALU.min)
        V(ts, rr, lf, 0.0, None, ALU.max)
        t = V(stt, rr, bb, 2.0, lf, ALU.mult, ALU.subtract)
        t = A(rr, rr, ACT.Exp, w=[t])
        log1p(rr, MM, q_a, q_f, [t])
        V(tt, lf, bb, q_f, ALU.subtract)
        order = [[2, 3, 0, 1], [3, 2, 1, 0]]
        seg = [slice(0, 4), slice(32, 36)]

        def view(ap, d, blk):
            a = ap[seg[d], 128 * blk:128 * blk + 128]
            return a if d == 0 else a[:, ::-1]

        def endof(ap, d, blk):
            i = 128 * blk + (127 if d == 0 else 0)
            return ap[seg[d], i:i + 1]

        t = V(ve.memset, small, 0.0)
        for d in range(2):
            for blk in range(4):
                t = V(ve.tensor_tensor_scan, view(bb, d, blk), view(lf, d, blk), view(zz, d, blk), 0.0, ALU.add, ALU.add)
        t = V(tt, rr, li, bb, ALU.subtract)
        for d in range(2):
            for n in range(4):
                blk = order[d][n]
                m0 = small[seg[d], n:n + 1]
                V(ve.tensor_tensor_scan, view(MM, d, blk), view(rr, d, blk), view(rr, d, blk), m0, ALU.max, ALU.max)
                V(tt, small[seg[d], n + 1:n + 2], endof(bb, d, blk), endof(MM, d, blk), ALU.add)
                V(tt, small[seg[d], 8 + n:9 + n], m0, endof(MM, d, blk), ALU.subtract)
                V(ts, q_w[seg[d], 128 * blk:128 * blk + 128], rr[seg[d], 128 * blk:128 * blk + 128], endof(MM, d, blk), None, ALU.subtract)
                V(ts, q_a[seg[d], 128 * blk:128 * blk + 128], MM[seg[d], 128 * blk:128 * blk + 128], -1.0, m0, ALU.mult, ALU.add)
                t = V(stt, q_f[seg[d], 128 * blk:128 * blk + 128], bb[seg[d], 128 * blk:128 * blk + 128], -1.0,
                      MM[seg[d], 128 * blk:128 * blk + 128], ALU.mult, ALU.subtract)
        for d in range(2):
            s_ = seg[d]
            A(q_w[s_, :], q_w[s_, :], ACT.Exp, w=[t])
            A(q_a[s_, 0:256], q_a[s_, 0:256], ACT.Exp)
            A(q_f[s_, 0:256], q_f[s_, 0:256], ACT.Exp)
            t2 = A(small[s_, 8:12], small[s_, 8:12], ACT.Exp)
        dd = take(32, parts=36)
        t = V(tt, dd.rearrange("p (i n) -> p i n", i=8), small[:, None, 8:12].to_broadcast([36, 8, 4]),
              k("m8")[0:36, :, None].to_broadcast([36, 8, 4]), ALU.mult, w=[t2])
        e = mm(PB[2][:, 0:32], ones[0:36, :], dd, w=[t, bank[2]], inc=True)
        bank[2] = V(cp, dec.rearrange("p i n -> p (i n)"), PB[2][:, 0:32], w=[e])
        wait("t", [t, t2])
        for qi, ap in enumerate((rr, q_w, q_a, q_f)):
            blks = 4 if qi == 1 else 2
            for blk in range(blks):
                for d in range(2):
                    e = mm(PB[3 + d][:, (qi * 4 + blk) * 4:(qi * 4 + blk) * 4 + 4],
                           ap[seg[d], 128 * blk:128 * blk + 128], ident[seg[d], seg[d]], w=[t, t2, bank[3 + d]], inc=True)
        for qi in range(4):
            blks = 4 if qi == 1 else 2
            for d in range(2):
                t = V(cp, gc[:, qi, 0:blks, 4 * d:4 * d + 4],
                      PB[3 + d][:, qi * 16:qi * 16 + 4 * blks].rearrange("p (b i) -> p b i", i=4), w=[e])
        bank[3] = bank[4] = t
        t_gates = t
        dump("gc", gc, [t])
        zf = take(2, 512)
        m12 = take(2, 512)
        bf = load(I["rows"][:, RO["b_f"]:RO["b_f"] + 512], 512)
        for kk in range(0, 8, 4):
            s = load(w_in[kk * 128:kk * 128 + 512, CF:CF + 512].rearrange("(a p) n -> p a n", p=128), 2048,
                     "p (a n) -> p a n", a=4)
            for a in range(4):
                for i in range(2):
                    e = mm(PB[4 + i][:, :], HT[:, kk + a, 128 * i:128 * i + 128], s.ap[:, a, :], kk + a == 0, kk + a == 7,
                           w=[s.tok, bank[4 + i]], inc=True)
            s.free = [e]
        for i in range(2):
            t = V(tt, zf[:, i, :], PB[4 + i][:, :], bf.ap, ALU.add, w=[e, bf.tok])
            bank[4 + i] = t
        bf.free = [t]
        fr = load(I["four"], 1280)
        f1 = fr.ap[:, 0:1024].rearrange("p (i n) -> p i n", i=2)
        cc, ns = fr.ap[:, 1024:1152], fr.ap[:, 1152:1280]
        for g in range(4):
            b = 6 + g % 2
            for i in range(2):
                e = mm(PB[b][:, :], zf[:, i, 128 * g:128 * g + 128], f1[:, i, :], i == 0, i == 1, w=[t, fr.tok, bank[b]], inc=True)
            bank[b] = A(m12[:, g % 2, :], PB[b][:, :], ACT.Copy, w=[e])
            b2 = 4 + g % 2
            mm(PB[b2][:, 0:256], cc, m12[:, g % 2, 0:256], True, False, w=[bank[b], bank[b2]])
            e = mm(PB[b2][:, 0:256], ns, m12[:, g % 2, 256:512], False, True, inc=True)
            bank[b2] = V(cp, yfT[:, g, :], PB[b2][:, 0:256], w=[e])
            wait("a", [e])
        fr.free = [e]
        dump("yfT", yfT, [last("v")])
        barrier_all()
        take = arena(kept)
        pads = [take(2, 258) for _ in range(2)]
        qT = take(2, 256)
        kT = take(2, 512)
        va = take(4, 257)
        hs = take(2, 256)
        kw = [take(256) for _ in range(2)]
        C = [take(2, 257) for _ in range(2)]
        wT = take(4, 128)
        sT = take(4, 128)
        inter = take(257)
        so = take(2, 256)
        e_c = last("v")
        t = V(ve.memset, pads[0], 0.0)
        t = V(ve.memset, pads[1], 0.0)
        tri = k("tri").rearrange("p (d t) -> p d t", d=2)
        selg = k("selg").rearrange("p (i t) -> p i t", i=8)
        barrier_all()

        def conv(dst, src, ci, T):
            cw = lambda j: col("conv_w_2", 16 * j + ci)
            bname, bi = ("b_q", ci) if ci < 8 else ("b_k", ci - 8)
            for z in range(T // 256):
                p = pads[0][:, z, :]
                V(ts, p[:, 1:257], src[0][:, 256 * z:256 * z + 256], col(bname, bi), None, ALU.add, w=[src[1], last("a")])
            P_ = pads[0][:, 0:T // 256, :]
            O = pads[1][:, 0:T // 256, 0:256]
            V(ts, O, P_[:, :, 0:256], cw(0), col("conv_b_2", ci), ALU.mult, ALU.add)
            V(stt, O, P_[:, :, 1:257], cw(1), O, ALU.mult, ALU.add)
            t = V(stt, O, P_[:, :, 2:258], cw(2), O, ALU.mult, ALU.add)
            return A(dst.rearrange("p (z t) -> p z t", t=256), O, ACT.Silu, w=[t, last("t")])

        bo = load(I["rows"][:, RO["b_v"]:RO["b_v"] + 2048], 2048)
        hg = load(I["rows"][:, RO["head_g"]:RO["head_g"] + 1024], 1024)
        for h in range(4):
            def wslot(c0):
                return load(w_in[:, c0 + 256 * h:c0 + 256 * h + 256].rearrange("(a p) n -> p a n", p=128), 2048,
                            "p (a n) -> p a n", a=8)
            sq_, sk, sv, so_ = wslot(CQ), wslot(CK), wslot(CV), wslot(CO_)
            tq = None
            for f in range(2):
                for kk in range(8):
                    e = mm(PB[f][:, 0:256], sq_.ap[:, kk, 128 * f:128 * f + 128], HT[:, kk, 0:256], kk == 0, kk == 7,
                           w=[sq_.tok, bank[f]], inc=kk == 7)
                tq = conv(qT[:, f, :], (PB[f], e), 2 * h + f, 256)
                bank[f] = last("v")
            sq_.free = [e]
            for f in range(2):
                for kk in range(8):
                    e = mm(PB[2 + f][:, :], sk.ap[:, kk, 128 * f:128 * f + 128], HT[:, kk, :], kk == 0, kk == 7,
                           w=[sk.tok, bank[2 + f]], inc=kk == 7)
                tq = conv(kT[:, f, :], (PB[2 + f], e), 8 + 2 * h + f, 512)
                bank[2 + f] = last("v")
            sk.free = [e]
            for i in range(4):
                b = 4 + i % 2
                for kk in range(8):
                    e = mm(PB[b][:, 0:256], HT[:, kk, 128 * i:128 * i + 128], sv.ap[:, kk, :], kk == 0, kk == 7,
                           w=[sv.tok, bank[b]], inc=kk == 7)
                V(tt, va[:, i, 0:256], PB[b][:, 0:256], bo.ap[:, 256 * h:256 * h + 256], ALU.add, w=[e, bo.tok])
                t_v = bank[b] = V(ve.memset, va[:, i, 256:257], 1.0)
            sv.free = [e]
            for i in range(2):
                b = 4 + i
                for kk in range(8):
                    e = mm(PB[b][:, 0:256], HT[:, kk, 128 * i:128 * i + 128], so_.ap[:, kk, :], kk == 0, kk == 7,
                           w=[so_.tok, bank[b]], inc=kk == 7)
                t = V(tt, so[:, i, :], PB[b][:, 0:256], bo.ap[:, 1024 + 256 * h:1280 + 256 * h], ALU.add, w=[e])
                bank[b] = t
                t_so = A(so[:, i, :], so[:, i, :], ACT.Sigmoid, w=[t])
            so_.free = [e]
            for d in range(2):
                x = 4 * d + h
                for n in range(4):
                    blk = order[d][n]
                    tcol = slice(128 * blk, 128 * blk + 128)
                    if n >= 2:
                        mm(PB[6][:, 0:128], kT[:, 0, tcol], qT[:, 0, tcol], True, False, w=[tq, bank[6]])
                        e = mm(PB[6][:, 0:128], kT[:, 1, tcol], qT[:, 1, tcol], False, True, inc=True)
                        e1 = mm(PB[7][:, 0:128], selg[0:36, x, :], MM[:, tcol], w=[t_gates, bank[7]], inc=True)
                        V(tt, wT[:, 0, :], tri[:, d, :], PB[7][:, 0:128], ALU.subtract, w=[e1, last("a")])
                        bank[7] = last("v")
                        t = A(wT[:, 0, :], wT[:, 0, :], ACT.Exp, bias=gc[:, 0, blk, x:x + 1], w=[last("v")])
                        t = V(stt, sT[:, 0, :], PB[6][:, 0:128], 0.0625, wT[:, 0, :], ALU.mult, ALU.mult, w=[t, e, last("t")])
                        bank[6] = t
                        e = mm(PB[6][:, 0:257], sT[:, 0, :], va[:, blk, :], w=[t, t_v], inc=True)
                        mm(PB[7][:, 0:257], qT[:, 0, tcol], C[d][:, 0, :], True, False, w=[t_C, bank[7]])
                        e2 = mm(PB[7][:, 0:257], qT[:, 1, tcol], C[d][:, 1, :], False, True, inc=True)
                        V(ts, inter, PB[7][:, 0:257], gc[:, 2, blk, x:x + 1], None, ALU.mult, w=[e2])
                        bank[7] = last("v")
                        t = V(tt, inter, inter, PB[6][:, 0:257], ALU.add, w=[e])
                        bank[6] = t
                        dn = st[:, 50:51]
                        V(ts, dn, inter[:, 256:257], -1.0, None, ALU.mult)
                        V(tt, dn, dn, inter[:, 256:257], ALU.max)
                        V(tt, dn, dn, gc[:, 3, blk, x:x + 1], ALU.max)
                        V(ve.reciprocal, dn, dn)
                        if d == 0:
                            V(ts, hs[:, blk, :], inter[:, 0:256], dn, None, ALU.mult)
                        else:
                            V(stt, hs[:, blk, :], inter[:, 0:256], dn, hs[:, blk, :], ALU.mult, ALU.add)
                    if n < 3:
                        for f in range(2):
                            e = tp(PB[6][:, 128 * f:128 * f + 128], kT[:, f, tcol], w=[tq, bank[6]], inc=True)
                        t = V(ts, kw[0], PB[6][:, 0:256], gc[:, 1, blk, x:x + 1], 0.0625, ALU.mult, ALU.mult, w=[e, last("t")])
                        bank[6] = t
                        for f in range(2):
                            e = mm(PB[f][:, 0:257], kw[0][:, 128 * f:128 * f + 128], va[:, blk, :], w=[t, t_v, bank[f]], inc=True)
                            if n == 0:
                                t_C = V(cp, C[d][:, f, :], PB[f][:, 0:257], w=[e])
                            else:
                                t_C = V(stt, C[d][:, f, :], C[d][:, f, :], dec[:, x, n:n + 1], PB[f][:, 0:257], ALU.mult, ALU.add, w=[e])
                            bank[f] = t_C
            if h == 0:
                dump("hs0", hs, [last("v")])
            for i in range(2):
                t = A(sT[:, 0:2, :].rearrange("p a b -> p (a b)"), hs[:, i, :], ACT.Square, accum_out=st[:, 52 + i:53 + i], w=[last("v"), last("t")])
            t = rstd_of(52, 2, 256, t)
            for i in range(2):
                V(stt, hs[:, i, :], hs[:, i, :], st[:, 52 + i:53 + i], hg.ap[:, 256 * h:256 * h + 256], ALU.mult, ALU.mult, w=[hg.tok])
                t = V(tt, hs[:, i, :], hs[:, i, :], so[:, i, :], ALU.mult, w=[t_so])
                for f in range(2):
                    e = tp(PB[6][:, 128 * f:128 * f + 128], hs[:, i, 128 * f:128 * f + 128], w=[t, bank[6]], inc=True)
                t = V(cp, hmT[:, 2 * h:2 * h + 2, 128 * i:128 * i + 128], PB[6][:, 0:256].rearrange("p (f t) -> p f t", f=2), w=[e])
                bank[6] = t
        bo.free = hg.free = [t]
        t_hm = t
        dump("hmT", hmT, [t])
        s1, s2 = sT[:, 0:2, :].rearrange("p a b -> p (a b)"), wT[:, 0:2, :].rearrange("p a b -> p (a b)")
        for p in range(4):
            def cslot(w, c0, a):
                return load(w[:, c0 + 256 * p:c0 + 256 * p + 256].rearrange("(a p) n -> p a n", p=128), 256 * a,
                            "p (a n) -> p a n", a=a)
            sf, sm, s4, s8 = (cslot(w_in, CB, 8), cslot(w_in, CB + D, 8), cslot(I["w_four_2"][0], 0, 4),
                              cslot(I["w_mproj_2"][0], 0, 8))
            for f in range(2):
                o = 2 * p + f
                for qi, (s, rhs, nk) in enumerate(((sf, HT[:, :, 0:256], 8), (sm, HT[:, :, 0:256], 8), (s4, yfT, 4), (s8, hmT, 8))):
                    for kk in range(nk):
                        e = mm(PB[qi + 4 * (o % 2)][:, 0:256], s.ap[:, kk, 128 * f:128 * f + 128], rhs[:, kk, :], kk == 0, kk == nk - 1,
                               w=[s.tok, t_hm, bank[qi + 4 * (o % 2)]], inc=kk == nk - 1)
                    s.free = [e]
                B = PB[4 * (o % 2):4 * (o % 2) + 4]
                A(s1, B[0][:, 0:256], ACT.Sigmoid, bias=col("b_gf", o), w=[e, last("v")])
                t = A(s2, B[1][:, 0:256], ACT.Sigmoid, bias=col("b_gm", o))
                V(tt, s1, s1, B[2][:, 0:256], ALU.mult, w=[t])
                V(tt, s2, s2, B[3][:, 0:256], ALU.mult)
                t_y = V(tt, yT[:, o, :], s1, s2, ALU.add)
                for qi in range(4):
                    bank[qi + 4 * (o % 2)] = t_y
        V(tt, AB[:, 40:48], mcol[:, 40:48, 0], col("norm_g_2", 24, 8), ALU.mult)
        barrier_all()
        take = arena()
        take(4096 + 1024)
        Gr = take(D)
        tmp = take(512)
        tg = row_of(Gr, AB[:, 40:48], tmp, [last("v")])
        for kk in range(0, 8, 2):
            s = load(I["w_out_2"][0][kk * 128:kk * 128 + 256, :].rearrange("(a p) n -> p a n", p=128), 2048,
                     "p (a n) -> p a n", a=2)
            for a in range(2):
                for i in range(2):
                    for j in range(2):
                        b = 4 + 2 * i + j
                        e = mm(PB[b][:, :], yT[:, kk + a, 128 * i:128 * i + 128], s.ap[:, a, 512 * j:512 * j + 512],
                               kk + a == 0, kk + a == 7, w=[s.tok, t_y, bank[b]], inc=True)
            s.free = [e]
        post(2, [Gr], [4, 5, 6, 7], tmp, e, tg)
        barrier_all()

    def log1p(z, w_, w2, o, wt):
        V(ts, w_, z, 2.0, None, ALU.add, w=wt)
        V(ve.reciprocal, w_, w_)
        V(tt, w_, w_, z, ALU.mult)
        V(tt, w2, w_, w_, ALU.mult)
        V(ts, o, w2, 1.0 / 17, None, ALU.mult)
        for n in (15, 13, 11, 9, 7, 5, 3):
            V(stt, o, o, 1.0 / n, w2, ALU.add, ALU.mult)
        V(stt, o, o, 1.0, w_, ALU.add, ALU.mult)
        return V(ts, o, o, 2.0, None, ALU.mult)

    TL = [(0, 128, 16), (1, 128, 144), (2, 16, 0)]
    T3 = 272

    def third():
        wait("s", [last("v"), last("a"), last("t"), t_c])
        t_m = load_once(X[0:16, 2, :], I["meta_tokens_3"])
        for e in "va":
            wait(e, [t_m, t_x])

        def tiles():
            return [(X[0:n, i, :], n) for i, n, c in TL]

        def norm_T(gname, xnb, w=()):
            t = rstd(tiles(), 0, D, junk=xnb, w=[last("v"), last("t")])
            return modulated_T([(X[0:n, i, :], n, i, c) for i, n, c in TL],
                               [(0, T3, lambda q: col(gname, q), None)], lambda i: xnb[:, D * i:D * i + D], [t])

        def project(yT, w_out, tls, w, tmp):
            for kk in range(0, 8, 2):
                s = load(w_out[kk * 128:kk * 128 + 256, :].rearrange("(a p) n -> p a n", p=128), 2048, "p (a n) -> p a n", a=2)
                for a in range(2):
                    for i, n, c in tls:
                        for j in range(2):
                            b = 2 * i + j
                            e = mm(PB[b][0:n, :], yT[:, kk + a, c:c + n], s.ap[:, a, 512 * j:512 * j + 512],
                                   kk + a == 0, kk + a == 7, w=[s.tok, bank[b], *w], inc=True)
                s.free = [e]
            for i, n, c in tls:
                for j in range(2):
                    b = 2 * i + j
                    bank[b] = V(tt, X[0:n, i, 512 * j:512 * j + 512], X[0:n, i, 512 * j:512 * j + 512], PB[b][0:n, :], ALU.add, w=[e])
            barrier_all()

        t_h = norm_T("a_norm", big[:, 0:3 * D])
        barrier_all()
        take = arena()
        w_in = I["a_w_in_3"][0]
        pj = take(3, 704)
        qr = take(3, 512)
        kr = take(128)
        qlT = take(3, T3)
        kvT = take(2, T3)
        qrT = take(4, T3)
        krT = take(T3)
        vt = take(3, D)
        yT = take(8, T3)
        for kk in range(0, 8, 2):
            s = load(w_in[kk * 128:kk * 128 + 256, 0:704].rearrange("(a p) n -> p a n", p=128), 1408, "p (a n) -> p a n", a=2)
            for a in range(2):
                for i, n, c in TL:
                    for j, (c0, c1) in enumerate(((0, 384), (384, 704))):
                        e = mm(PB[2 * i + j][0:n, 0:c1 - c0], HT[:, kk + a, c:c + n], s.ap[:, a, c0:c1],
                               kk + a == 0, kk + a == 7, w=[s.tok, bank[2 * i + j]], inc=True)
            s.free = [e]
        for i, n, c in TL:
            bank[2 * i] = V(cp, pj[0:n, i, 0:384], PB[2 * i][0:n, 0:384], w=[e])
            bank[2 * i + 1] = V(cp, pj[0:n, i, 384:704], PB[2 * i + 1][0:n, 0:320])
        for p in range(4):
            s = load(w_in[:, 704 + 256 * p:960 + 256 * p].rearrange("(a p) n -> p a n", p=128), 2048, "p (a n) -> p a n", a=8)
            for f in range(2):
                b = 6 + f
                for kk in range(8):
                    e = mm(PB[b][:, 0:T3], s.ap[:, kk, 128 * f:128 * f + 128], HT[:, kk, 0:T3], kk == 0, kk == 7,
                           w=[s.tok, bank[b]], inc=kk == 7)
                bank[b] = A(yT[:, 2 * p + f, :], PB[b][:, 0:T3], ACT.Silu, w=[e])
            s.free = [e]
        junk = qr.rearrange("p a b -> p (a b)")
        for i, n, c in TL:
            V(tt, junk[0:n, 0:640], pj[0:n, i, 0:640], pj[0:n, i, 0:640], ALU.mult)
            V(ve.tensor_reduce, st[0:n, 2 * i:2 * i + 1], junk[0:n, 0:384], AX, ALU.add)
            V(ve.tensor_reduce, st[0:n, 2 * i + 1:2 * i + 2], junk[0:n, 384:640], AX, ALU.add)
            rstd_of(2 * i, 1, 384, None, parts=n)
            rstd_of(2 * i + 1, 1, 256, None, parts=n)
            V(ts, pj[0:n, i, 0:384], pj[0:n, i, 0:384], st[0:n, 2 * i:2 * i + 1], None, ALU.mult)
            V(ts, pj[0:n, i, 384:640], pj[0:n, i, 384:640], st[0:n, 2 * i + 1:2 * i + 2], None, ALU.mult)
        t = last("v")
        for q in range(5):
            b = q % 2
            for i, n, c in TL:
                e = tp(PB[b][:, c:c + n], pj[0:n, i, 128 * q:128 * q + 128], w=[t, bank[b]], inc=True)
            dst, g = (qlT[:, q, :], col("a_qn", q)) if q < 3 else (kvT[:, q - 3, :], col("a_kvn", q - 3))
            bank[b] = V(ts, dst, PB[b][:, 0:T3], g, None, ALU.mult, w=[e])
        t_l = last("v")
        r3 = k("rope3").rearrange("p (i c d) -> p i c d", i=3, c=2)
        scr = take(2, 256)
        for i, n, c in TL:
            for z in range(2):
                t = rope(kr[0:n, 64 * z:64 * z + 32], kr[0:n, 64 * z + 32:64 * z + 64], pj[0:n, i, 640:672], pj[0:n, i, 672:704],
                         r3[0:n, i, 0, :], r3[0:n, i, 1, :], [scr[0:n, 0, 0:32], scr[0:n, 1, 0:32]], [last("t")])
            e = tp(PB[2][:, c:c + n], kr[0:n, :], w=[t, bank[2]], inc=True)
        bank[2] = V(cp, krT, PB[2][:, 0:T3], w=[e])
        wu = I["a_w_uq_3"][0]
        uq = [load(wu[128 * q:128 * q + 128, :], 1536) for q in range(3)]
        for i, n, c in TL:
            b = 3 + i
            for q in range(3):
                e = mm(PB[b][0:n, :].rearrange("p (h d) -> p h d", h=8), qlT[:, q, c:c + n],
                       uq[q].ap.rearrange("p (h d) -> p h d", h=8)[:, :, 128:192], q == 0, q == 2,
                       w=[uq[q].tok, t_l, bank[b]], inc=True)
            V(cp, qr[0:n, i, :], PB[b][0:n, :], w=[e])
            bank[b] = last("v")
            a = qr[0:n, i, :].rearrange("p (h c d) -> p c h d", c=2, d=32)
            o = pj[0:n, i, 0:512].rearrange("p (h c d) -> p c h d", c=2, d=32)
            t = rope(o[:, 0], o[:, 1], a[:, 0], a[:, 1], r3[0:n, i, 0, None, :].to_broadcast([n, 8, 32]),
                     r3[0:n, i, 1, None, :].to_broadcast([n, 8, 32]),
                     [scr[0:n, 0, :].rearrange("p (h d) -> p h d", h=8), scr[0:n, 1, :].rearrange("p (h d) -> p h d", h=8)], [])
        for q in range(4):
            b = q % 2
            for i, n, c in TL:
                e = tp(PB[b][:, c:c + n], pj[0:n, i, 128 * q:128 * q + 128], w=[t, bank[b]], inc=True)
            bank[b] = V(cp, qrT[:, q, :], PB[b][:, 0:T3], w=[e])
        t_r = last("v")
        wk = I["a_w_ukv_3"][0]
        uk = [load(wk[128 * q:128 * q + 128, :], 2048) for q in range(2)]
        for i, n, c in TL:
            for j in range(2):
                b = 4 + (2 * i + j) % 4
                for q in range(2):
                    e = mm(PB[b][0:n, :].rearrange("p (h d) -> p h d", h=4), kvT[:, q, c:c + n],
                           uk[q].ap.rearrange("p (h z d) -> p h z d", h=8, z=2)[:, 4 * j:4 * j + 4, 1, :], q == 0, q == 1,
                           w=[uk[q].tok, bank[b]], inc=True)
                bank[b] = A(vt[0:n, i, 512 * j:512 * j + 512], PB[b][0:n, :], ACT.Copy, w=[e])
        mask = load(I["mask3"], 3 * T3, "p (i t) -> p i t", i=3)
        barrier_all()
        prob = [qr[:, i, 0:T3] for i in range(3)]
        pT = pj.rearrange("p a b -> p (a b)")[:, 0:3 * T3].rearrange("p (i t) -> p i t", i=3)
        qn, kn = scr.rearrange("p a b -> p (a b)")[:, 0:T3], take(T3)
        SC = float(192) ** -0.5
        for h in range(8):
            for (dst, src, nk, c0, b) in ((qn, qlT, 3, None, 0), (kn, kvT, 2, None, 1)):
                for q in range(nk):
                    wa = uq[q].ap[:, 192 * h:192 * h + 128] if b == 0 else uk[q].ap[:, 256 * h:256 * h + 128]
                    e = mm(PB[b][:, 0:T3], wa, src[:, q, :], q == 0, q == nk - 1, w=[bank[b]], inc=True)
                bank[b] = A(dst, PB[b][:, 0:T3], ACT.Copy, w=[e])
            t_qk = last("a")
            r = 64 * (h % 2)
            for i, n, c in TL:
                b = 2 + i
                mm(PB[b][0:n, 0:T3], qn[:, c:c + n], kn[:, :], True, False, w=[t_qk, bank[b]])
                e = mm(PB[b][0:n, 0:T3], qrT[r:r + 64, h // 2, c:c + n], krT[r:r + 64, :], False, True, inc=True)
                V(stt, prob[i][0:n, :], PB[b][0:n, 0:T3], SC, mask.ap[0:n, i, :], ALU.mult, ALU.add, w=[e, mask.tok, last("t")])
                bank[b] = last("v")
                mx = st[0:n, 40 + i:41 + i]
                V(ve.tensor_reduce, mx, prob[i][0:n, :], AX, ALU.max)
                t = V(ts, mx, mx, -1.0, None, ALU.mult)
                t = A(prob[i][0:n, :], prob[i][0:n, :], ACT.Exp, bias=mx, accum_out=st[0:n, 44 + i:45 + i], w=[t])
                V(ve.reciprocal, mx, st[0:n, 44 + i:45 + i], w=[t])
                t = V(ts, prob[i][0:n, :], prob[i][0:n, :], mx, None, ALU.mult)
            for ki, kn_, kc in TL:
                b = 5 + ki
                for i, n, c in TL:
                    if c >= kc:
                        e = tp(PB[b][0:kn_, c:c + n], prob[i][0:n, kc:kc + kn_], w=[t, bank[b]], inc=True)
                bank[b] = V(cp, pT[0:kn_, ki, kc:T3], PB[b][0:kn_, kc:T3], w=[e])
            t = last("v")
            b = 0
            for z, (ki, kn_, kc) in enumerate((TL[2], TL[0], TL[1])):
                e = mm(PB[b][:, kc:T3], vt[0:kn_, ki, 128 * h:128 * h + 128], pT[0:kn_, ki, kc:T3], z == 0, z == 2,
                       w=[t, bank[b]], inc=True)
            bank[b] = V(tt, yT[:, h, :], PB[b][:, 0:T3], yT[:, h, :], ALU.mult, w=[e])
        for s in uq + uk:
            s.free = [last("t")]
        mask.free = [last("v")]
        dump("yT3", yT, [last("v")])
        project(yT, I["a_w_out_3"][0], TL, [last("v")], None)
        dump("mla", X[:, 0:2, :], [last("v")])

        norm_T("b_norm", big[:, 0:3 * D])
        barrier_all()
        take = arena()
        uT = take(8, T3)
        gT = take(8, T3)
        pad = [take(T3 + 3) for _ in range(2)]
        al = take(2, T3)
        ml = take(2, T3)
        bl = take(2, T3)
        sp = take(8)
        z8 = take(3, 8)
        w_in = I["b_w_in_3"][0]
        lam = col("lam", 0, 8)
        V(ts, sp, lam, 0.0, None, ALU.min)
        t = V(stt, z8[:, 0, :], sp, 2.0, lam, ALU.mult, ALU.subtract)
        t = A(z8[:, 0, :], z8[:, 0, :], ACT.Exp, w=[t])
        l8 = take(8)
        log1p(z8[:, 0, :], z8[:, 1, :], z8[:, 2, :], l8, [t])
        V(tt, sp, l8, sp, ALU.subtract)
        V(ts, sp, sp, -8.0, None, ALU.mult)
        V(ve.memset, pad[0][:, 0:3], 0.0)
        V(ve.memset, pad[1][:, 0:3], 0.0)
        for p in range(4):
            su = load(w_in[:, 256 * p:256 * p + 256].rearrange("(a p) n -> p a n", p=128), 2048, "p (a n) -> p a n", a=8)
            sg = load(w_in[:, D + 256 * p:D + 256 * p + 256].rearrange("(a p) n -> p a n", p=128), 2048, "p (a n) -> p a n", a=8)
            for f in range(2):
                o = 2 * p + f
                b = 2 * (o % 4)
                for kk in range(8):
                    e = mm(PB[b][:, 0:T3], su.ap[:, kk, 128 * f:128 * f + 128], HT[:, kk, 0:T3], kk == 0, kk == 7,
                           w=[su.tok, bank[b]], inc=kk == 7)
                su.free = [e]
                P_ = pad[f]
                V(cp, P_[:, 3:3 + T3], PB[b][:, 0:T3], w=[e])
                bank[b] = last("v")
                V(ts, uT[:, o, :], P_[:, 0:T3], col("conv_w_3", o), col("conv_b_3", o), ALU.mult, ALU.add)
                for j in range(1, 4):
                    V(stt, uT[:, o, :], P_[:, j:j + T3], col("conv_w_3", 8 * j + o), uT[:, o, :], ALU.mult, ALU.add)
                for kk in range(8):
                    e = mm(PB[b + 1][:, 0:T3], sg.ap[:, kk, 128 * f:128 * f + 128], HT[:, kk, 0:T3], kk == 0, kk == 7,
                           w=[sg.tok, bank[b + 1]], inc=kk == 7)
                sg.free = [e]
                bank[b + 1] = A(gT[:, o, :], PB[b + 1][:, 0:T3], ACT.Silu, w=[e])
        t_u = last("v")
        rg = load(I["b_w_rg_3"][0].rearrange("g (a p) n -> p g a n", p=128), 2048, "p (g a n) -> p g a n", g=4, a=2)
        ig = load(I["b_w_ig_3"][0].rearrange("g (a p) n -> p g a n", p=128), 2048, "p (g a n) -> p g a n", g=4, a=2)
        for o in range(8):
            g, f, z = o // 2, o % 2, o % 2
            b = 2 * (o % 4)
            for q, (s, bb) in enumerate(((rg, b), (ig, b + 1))):
                for kk in range(2):
                    e = mm(PB[bb][:, 0:T3], s.ap[:, g, kk, 128 * f:128 * f + 128], uT[:, 2 * g + kk, :], kk == 0, kk == 1,
                           w=[s.tok, t_u, bank[bb]], inc=True)
            a_, m_, b_ = al[:, z, :], ml[:, z, :], bl[:, z, :]
            A(a_, PB[b][:, 0:T3], ACT.Sigmoid, bias=col("b_rg", o), w=[e, last("v")])
            t = A(b_, PB[b + 1][:, 0:T3], ACT.Sigmoid, bias=col("b_ig", o))
            bank[b] = bank[b + 1] = t
            t = V(ts, a_, a_, sp[:, o:o + 1], None, ALU.mult, w=[t])
            V(tt, b_, b_, uT[:, o, :], ALU.mult)
            A(m_, a_, ACT.Tanh, w=[t])
            t = A(a_, a_, ACT.Exp)
            t2 = V(tt, pad[0][:, 3:3 + T3], a_, a_, ALU.mult, w=[t])
            V(stt, pad[0][:, 3:3 + T3], pad[0][:, 3:3 + T3], 1.0, m_, ALU.add, ALU.mult)
            t = V(ts, m_, pad[0][:, 3:3 + T3], -1.0, None, ALU.mult)
            t = A(m_, m_, ACT.Sqrt, w=[t])
            V(ve.memset, m_[:, 0:1], 1.0, w=[t])
            V(tt, b_, b_, m_, ALU.mult)
            V(ve.tensor_tensor_scan, m_, a_, b_, 0.0, ALU.mult, ALU.add)
            V(tt, gT[:, o, :], gT[:, o, :], m_, ALU.mult)
        rg.free = ig.free = [e]
        dump("gT3", gT, [last("v")])
        project(gT, I["b_w_out_3"][0], TL[0:2], [last("v")], None)
        fg = load(I["rows"][:, RO["final_g"]:RO["final_g"] + 1024], 1024)
        t = rstd([(X[:, i, :], 128) for i in range(2)], 0, D, junk=uT.rearrange("p a b -> p (a b)"))
        for i in range(2):
            t = V(stt, X[:, i, :], X[:, i, :], st[:, i:i + 1], fg.ap, ALU.mult, ALU.mult, w=[fg.tok])
        fg.free = [t]
        store(out.rearrange("a (t p) d -> p (a t) d", p=128), X[:, 0:2, :], [t])

    for nm, fn in (("first", first), ("second", second), ("third", third)):
        if only is None or nm in only:
            fn()
    for s in stores:
        nc.sync.wait_ge(s, 16)


WEIGHTS = ["x", "ctx", "w_mod", "w_in", "w_out", "w_router", "w1", "w3", "w2", "ctx_2", "w_ada_2", "w13_a_2", "w2_a_2",
           "w_in_2", "w_four_2", "w_mproj_2", "w_out_2", "w13_b_2", "w2_b_2", "meta_tokens_3", "a_w_in_3", "a_w_uq_3",
           "a_w_ukv_3", "a_w_out_3", "b_w_in_3", "b_w_rg_3", "b_w_ig_3", "b_w_out_3"]


def constants():
    f = np.float32
    K = {n: np.zeros((128, w), f) for n, w in CONSTS}
    K["ident"][:] = np.eye(128)
    K["ones"][:] = 1
    inv = (f(10000.0) ** (-np.arange(16, dtype=f) / f(16))).astype(f)
    tok = np.arange(256)
    ang = np.concatenate([(tok // 64).astype(f)[:, None] * inv, (tok % 64).astype(f)[:, None] * inv], 1).astype(f)
    K["rope1"][:] = np.stack([np.cos(ang), np.sin(ang)], 1).reshape(2, 128, 64).transpose(1, 0, 2).reshape(128, 128)
    inv = (f(10000.0) ** (-np.arange(0, 64, 2, dtype=f) / f(64))).astype(f)
    r3 = np.zeros((128, 3, 2, 32), f)
    for i, n, c in ((0, 128, 16), (1, 128, 144), (2, 16, 0)):
        a = (np.arange(c, c + n, dtype=f)[:, None] * inv).astype(f)
        r3[:n, i, 0], r3[:n, i, 1] = np.cos(a), np.sin(a)
    K["rope3"][:] = r3.reshape(128, 192)
    K["slot"][:] = np.arange(1, 33)
    s, t = np.arange(128)[:, None], np.arange(128)[None, :]
    K["tri"][:] = np.concatenate([np.where(s <= t, 0, NEG), np.where(s >= t, 0, NEG)], 1)
    for i in range(8):
        p = 32 * (i // 4) + i % 4
        K["selg"][p, 128 * i:128 * i + 128] = 1
        K["m8"][p, i] = 1
    consts = np.concatenate([K[n] for n, _ in CONSTS], 1)
    mask = np.full((128, 3, 272), NEG, f)
    for i, n, c in ((0, 128, 16), (1, 128, 144), (2, 16, 0)):
        mask[:n, i] = np.where(np.arange(272)[None, :] <= np.arange(c, c + n)[:, None], 0, NEG)
    r, w = np.arange(256) // 64, np.arange(256) % 64
    th = 2 * np.pi * (np.outer(r, r) / 4 + np.outer(w, w) / 64)
    ct = np.concatenate([np.cos(th), np.sin(th)], 1).reshape(2, 128, 512).transpose(1, 0, 2).reshape(128, 1024)
    pc = 2 * np.pi * np.outer(np.arange(128), np.arange(128)) / 128
    nrm = 1 / np.sqrt(256 * 128)
    four = np.concatenate([ct, np.cos(pc) * nrm, -np.sin(pc) * nrm], 1).astype(f)
    return {"consts": consts, "mask3": mask.reshape(128, 816), "four": four}


def layout(I):
    def c(v):
        v = np.asarray(v).reshape(-1)
        return v.reshape(-1, 128).T
    b_in = np.asarray(I["b_in_2"])[0]
    gate = np.zeros((128, 2), b_in.dtype)
    for d in range(2):
        for q in range(2):
            gate[32 * d:32 * d + 4, q] = b_in[4608 + 8 * d + 4 * q:4612 + 8 * d + 4 * q]
    parts = {"c": c(I["c"]), "c_ctx": c(I["c_ctx"]), "b_mod": c(I["b_mod"]), "g_mix": c(I["g_mix"]),
             "g_ffn": c(I["g_ffn"]), "c_2": c(I["c_2"]), "c_ctx_2": c(I["c_ctx_2"]), "b_ada_2": c(I["b_ada_2"]),
             "norm_g_2": c(I["norm_g_2"]), "b_q": c(b_in[512:1536]), "b_k": c(b_in[1536:2560]),
             "b_gf": c(b_in[4624:5648]), "b_gm": c(b_in[5648:6672]), "conv_w_2": c(I["conv_w_2"]),
             "conv_b_2": c(I["conv_b_2"]), "b_s": np.asarray(I["b_s"])[0].T, "a_norm": c(I["a_norm_g_3"]),
             "a_qn": c(I["a_q_norm_g_3"]), "a_kvn": c(I["a_kv_norm_g_3"]), "b_norm": c(I["b_norm_g_3"]),
             "conv_w_3": c(I["b_conv_w_3"]), "conv_b_3": c(I["b_conv_b_3"]), "b_rg": c(I["b_b_rg_3"]),
             "b_ig": c(I["b_b_ig_3"]), "lam": c(I["b_lam_3"]), "b_gate": gate}
    cols = np.concatenate([parts[n] for n, _ in COLS], 1)
    rows = {"q_gain": np.tile(np.asarray(I["q_gain"])[0], 8), "k_gain": np.tile(np.asarray(I["k_gain"])[0], 2),
            "v_gain": np.asarray(I["v_gain"])[0], "g_final": I["g_final"], "b_f": b_in[0:512], "b_v": b_in[2560:3584],
            "b_o": b_in[3584:4608], "head_g": np.asarray(I["head_g_2"])[0], "final_g": I["final_norm_g_3"]}
    row = np.concatenate([np.asarray(rows[n]) for n, _ in ROWS])
    return {"cols": np.ascontiguousarray(cols), "rows": np.ascontiguousarray(np.broadcast_to(row, (128, NROW))),
            "w_sT": np.ascontiguousarray(np.asarray(I["w_s"])[0].transpose(2, 0, 1).reshape(128, 1024))}


def arrays_of(inputs):
    out = {n: np.ascontiguousarray(inputs[n]) for n in WEIGHTS}
    out.update(layout(inputs))
    out.update(constants())
    return out


def kernel(**inputs):
    import concourse.bacc as _bacc
    from concourse.bass_utils import run_bass_kernel_spmd as _run

    nc = _bacc.Bacc("TRN2", target_bir_lowering=False, num_devices=1)
    arrays, I = {}, {}
    for name, a in arrays_of(inputs).items():
        arrays[f"in_{name}"] = a
        I[name] = nc.dram_tensor(f"in_{name}", a.shape, mybir.dt.from_np(a.dtype), kind="ExternalInput").ap()
    o = nc.dram_tensor("out_0", (1, 256, D), F32, kind="ExternalOutput").ap()
    build(nc, I, o)
    r = _run(nc, [arrays], core_ids=[0])
    return r.results[0]["out_0"]
```

```python
from contextlib import ExitStack

import numpy as np
import concourse.bass as bass
from concourse import mybir

F32 = mybir.dt.float32
F32R = mybir.dt.float32r
ALU = mybir.AluOpType
ACT = mybir.ActivationFunctionType
AX = mybir.AxisListType.X
D = 1024
NSLOT = 6
BIG = 13200
NEG = -1e30

COLS = [("c", 8), ("c_ctx", 8), ("b_mod", 48), ("g_mix", 8), ("g_ffn", 8),
        ("c_2", 8), ("c_ctx_2", 8), ("b_ada_2", 72), ("norm_g_2", 48), ("b_q", 8), ("b_k", 8), ("b_gf", 8),
        ("b_gm", 8), ("conv_w_2", 48), ("conv_b_2", 16), ("b_s", 8),
        ("a_norm", 8), ("a_qn", 3), ("a_kvn", 2), ("b_norm", 8), ("conv_w_3", 32), ("conv_b_3", 8),
        ("b_rg", 8), ("b_ig", 8), ("lam", 8), ("b_gate", 2)]
CO, _n = {}, 0
for _name, _w in COLS:
    CO[_name] = _n
    _n += _w
NCOL = _n
ROWS = [("q_gain", 512), ("k_gain", 128), ("v_gain", 512), ("g_final", 1024), ("b_v", 1024),
        ("b_o", 1024), ("head_g", 1024), ("b_f", 512), ("final_g", 1024)]
RO, _n = {}, 0
for _name, _w in ROWS:
    RO[_name] = _n
    _n += _w
NROW = _n
CONSTS = [("ident", 128), ("ones", 128), ("rope1", 128), ("rope3", 192), ("slot", 32), ("tri", 256),
          ("m8", 8), ("sel_i", 36), ("sel_f", 36)]
KO, _n = {}, 0
for _name, _w in CONSTS:
    KO[_name] = _n
    _n += _w
NCONST = _n


def build(nc, I, out, dbg=None):
    ctx = ExitStack()
    with ctx:
        _build(nc, I, out, ctx, dbg)


def _build(nc, I, out, ctx, dbg):
    def sb(name, shape, dt=F32):
        return ctx.enter_context(nc.sbuf_tensor(name, shape, dt))

    def sem(name):
        return ctx.enter_context(nc.semaphore(name))

    ring = sb("ring", [128, NSLOT, 2048])
    X = sb("X", [128, 4, D])
    HH = sb("HH", [128, 8, 512], F32R)
    HL = sb("HL", [128, 8, 512], F32R)
    WB = sb("WB", [128, 2, 2, 2048], F32R)
    RB = sb("RB", [128, 2, 2, 512], F32R)
    big = sb("big", [128, BIG])
    cols = sb("cols", [128, NCOL])
    K = sb("K", [128, NCONST])
    cs = sb("cs", [128, 2, 8, 2])
    mraw = sb("mraw", [128, 512])
    mcol1 = sb("mcol1", [128, 48, 2])
    mcol2 = sb("mcol2", [128, 72, 2])
    AB = sb("AB", [128, 64])
    BO = sb("BO", [128, 36])
    st = sb("st", [128, 64])
    PB = [ctx.enter_context(nc.psum_tensor(f"pb{i}", [128, 512], F32)) for i in range(8)]

    eng = {"v": nc.vector, "a": nc.scalar, "g": nc.gpsimd, "t": nc.tensor, "s": nc.sync}
    esem = {e: sem("s_" + e) for e in "vagt"}
    count = {e: 0 for e in "vagt"}
    waited = {e: {} for e in "vagts"}

    def wait(e, toks):
        for t in toks:
            if t is None:
                continue
            s, n, key = t
            if waited[e].get(key, 0) < n:
                eng[e].wait_ge(s, n)
                waited[e][key] = n

    def done(e, ins):
        count[e] += 1
        ins.then_inc(esem[e], 1)
        return (esem[e], count[e], e)

    def last(e):
        return (esem[e], count[e], e) if count[e] else None

    def V(name, *args, w=(), **kw):
        wait("v", [last("v"), *w])
        return done("v", name(*args, **kw))

    def A(out_, in_, func, w=(), **kw):
        wait("a", [last("a"), *w])
        return done("a", nc.scalar.activation(out_, in_, func, **kw))

    def G(name, *args, w=(), **kw):
        wait("g", [last("g"), *w])
        return done("g", name(*args, **kw))

    def mm(o, l, r, start=True, stop=True, w=(), inc=False):
        wait("t", w)
        i = nc.tensor.matmul(o, l, r, start=start, stop=stop)
        return done("t", i) if inc else None

    def tp(o, in_, w=(), inc=False):
        n = in_.shape[0]
        wait("t", w)
        i = nc.tensor.transpose(o, in_, ident[0:n, 0:n])
        return done("t", i) if inc else None

    ve = nc.vector
    tt, ts, stt, cp = ve.tensor_tensor, ve.tensor_scalar, ve.scalar_tensor_tensor, ve.tensor_copy

    nload = [0]
    stores = []

    def store(dst, src, w):
        wait("s", w)
        s = sem(f"st{len(stores)}")
        nc.sync.dma_start(dst, src).then_inc(s, 16)
        stores.append(s)
        return (s, 16, f"st{len(stores)}")

    def dump(name, ap, w):
        if dbg is not None and name in dbg:
            t = store(dbg[name], ap, w)
            wait("v", [t])
            wait("a", [t])

    def load_once(dst, src):
        nload[0] += 1
        s = sem(f"ld{nload[0]}")
        nc.sync.dma_start(dst, src).then_inc(s, 16)
        return (s, 16, f"ld{nload[0]}")

    class Slot:
        pass

    slot_sem = [sem(f"rs{i}") for i in range(NSLOT)]
    slot_use = [0] * NSLOT
    slot_last = [None] * NSLOT
    nslot = [0]

    def load(src, n, pat=None, parts=128, **dims):
        while slot_last[nslot[0] % NSLOT] is not None and slot_last[nslot[0] % NSLOT].free is None:
            nslot[0] += 1
        i = nslot[0] % NSLOT
        nslot[0] += 1
        if slot_last[i] is not None:
            wait("s", slot_last[i].free)
        s = Slot()
        s.i = i
        ap = ring[0:parts, i, 0:n]
        s.ap = ap.rearrange(pat, **dims) if pat else ap
        nc.sync.dma_start(s.ap, src).then_inc(slot_sem[i], 16)
        slot_use[i] += 16
        s.tok = (slot_sem[i], slot_use[i], f"rs{i}")
        s.free = None
        slot_last[i] = s
        return s

    def scratch():
        while slot_last[nslot[0] % NSLOT] is not None and slot_last[nslot[0] % NSLOT].free is None:
            nslot[0] += 1
        i = nslot[0] % NSLOT
        nslot[0] += 1
        s = Slot()
        s.ap = ring[:, i, :]
        s.tok = None
        if slot_last[i] is not None:
            for e in "va":
                wait(e, [*slot_last[i].free, slot_last[i].tok])
        s.free = None
        slot_last[i] = s
        return s

    class Halves:
        pass

    wb_free = [None, None]

    class Stream:

        def __init__(self, specs):
            self.specs, self.n, self.out = specs, 0, []

        def ahead(self):
            if self.n == len(self.specs):
                return
            src, n, pat, dims = self.specs[self.n]
            s = load(src, n, pat, **dims)
            b = wbn[0] % 2
            wbn[0] += 1
            assert wb_free[b] != "held"
            h = Halves()
            h.b = b
            flat = ring[:, s.i, :]
            h.toks = []
            m = (n // 2 + 1) // 2 * 2
            for (x, y) in ((0, m), (m, n)):
                ta = A(WB[:, b, 0, x:y], flat[:, x:y], ACT.Copy, w=[s.tok, wb_free[b]])
                tv = V(tt, WB[:, b, 1, x:y], flat[:, x:y], WB[:, b, 0, x:y].bitcast(F32), ALU.subtract,
                       w=[ta, s.tok, wb_free[b]])
                h.toks.append((ta, tv))
            s.free = [ta, tv]
            h.H, h.L = WB[:, b, 0, 0:n], WB[:, b, 1, 0:n]
            if pat:
                h.H, h.L = h.H.rearrange(pat, **dims), h.L.rearrange(pat, **dims)
            wb_free[b] = "held"
            self.out.append(h)
            self.n += 1

        def get(self, i, ahead=True):
            while self.n <= i:
                self.ahead()
            if self.n == i + 1 and ahead:
                self.ahead()
            return self.out[i]

        def done(self, i, t):
            wb_free[self.out[i].b] = t

    wbn = [0]

    def mm3(o, l, r, start, stop, w=(), inc=False):
        mm(o, l[0], r[0], start, False, w=w)
        mm(o, l[0], r[1], False, False)
        return mm(o, l[1], r[0], False, stop, inc=inc)

    rbn = [0]
    rb_free = [None, None]

    def halves(x, n, w):
        b = rbn[0] % 2
        rbn[0] += 1
        ta = A(RB[:, b, 0, 0:n], x, ACT.Copy, w=[*w, rb_free[b]])
        tv = V(tt, RB[:, b, 1, 0:n], x, RB[:, b, 0, 0:n].bitcast(F32), ALU.subtract, w=[ta, *w, rb_free[b]])
        return b, (RB[:, b, 0, 0:n], RB[:, b, 1, 0:n]), [ta, tv]

    bank = [None] * 8

    def barrier():
        return [last(e) for e in "vagt"]

    def barrier_all():
        b = barrier()
        for e in "vagt":
            wait(e, b)

    t_k = load_once(K[:], I["consts"])
    t_cols = load_once(cols[:], I["cols"])
    xv = I["x"].rearrange("a (t p) d -> p (a t) d", p=128)
    xc = I["ctx"].rearrange("a (t p) d -> p (a t) d", p=128)
    t_x = load_once(X[:, 0:2, :], xv)
    t_c = load_once(X[:, 2:4, :], xc)

    def k(name, n=None):
        w = dict(CONSTS)[name]
        return K[:, KO[name]:KO[name] + (n or w)]

    ident = k("ident")
    ones = k("ones")

    def col(name, i=0, n=1):
        return cols[:, CO[name] + i:CO[name] + i + n]

    def arena(start=0):
        at = [start]

        def take(*shape, parts=128):
            n = 1
            for s in shape:
                n *= s
            ap = big[0:parts, at[0]:at[0] + n]
            at[0] += n
            assert at[0] <= BIG, at[0]
            if len(shape) == 2:
                ap = ap.rearrange("p (a b) -> p a b", a=shape[0])
            elif len(shape) == 3:
                ap = ap.rearrange("p (a b c) -> p a b c", a=shape[0], b=shape[1])
            return ap
        return take

    for e in "vagt":
        wait(e, [t_k, t_cols])
    wait("a", [V(ve.memset, st[:], 1.0)])

    def rstd(tiles, base, d, w=(), junk=None, eps=1e-6):
        t = None
        for i, (ap, n) in enumerate(tiles):
            t = A(junk[0:n, 0:d], ap, ACT.Square, accum_out=st[0:n, base + i:base + i + 1], w=w)
        return rstd_of(base, len(tiles), d, t, eps)

    def rstd_of(base, n, d, t, eps=1e-6, src=None, dst=None, parts=128):
        s = st[0:parts, base:base + n] if src is None else src
        t = V(ts, s, s, 1.0 / d, eps, ALU.mult, ALU.add, w=[t])
        t = A(s, s, ACT.Sqrt, w=[t])
        return V(ve.reciprocal, s, s, w=[t])

    def transposed(tiles, regions, xn, w, ready, f32=None, both=True):
        c0, c1 = regions[0][0], regions[-1][1]
        late = None
        for kk in range(8):
            b = kk % 4
            for i, (ap, n, r, c) in enumerate(tiles):
                t = tp(PB[b][:, c:c + n], xn(i)[0:n, kk * 128:kk * 128 + 128], w=[ready[i], bank[b]], inc=True)
            v = tmpT[:, kk % 2, :] if f32 is None else f32[:, kk, :]
            for (x, y, a, s) in regions:
                if s is None:
                    t2 = V(ts, v[:, x:y], PB[b][:, x:y], a(kk), None, ALU.mult, w=[t, ta_T[kk % 2]])
                else:
                    t2 = V(ts, v[:, x:y], PB[b][:, x:y], a(kk), s(kk), ALU.mult, ALU.add, w=[t, ta_T[kk % 2]])
            bank[b] = t2
            if both:
                ta = A(HH[:, kk, c0:c1], v[:, c0:c1], ACT.Copy, w=[t2, *w])
                ta_T[kk % 2] = ta
                if late:
                    late()
                late = (lambda kk=kk, v=v, ta=ta: V(tt, HL[:, kk, c0:c1], v[:, c0:c1], HH[:, kk, c0:c1].bitcast(F32),
                                                    ALU.subtract, w=[ta, *w]))
        if both:
            t2 = late()
        return t2

    tmpT = sb("tmpT", [128, 2, 512])
    ta_T = [None, None]

    def scaled(tiles, xn, w):
        ready = []
        for i, (ap, n, r, c) in enumerate(tiles):
            if i % 2 == 0:
                ready.append(V(ts, xn(i)[0:n, :], ap, st[0:n, r:r + 1], None, ALU.mult, w=w))
            else:
                ready.append(A(xn(i)[0:n, :], ap, ACT.Copy, scale=st[0:n, r:r + 1], w=w))
        return ready

    def modulated_T(tiles, regions, xn, w, f32=None, both=True):
        ready = scaled(tiles, xn, w)
        return transposed(tiles, regions, xn, [last("t")], ready, f32, both)

    def gemv(w_dram, which, bname, nchunk, mcol, acc):
        for nb in range((nchunk + 3) // 4):
            q = min(4, nchunk - 4 * nb)
            for kk in range(8):
                s = load(w_dram[kk * 128:kk * 128 + 128, nb * 2048:nb * 2048 + q * 512], q * 512)
                for j in range(q):
                    e = mm(PB[acc][32 * j:32 * j + 2, :], cs[:, which, kk, :], s.ap[:, 512 * j:512 * j + 512],
                           kk == 0, kk == 7, w=[s.tok, bank[acc]], inc=j == q - 1)
                s.free = [e]
                yield
            for j in range(q):
                f = A(mraw[32 * j:32 * j + 2, :], PB[acc][32 * j:32 * j + 2, :], ACT.Copy, w=[e, last("t")])
            bank[acc] = f
            for j in range(q):
                for i in range(4):
                    e = mm(PB[acc][:, 2 * i:2 * i + 2], mraw[32 * j:32 * j + 2, 128 * i:128 * i + 128],
                           ident[32 * j:32 * j + 2, 32 * j:32 * j + 2], w=[f, bank[acc]], inc=i == 3)
                c = 16 * nb + 4 * j
                bank[acc] = V(tt, mcol[:, c:c + 4, :], PB[acc][:, 0:8].rearrange("p (i c) -> p i c", c=2),
                              col(bname, c, 4)[:, :, None].to_broadcast([128, 4, 2]), ALU.add, w=[e])
                wait("t", [bank[acc]])
            yield

    def run(g):
        for _ in g:
            pass

    def steps(g, n):
        for _ in range(n):
            next(g, None)

    def row_of(dst, c8, tmp, w, bank_=3):
        for kk in range(8):
            d = tmp[:, (kk % 2) * 128:(kk % 2) * 128 + 128]
            t = V(ts, d, ident, c8[:, kk:kk + 1], None, ALU.mult, w=[*w, last("t")])
            e = mm(PB[bank_][:, (kk % 4) * 128:(kk % 4) * 128 + 128], ones, d, w=[t, bank[bank_]], inc=True)
            if kk % 4 == 3:
                bank[bank_] = A(dst[:, (kk - 3) * 128:(kk + 1) * 128], PB[bank_][:, :], ACT.Copy, w=[e])
        return bank[bank_]

    def rope(dst1, dst2, x1, x2, cos, sin, t1, w):
        V(tt, t1[0], x1, cos, ALU.mult, w=w)
        V(tt, t1[1], x2, sin, ALU.mult)
        V(tt, dst1, t1[0], t1[1], ALU.subtract)
        V(tt, t1[0], x1, sin, ALU.mult)
        V(tt, t1[1], x2, cos, ALU.mult)
        return V(tt, dst2, t1[0], t1[1], ALU.add)

    only = dbg.get("only") if dbg else None

    def XT(kk, c, n=128):
        return HH[:, kk, c:c + n], HL[:, kk, c:c + n]

    def both(*gens):
        gens = list(gens)
        while gens:
            for g in list(gens):
                try:
                    next(g)
                except StopIteration:
                    gens.remove(g)

    def rows2(w, c0=0, n=D):
        return [(w[q * 256:q * 256 + 256, c0:c0 + n].rearrange("(a p) n -> p a n", p=128), 2 * n, "p (a n) -> p a n",
                 dict(a=2)) for q in range(w.shape[0] // 256)]

    def cols256(w, c0, a=8, n=256):
        return (w[:, c0:c0 + n].rearrange("(a p) n -> p a n", p=128), a * n, "p (a n) -> p a n", dict(a=a))

    def first():
        for i, (l, c) in enumerate((("c", "c_ctx"), ("c_2", "c_ctx_2"))):
            A(cs[:, i, :, 0], col(l, 0, 8), ACT.Silu)
            t = A(cs[:, i, :, 1], col(c, 0, 8), ACT.Silu)
        wait("t", [t])
        take = arena()
        xn = take(4, D)
        tl = [(X[:, i, :], 128, i, 128 * i) for i in range(4)]
        t = rstd([(X[:, i, :], 128) for i in range(4)], 0, D, w=[t_x, t_c], junk=xn[:, 0, :])
        ready = scaled(tl, lambda i: xn[:, i, :], [t])
        wait("s", ready)
        t_c2 = load_once(X[:, 2:4, :], I["ctx_2"].rearrange("a (t p) d -> p (a t) d", p=128))
        run(gemv(I["w_mod"][0], 0, "b_mod", 12, mcol1, 7))
        for i, (g, ch, which) in enumerate((("g_mix", 1, 0), ("g_mix", 1, 1), ("g_ffn", 4, 0))):
            V(stt, AB[:, 8 * i:8 * i + 8], mcol1[:, 8 * ch:8 * ch + 8, which], 1.0, col(g, 0, 8), ALU.add, ALU.mult)
        t_h = transposed(tl, [(0, 256, lambda q: AB[:, q:q + 1], lambda q: mcol1[:, q, 0:1]),
                              (256, 512, lambda q: AB[:, 8 + q:9 + q], lambda q: mcol1[:, q, 1:2])],
                         lambda i: xn[:, i, :], [], ready)
        barrier_all()
        g2 = gemv(I["w_ada_2"][0], 1, "b_ada_2", 18, mcol2, 7)
        take = arena()
        qkv = take(4, 768)
        gm = take(2, D)
        w_in = I["w_in"][0]
        S = Stream(rows2(w_in, 0, 768) + rows2(w_in, 768, 1024) + rows2(I["w_out"][0]))
        for q in range(4):
            w_ = S.get(q)
            for a in range(2):
                kk = 2 * q + a
                for i in range(2):
                    mm3(PB[i][:, :], XT(kk, 128 * i), (w_.H[:, a, 0:512], w_.L[:, a, 0:512]), kk == 0, kk == 7,
                        w=[*w_.toks[a], bank[i]])
                for i in range(4):
                    e = mm3(PB[2 + i][:, 0:256], XT(kk, 128 * i), (w_.H[:, a, 512:768], w_.L[:, a, 512:768]),
                            kk == 0, kk == 7, w=[bank[2 + i]], inc=i == 3)
            S.done(q, e)
            steps(g2, 2)
        for i in range(2):
            bank[i] = A(qkv[:, i, 0:512], PB[i][:, :], ACT.Copy, w=[e])
        for i in range(4):
            bank[2 + i] = V(cp, qkv[:, i, 512:768], PB[2 + i][:, 0:256], w=[e])
        t_qkv = [bank[1], bank[5]]
        GB = (6, 0, 1, 2)
        for q in range(4):
            w_ = S.get(4 + q)
            for a in range(2):
                kk = 2 * q + a
                for i in range(2):
                    for j in range(2):
                        b = GB[2 * i + j]
                        e = mm3(PB[b][:, :], XT(kk, 128 * i), (w_.H[:, a, 512 * j:512 * j + 512], w_.L[:, a, 512 * j:512 * j + 512]),
                                kk == 0, kk == 7, w=[*w_.toks[a], bank[b]], inc=i + j == 2)
            S.done(4 + q, e)
            steps(g2, 2)
        t_proj = e
        for i in range(2):
            for j in range(2):
                b = GB[2 * i + j]
                bank[b] = A(gm[:, i, 512 * j:512 * j + 512], PB[b][:, :], ACT.Gelu, w=[e])
        t_gm = bank[GB[3]]
        nrm = take(640)
        cos = [k("rope1")[:, 64 * i:64 * i + 32] for i in range(2)]
        sin = [k("rope1")[:, 64 * i + 32:64 * i + 64] for i in range(2)]
        qT = take(4, 256)
        kT = take(512)
        qp = take(512)
        kp = take(128)
        gains = load(I["rows"][:, 0:1152], 1152)
        s1, s2 = take(256), take(256)
        pr = [[take(512), take(512)] for _ in range(2)]
        pT = [take(4, 256), take(4, 256)]
        junk = pT[0].rearrange("p a b -> p (a b)")
        for i in range(4):
            n0 = 0 if i < 2 else 512
            nh = 10 if i < 2 else 2
            src = qkv[:, i, n0:640]
            dst = nrm[:, n0:640]
            ss = st[:, 16:16 + nh]
            V(tt, junk[:, 0:nh * 64], src, src, ALU.mult, w=t_qkv)
            t = V(ve.tensor_reduce, ss, junk[:, 0:nh * 64].rearrange("p (h d) -> p h d", d=64), AX, ALU.add)
            t = rstd_of(0, 0, 64, t, src=ss)
            V(tt, dst.rearrange("p (h d) -> p h d", d=64), src.rearrange("p (h d) -> p h d", d=64),
              ss[:, :, None].to_broadcast([128, nh, 64]), ALU.mult)
            t = V(tt, dst, dst, gains.ap[:, n0:640], ALU.mult, w=[gains.tok])
            if i < 2:
                for (src, dst, hn) in ((nrm[:, 0:512], qp, 8), (nrm[:, 512:640], kp, 2)):
                    a = src.rearrange("p (h c d) -> p c h d", c=2, d=32)
                    for j in range(2 if hn == 8 else 1):
                        o = (dst.rearrange("p (i j c d) -> p c j i d", j=2, c=2, d=32)[:, :, j] if hn == 8 else
                             dst.rearrange("p (h c d) -> p c h d", c=2, d=32))
                        m = hn // 2 if hn == 8 else hn
                        cc = cos[i][:, None, :].to_broadcast([128, m, 32])
                        si = sin[i][:, None, :].to_broadcast([128, m, 32])
                        sc = [z[:, 0:32 * m].rearrange("p (h d) -> p h d", h=m) for z in (s1, s2)]
                        t = rope(o[:, 0], o[:, 1], a[:, 0, 4 * j:4 * j + m], a[:, 1, 4 * j:4 * j + m], cc, si, sc, [last("t")])
                for c in range(4):
                    e = tp(PB[2][:, 128 * c:128 * c + 128], qp[:, 128 * c:128 * c + 128], w=[t, bank[2]], inc=True)
                bank[2] = A(qT[:, :, 128 * i:128 * i + 128], PB[2][:, :].rearrange("p (c t) -> p c t", c=4), ACT.Copy, w=[e])
                e = tp(PB[3][:, 0:128], kp, w=[t, bank[3]], inc=True)
            else:
                e = tp(PB[3][:, 0:128], nrm[:, 512:640], w=[t, bank[3]], inc=True)
                wait("v", [e])
            bank[3] = A(kT[:, 128 * i:128 * i + 128], PB[3][:, 0:128], ACT.Copy, w=[e])
            steps(g2, 3)
        t_q = last("a")
        dump("kT1", kT, [t_q])
        soft = [None] * 8

        def scores(h):
            pl, r = h % 4, 64 * (h // 4)
            for i in range(2):
                e = mm(PB[i][:, :], qT[r:r + 64, pl, 128 * i:128 * i + 128], kT[r:r + 64, :], w=[t_q, bank[i]], inc=True)
                mx, p = st[:, 32 + i:33 + i], pr[h % 2][i]
                V(ve.tensor_reduce, mx, PB[i][:, :], AX, ALU.max, w=[e])
                t = V(ts, mx, mx, -0.125, None, ALU.mult)
                bank[i] = A(p, PB[i][:, :], ACT.Exp, bias=mx, scale=0.125, accum_out=st[:, 34 + i:35 + i], w=[t, soft[h - 2] if h > 1 else None])
                V(ve.reciprocal, st[:, 36 + i:37 + i], st[:, 34 + i:35 + i], w=[bank[i]])
                t = V(ts, p, p, st[:, 36 + i:37 + i], None, ALU.mult)
            return t

        def values(h, t):
            for i in range(2):
                for s_ in range(4):
                    e = tp(PB[2 + i][:, 128 * s_:128 * s_ + 128], pr[h % 2][i][:, 128 * s_:128 * s_ + 128], w=[t, bank[2 + i]], inc=True)
                bank[2 + i] = A(pT[h % 2][:, :, 128 * i:128 * i + 128], PB[2 + i][:, :].rearrange("p (s t) -> p s t", s=4),
                                ACT.Copy, w=[e])
            soft[h] = e
            steps(g2, 2)
            b = 4 + h % 2
            ro = 64 * (h % 2)
            for s_ in range(4):
                e = mm(PB[b][ro:ro + 64, 0:256], qkv[:, s_, 640 + 64 * (h // 4):704 + 64 * (h // 4)], pT[h % 2][:, s_, :],
                       s_ == 0, s_ == 3, w=[bank[3], bank[b]], inc=s_ == 3)
            ta = A(HH[ro:ro + 64, h // 2, 0:256], PB[b][ro:ro + 64, 0:256], ACT.Copy, w=[e, t_proj])
            bank[b] = V(tt, HL[ro:ro + 64, h // 2, 0:256], PB[b][ro:ro + 64, 0:256], HH[ro:ro + 64, h // 2, 0:256].bitcast(F32),
                        ALU.subtract, w=[ta])

        ws = load(I["w_sT"], 1024, "p (g i) -> p g i", g=8)

        def gating():
            t = None
            for i in range(2):
                t = A(s12, gm[:, i, 512:1024], ACT.Square, accum_out=st[:, 40 + i:41 + i], w=[last("v")])
            t = rstd_of(40, 2, 512, t)
            for i in range(2):
                vv = gm[:, i, 512:1024]
                t = V(stt, vv, vv, st[:, 40 + i:41 + i], gains.ap[:, 640:1152], ALU.mult, ALU.mult)
                for g in range(8):
                    e = mm(PB[6][:, 64 * g:64 * g + 64], ws.ap[:, g, :], vv[:, 64 * g:64 * g + 64], w=[t, ws.tok, bank[6]], inc=g == 7)
                yield
                V(tt, vv.rearrange("p (g d) -> p g d", g=8), PB[6][:, :].rearrange("p (g d) -> p g d", g=8),
                  col("b_s", 0, 8)[:, :, None].to_broadcast([128, 8, 64]), ALU.add, w=[e])
                t = V(tt, vv, vv, gm[:, i, 0:512], ALU.mult)
                yield
                for c in range(4):
                    e = tp(PB[6][:, 128 * c:128 * c + 128], vv[:, 128 * c:128 * c + 128], w=[t, bank[6]], inc=c == 3)
                bank[6] = halves_of(PB[6][:, :].rearrange("p (c t) -> p c t", c=4), HH[:, 4:8, 128 * i:128 * i + 128],
                                    HL[:, 4:8, 128 * i:128 * i + 128], [e, t_proj])
                yield

        s12 = big[:, 13200 - 512:13200]
        gg = gating()
        t = scores(0)
        for h in range(8):
            t2 = scores(h + 1) if h < 7 else None
            values(h, t)
            t = t2
            steps(gg, 1)
        run(gg)
        run(g2)
        ws.free = [last("t")]
        gains.free = [last("v")]
        t_mix = [last("v"), last("a")]
        sc = scratch()
        gt = sc.ap[:, 0:1024]
        t_g = row_of(gt, mcol1[:, 16:24, 0], s1, [])
        for q in range(4):
            w_ = S.get(8 + q)
            for a in range(2):
                kk = 2 * q + a
                for i in range(2):
                    for j in range(2):
                        b = 2 * i + j + 4
                        e = mm3(PB[b][:, :], XT(kk, 128 * i), (w_.H[:, a, 512 * j:512 * j + 512], w_.L[:, a, 512 * j:512 * j + 512]),
                                kk == 0, kk == 7, w=[*w_.toks[a], *t_mix, bank[b]], inc=i + j == 2)
            S.done(8 + q, e)
        tmp = pr[0][0]
        for i in range(2):
            for j in range(2):
                b = 2 * i + j + 4
                V(tt, tmp, PB[b][:, :], gt[:, 512 * j:512 * j + 512], ALU.mult, w=[e, t_g])
                bank[b] = V(tt, X[:, i, 512 * j:512 * j + 512], X[:, i, 512 * j:512 * j + 512], tmp, ALU.add)
        sc.free = [last("v")]
        dump("x1", X[:, 0:2, :], [last("v")])
        barrier_all()

        gT = big[:, 0:4096].rearrange("p (e t) -> p e t", e=16)
        take = arena()
        xn = take(2, D)
        rT = take(256, parts=16)
        rW = take(256, parts=16)
        rM = take(256, parts=16)
        m8 = take(8, parts=16)
        take = arena(4096)
        pos = take(2, 512)
        act = take(3072)
        xeT = take(8, 512)
        aff = take(2, 16)
        slotT = take(2, 16)
        hTf = act[:, 0:2048].rearrange("p (a b) -> p a b", a=8)
        t = rstd([(X[:, i, :], 128) for i in range(2)], 0, D, junk=act[:, 0:D])
        t_h = modulated_T([(X[:, i, :], 128, i, 128 * i) for i in range(2)],
                          [(0, 256, lambda q: AB[:, 16 + q:17 + q], lambda q: mcol1[:, 24 + q, 0:1])],
                          lambda i: xn[:, i, :], [t], f32=hTf, both=False)
        s = load(I["w_router"][0].rearrange("(a p) n -> p a n", p=128), 128, "p (a n) -> p a n", a=8)
        for i in range(2):
            for kk in range(8):
                e = mm(PB[4][:, 16 * i:16 * i + 16], hTf[:, kk, 128 * i:128 * i + 128], s.ap[:, kk, :],
                       kk == 0, kk == 7, w=[t_h, s.tok, bank[4]], inc=kk == 7)
        s.free = [e]
        lg = PB[4][:, 0:32].rearrange("p (i e) -> p i e", i=2)
        mx = st[:, 8:10]
        V(ve.tensor_reduce, mx, lg, AX, ALU.max, w=[e])
        t = V(tt, aff, lg, mx[:, :, None].to_broadcast([128, 2, 16]), ALU.subtract)
        bank[4] = t
        t = A(aff, aff, ACT.Exp, w=[t])
        V(ve.tensor_reduce, mx, aff, AX, ALU.add, w=[t])
        V(ve.reciprocal, mx, mx)
        t_aff = V(tt, aff, aff, mx[:, :, None].to_broadcast([128, 2, 16]), ALU.mult)
        dump("aff", aff, [t_aff])
        for i in range(2):
            e = tp(PB[4][0:16, 128 * i:128 * i + 128], aff[:, i, :], w=[t_aff, bank[4]], inc=True)
        bank[4] = V(cp, rT, PB[4][0:16, 0:256], w=[e])
        cur = rT
        for r in range(4):
            V(ve.max, m8, cur)
            V(ve.match_replace, rW, m8, cur, -1.0)
            cur = rW
        V(ts, rM, rW, 0.0, None, ALU.is_lt)
        V(ve.memset, rT, 0.0)
        V(ve.tensor_tensor_scan, rW, rM, rT, 0.0, ALU.add, ALU.add)
        t = V(tt, rW, rW, rM, ALU.mult)
        for i in range(2):
            e = tp(PB[4][:, 16 * i:16 * i + 16], rW[:, 128 * i:128 * i + 128], w=[t, bank[4]], inc=True)
        bank[4] = V(cp, slotT, PB[4][:, 0:32].rearrange("p (i e) -> p i e", i=2), w=[e])
        for i in range(2):
            t_pos = V(tt, pos[:, i, :].rearrange("p (e s) -> p e s", e=16), slotT[:, i, :, None].to_broadcast([128, 16, 32]),
                      k("slot")[:, None, :].to_broadcast([128, 16, 32]), ALU.is_equal)
        wait("t", [t_pos])
        for kk in range(8):
            b = kk % 2
            for i in range(2):
                e = mm(PB[b][:, :], xn[:, i, kk * 128:kk * 128 + 128], pos[:, i, :], i == 0, i == 1, w=[bank[b]], inc=i == 1)
            bank[b] = V(ts, xeT[:, kk, :], PB[b][:, :], AB[:, 16 + kk:17 + kk], mcol1[:, 24 + kk, 0:1], ALU.mult, ALU.add, w=[e])
        t_xe = bank[1]
        wait("a", [e])
        gg = act[:, 0:2048].rearrange("p (e c s) -> p e c s", e=16, c=4)

        def scatter_weights(i):
            V(tt, pos[:, i, :].rearrange("p (e s) -> p e s", e=16), pos[:, i, :].rearrange("p (e s) -> p e s", e=16),
              aff[:, i, :, None].to_broadcast([128, 16, 32]), ALU.mult)
            for c in range(4):
                t = V(cp, gg[:, :, c, :], pos[:, i, :].rearrange("p (e s) -> p e s", e=16), w=[last("t")])
            for q in range(4):
                b = 2 + q % 2
                for r in range(4):
                    e = tp(PB[b][:, 128 * r:128 * r + 128], gg[:, 4 * q + r].rearrange("p c s -> p (c s)"),
                           w=[t, bank[b]], inc=r == 3)
                bank[b] = A(gT[:, 4 * q:4 * q + 4, 128 * i:128 * i + 128], PB[b][:, :].rearrange("p (r t) -> p r t", r=4), ACT.Copy, w=[e])

        scatter_weights(0)
        scatter_weights(1)
        wait("t", [last("v"), last("a")])
        wait("v", [last("t"), last("a")])
        wait("a", [last("t"), last("v")])
        sil = [pos[:, 0, :], pos[:, 1, :]]
        hidT = [act[:, 512 * z:512 * z + 512].rearrange("p (c m) -> p c m", c=4) for z in range(2)]
        ye = [act[:, 1024 + 1024 * z:2048 + 1024 * z] for z in range(2)]
        sil_free = [None, None]
        ye_free = [None, None]
        w1, w3, w2 = I["w1"][0], I["w3"][0], I["w2"][0]

        def scatter(x, t):
            for i in range(2):
                for j in range(2):
                    e = mm(PB[4 + 2 * i + j][:, :], gT[:, x, 128 * i:128 * i + 128], ye[x % 2][:, 512 * j:512 * j + 512],
                           x == 0, x == 15, w=[t, bank[4 + 2 * i + j]], inc=True)
            ye_free[x % 2] = e
            return e

        t_ye = None
        for x in range(16):
            z = x % 2
            for half, w_ in ((0, w1), (1, w3)):
                for kk in range(8):
                    s = load(w_[x, kk * 128:kk * 128 + 128, :], 2048)
                    for j in range(4):
                        e = mm(PB[half][32 * j:32 * j + 32, :], xeT[:, kk, 32 * x:32 * x + 32], s.ap[:, 512 * j:512 * j + 512],
                               kk == 0, kk == 7, w=[s.tok, bank[half]], inc=j == 3)
                    s.free = [e]
                if half == 0:
                    t_s = A(sil[z], PB[0][:, :], ACT.Silu, w=[e, sil_free[z]])
                    bank[0] = t_s
                    if x:
                        scatter(x - 1, t_ye)
            t = V(tt, sil[z], sil[z], PB[1][:, :], ALU.mult, w=[e, t_s])
            bank[1] = t
            for c in range(4):
                e = tp(PB[2][:, 128 * c:128 * c + 128], sil[z][:, 128 * c:128 * c + 128], w=[t, bank[2]], inc=c == 3)
            sil_free[z] = e
            t = V(cp, hidT[z], PB[2][:, :].rearrange("p (c m) -> p c m", c=4), w=[e])
            bank[2] = t
            for c in range(4):
                sl_ = [load(w2[x].rearrange("(j c p) n -> c p j n", j=4, c=4)[c][:, 2 * hf:2 * hf + 2, :], 2048,
                            "p (j n) -> p j n", j=2) for hf in range(2)]
                for n in range(2):
                    for j in range(4):
                        s = sl_[j // 2]
                        e = mm(PB[2 + n][32 * j:32 * j + 32, :], hidT[z][:, c, 32 * j:32 * j + 32],
                               s.ap[:, j % 2, 512 * n:512 * n + 512], c == 0, c == 3, w=[s.tok, t, bank[2 + n]], inc=j % 2 == 1)
                        if n == 1:
                            s.free = [e]
            A(ye[z][:, 0:512], PB[2][:, :], ACT.Copy, w=[e, ye_free[z]])
            t_ye = A(ye[z][:, 512:1024], PB[3][:, :], ACT.Copy)
            bank[2] = bank[3] = t_ye
            if x == 2 and t_c2:
                ctx_ahead(t_c2)
            if x == 4:
                t_g = row_of(tmp_row, mcol1[:, 40:48, 0], sil[1], [last("t"), last("a")])
                sil_free[1] = last("t")
        e = scatter(15, t_ye)
        gf = load(I["rows"][:, RO["g_final"]:RO["g_final"] + 1024], 1024)
        for i in range(2):
            for j in range(2):
                b = 4 + 2 * i + j
                V(tt, sil[1], PB[b][:, :], tmpT[:, j, :], ALU.mult, w=[e, t_g])
                bank[b] = V(tt, X[:, i, 512 * j:512 * j + 512], X[:, i, 512 * j:512 * j + 512], sil[1], ALU.add)
        dump("x2", X[:, 0:2, :], [last("v")])
        t = rstd([(X[:, i, :], 128) for i in range(2)], 0, D, junk=ye[0], w=[last("v"), e])
        for i in range(2):
            t = V(stt, X[:, i, :], X[:, i, :], st[:, i:i + 1], gf.ap, ALU.mult, ALU.mult, w=[gf.tok])
        gf.free = [t]
        dump("xf", X[:, 0:2, :], [t])
        barrier_all()

    tmp_row = tmpT[:, :, :].rearrange("p a b -> p (a b)")

    def halves_of(x, h, l, w):
        ta = A(h, x, ACT.Copy, w=w)
        return V(tt, l, x, h.bitcast(F32), ALU.subtract, w=[ta, *w])

    def ng(i):
        return col("norm_g_2", 8 * i, 8)

    def ada_scales():
        for i, (g, ch, which) in enumerate(((0, 1, 0), (0, 1, 1), (2, 4, 0), (2, 4, 1), (4, 7, 0))):
            V(stt, AB2[:, 8 * i:8 * i + 8], mcol2[:, 8 * ch:8 * ch + 8, which], 1.0, ng(g), ALU.add, ALU.mult)
        V(stt, AB2[:, 40:48], mcol2[:, 16:24, 0], 0.5, ng(1), ALU.mult, ALU.mult)
        V(stt, AB2[:, 48:56], mcol2[:, 16:24, 1], 0.5, ng(1), ALU.mult, ALU.mult)
        V(tt, AB2[:, 56:64], mcol2[:, 40:48, 0], ng(3), ALU.mult)
        return V(stt, AB2[:, 64:72], mcol2[:, 64:72, 0], 0.5, ng(5), ALU.mult, ALU.mult)

    def ctx_ahead(t_c2):
        ada_scales()
        sc = scratch()
        t = rstd([(X[:, 2 + i, :], 128) for i in range(2)], 2, D, w=[t_c2], junk=sc.ap[:, 0:D])
        modulated_T([(X[:, 2 + i, :], 128, 2 + i, 256 + 128 * i) for i in range(2)],
                    [(256, 512, lambda q: AB2[:, 8 + q:9 + q], lambda q: mcol2[:, q, 1:2])],
                    lambda i: sc.ap[:, D * i:D * i + D], [t])
        sc.free = [last("t"), last("v"), last("a")]

    AB2 = sb("AB2", [128, 72])

    def post(nt, G_, banks, tmp, e, t_g):
        for i in range(nt):
            for j in range(2):
                t = A(tmp[j], PB[banks[2 * i + j]][:, :], ACT.Square, accum_out=st[:, 8 + 2 * i + j:9 + 2 * i + j], w=[e])
        sv = st[:, 8:8 + 2 * nt].rearrange("p (i j) -> p i j", j=2)
        t = V(tt, st[:, 0:nt], sv[:, :, 0], sv[:, :, 1], ALU.add, w=[t])
        rstd_of(0, nt, D, t)
        for i in range(nt):
            for j in range(2):
                b = banks[2 * i + j]
                V(stt, tmp[0], PB[b][:, :], st[:, i:i + 1], G_[i // 2][:, 512 * j:512 * j + 512], ALU.mult, ALU.mult, w=[t_g])
                bank[b] = V(tt, X[:, i, 512 * j:512 * j + 512], X[:, i, 512 * j:512 * j + 512], tmp[0], ALU.add)

    def half_ffn(nt, done_ctx, pre, sh, gates, w13, w2):
        take = arena()
        T = 128 * nt
        hid = take(22, T)
        xn = hid.rearrange("p a b -> p (a b)")
        tmp = [take(512), take(512)]
        sl = [take(T), tmp[1]]
        sc = scratch()
        Gr = [sc.ap[:, D * z:D * z + D] for z in range(len(gates))]
        t_g = None
        nn = 2 if done_ctx else nt
        t = rstd([(X[:, i, :], 128) for i in range(nn)], 0, D, junk=xn[:, 0:D])
        reg = []
        for z, p in enumerate(pre[:nn // 2]):
            reg.append((256 * z, 256 * z + 256, (lambda q, p=p: AB2[:, 8 * p + q:8 * p + q + 1]),
                        (lambda q, z=z: mcol2[:, sh * 8 + q, z:z + 1])))
        S = Stream([x for p in range(11) for x in (cols256(w13, 256 * p), cols256(w13, 2816 + 256 * p))] + rows2(w2))
        t_h = modulated_T([(X[:, i, :], 128, i, 128 * i) for i in range(nn)], reg, lambda i: xn[:, D * i:D * i + D], [t])
        S.ahead()
        wait("v", [last("t")])
        wait("t", [last("v"), last("a")])
        sfree = [last("v")] * 2
        for p in range(11):
            bs = 4 * (p % 2)
            for q in range(2):
                w_ = S.get(2 * p + q)
                for f in range(2):
                    b = bs + 2 * q + f
                    for kk in range(8):
                        e = mm3(PB[b][:, 0:T], (w_.H[:, kk, 128 * f:128 * f + 128], w_.L[:, kk, 128 * f:128 * f + 128]),
                                XT(kk, 0, T), kk == 0, kk == 7, w=[*w_.toks[kk // 4], bank[b]], inc=kk == 7)
                    if q == 0:
                        bank[b] = A(sl[f][:, 0:T], PB[b][:, 0:T], ACT.Silu, w=[e, sfree[f]])
                    else:
                        sfree[f] = bank[b] = V(tt, hid[:, 2 * p + f, :], sl[f][:, 0:T], PB[b][:, 0:T], ALU.mult,
                                               w=[e, bank[bs + f]])
                S.done(2 * p + q, e)
            if p == 0:
                for z, c8 in enumerate(gates):
                    t_g = row_of(Gr[z], c8, tmp[0] if T == 256 else RBf, [], bank_=7)
        nx = halves(hid[:, 0, :], T, [sfree[0], sfree[1]])
        for n in range(22):
            w_ = S.get(22 + n // 2)
            cur = nx
            if n < 21:
                nx = halves(hid[:, n + 1, :], T, [sfree[0], sfree[1]])
            b_, (h_, l_), tk = cur
            a = n % 2
            for i in range(nt):
                for j in range(2):
                    b = 2 * i + j
                    e = mm3(PB[b][:, :], (h_[:, 128 * i:128 * i + 128], l_[:, 128 * i:128 * i + 128]),
                            (w_.H[:, a, 512 * j:512 * j + 512], w_.L[:, a, 512 * j:512 * j + 512]), n == 0, n == 21,
                            w=[*w_.toks[a], *tk, bank[b]], inc=i == nt - 1 and j == 1)
            rb_free[b_] = e
            if a == 1:
                S.done(22 + n // 2, e)
        post(nt, Gr, list(range(8)), tmp, e, t_g)
        sc.free = [last("v")]
        barrier_all()

    RBf = sb("RBf", [128, 256])

    def second():
        if only and "first" not in only:
            for i, (l, c) in enumerate((("c", "c_ctx"), ("c_2", "c_ctx_2"))):
                A(cs[:, i, :, 0], col(l, 0, 8), ACT.Silu)
                A(cs[:, i, :, 1], col(c, 0, 8), ACT.Silu)
            wait("t", [last("a")])
            run(gemv(I["w_ada_2"][0], 1, "b_ada_2", 18, mcol2, 7))
            wait("s", [t_c])
            t_c2 = load_once(X[:, 2:4, :], I["ctx_2"].rearrange("a (t p) d -> p (a t) d", p=128))
            wait("v", [t_c2, t_x])
            wait("a", [t_c2, t_x])
            ctx_ahead(t_c2)
            barrier_all()
        half_ffn(4, True, (0, 1), 0, (AB2[:, 40:48], AB2[:, 48:56]), I["w13_a_2"][0], I["w2_a_2"][0])
        dump("ffa", X[:], [last("v")])
        mixer()
        dump("mix2", X[:, 0:2, :], [last("v")])
        half_ffn(2, False, (4,), 6, (AB2[:, 64:72],), I["w13_b_2"][0], I["w2_b_2"][0])
        dump("ffb", X[:, 0:2, :], [last("v")])

    CF, CQ, CK, CV, CO_, CG, CB = 0, 512, 1536, 2560, 3584, 4608, 4624

    def mixer():
        w_in = I["w_in_2"][0]
        xn = big[:, 0:4096].rearrange("p (a b) -> p a b", a=4)
        specs = [cols256(w_in, CG, 8, 128)]
        specs += [(w_in[512 * q:512 * q + 512, CF:CF + 512].rearrange("(a p) n -> p a n", p=128), 2048, "p (a n) -> p a n",
                   dict(a=4)) for q in range(2)]
        at = {}
        for h in range(5):
            for c0 in ((CQ, CK, CV) if h < 4 else ()):
                at[(c0, h)] = len(specs)
                specs.append(cols256(w_in, c0 + 256 * h))
            if h:
                at[(CO_, h - 1)] = len(specs)
                specs.append(cols256(w_in, CO_ + 256 * (h - 1)))
        m0 = len(specs)
        for p in range(4):
            specs += [cols256(w_in, CB + 256 * p), cols256(w_in, CB + D + 256 * p), cols256(I["w_four_2"][0], 256 * p, 4),
                      cols256(I["w_mproj_2"][0], 256 * p)]
        o0 = len(specs)
        specs += rows2(I["w_out_2"][0])
        S = Stream(specs)
        t = rstd([(X[:, i, :], 128) for i in range(4)], 0, D, junk=xn[:, 0, :])
        modulated_T([(X[:, i, :], 128, i, 128 * i) for i in range(4)],
                    [(0, 256, lambda q: AB2[:, 16 + q:17 + q], lambda q: mcol2[:, 24 + q, 0:1]),
                     (256, 512, lambda q: AB2[:, 24 + q:25 + q], lambda q: mcol2[:, 24 + q, 1:2])],
                    lambda i: xn[:, i, :], [t])
        S.ahead()
        barrier_all()
        take = arena()
        yfT = take(4, 256)
        hmT = take(8, 256)
        gr = 512
        MM = take(gr, parts=36)
        dec = take(8, 4)
        gc = take(4, 4, 8)
        kept = 3072 + 512 + 32 + 128
        qT = [take(2, 256) for _ in range(2)]
        kT = [take(2, 512) for _ in range(2)]
        va = [take(4, 257) for _ in range(2)]
        so = take(2, 256)
        hs = take(2, 256)
        C = [take(2, 257) for _ in range(2)]
        inter = [take(257) for _ in range(2)]
        pads = [take(2, 258) for _ in range(2)]
        tf = tmp_row
        kw = [tf[:, 0:256], tf[:, 256:512]]
        wT = [tf[:, 512:640], tf[:, 640:768]]
        sT = [tf[:, 768:896], tf[:, 896:1024]]
        bo = load(I["rows"][:, RO["b_v"]:RO["b_v"] + 2048], 2048)
        hg = load(I["rows"][:, RO["head_g"]:RO["head_g"] + 1536], 1536)
        for z in range(2):
            V(ve.memset, pads[z], 0.0)
            t_va = V(ve.memset, va[z], 1.0)
        order = [[2, 3, 0, 1], [3, 2, 1, 0]]
        seg = [slice(0, 4), slice(32, 36)]

        w_ = S.get(0)
        for kk in range(8):
            e = mm3(PB[0][:, :], (w_.H[:, kk, :], w_.L[:, kk, :]), XT(kk, 0, 512), kk == 0, kk == 7,
                    w=[*w_.toks[kk // 4], bank[0]], inc=kk == 7)
        S.done(0, e)
        sc1, sc2, sc3 = scratch(), scratch(), scratch()

        def row36(s, i):
            return s.ap[0:36, 512 * i:512 * i + 512]

        li, lf, bb, rr = (row36(sc1, i) for i in range(4))
        q_a, q_f, q_w, zz = (row36(sc2, i) for i in range(4))
        g16 = pads[0].rearrange("p a b -> p (a b)")[0:16, 0:512]
        small = BO[0:36, 0:32]
        t_pad = [None]

        def gates():
            t = V(cp, g16, PB[0][0:16, :], w=[e])
            bank[0] = t
            mm(PB[2][0:36, :], k("sel_i")[0:16, :], g16, w=[t, bank[2]])
            e1 = mm(PB[3][0:36, :], k("sel_f")[0:16, :], g16, w=[t, bank[3]], inc=True)
            yield
            V(ts, li, PB[2][0:36, :], col("b_gate", 0)[0:36, :], None, ALU.add, w=[e1])
            bank[2] = bank[3] = V(ts, lf, PB[3][0:36, :], col("b_gate", 1)[0:36, :], None, ALU.add)
            t_pad[0] = V(ve.memset, pads[0], 0.0)
            V(ts, bb, lf, 0.0, None, ALU.min)
            t = V(stt, rr, bb, 2.0, lf, ALU.mult, ALU.subtract)
            V(ve.memset, zz, 0.0)
            t = A(rr, rr, ACT.Exp, w=[t])
            yield
            yield from log1p(rr, MM, q_a, q_f, [t])
            V(tt, lf, bb, q_f, ALU.subtract)

            def view(ap, d, blk):
                a = ap[seg[d], 128 * blk:128 * blk + 128]
                return a if d == 0 else a[:, ::-1]

            def endof(ap, d, blk):
                i = 128 * blk + (127 if d == 0 else 0)
                return ap[seg[d], i:i + 1]

            V(ve.memset, small, 0.0)
            for d in range(2):
                yield
                for blk in range(4):
                    V(ve.tensor_tensor_scan, view(bb, d, blk), view(lf, d, blk), view(zz, d, blk), 0.0, ALU.add, ALU.add)
            V(tt, rr, li, bb, ALU.subtract)
            for d in range(2):
                for n in range(4):
                    blk = order[d][n]
                    tc_ = slice(128 * blk, 128 * blk + 128)
                    m_0 = small[seg[d], n:n + 1]
                    V(ve.tensor_tensor_scan, view(MM, d, blk), view(rr, d, blk), view(rr, d, blk), m_0, ALU.max, ALU.max)
                    V(tt, small[seg[d], n + 1:n + 2], endof(bb, d, blk), endof(MM, d, blk), ALU.add)
                    V(tt, small[seg[d], 8 + n:9 + n], m_0, endof(MM, d, blk), ALU.subtract)
                    V(ts, q_w[seg[d], tc_], rr[seg[d], tc_], endof(MM, d, blk), None, ALU.subtract)
                    if n >= 2:
                        V(ts, q_a[seg[d], tc_], MM[seg[d], tc_], -1.0, m_0, ALU.mult, ALU.add)
                        V(stt, q_f[seg[d], tc_], bb[seg[d], tc_], -1.0, MM[seg[d], tc_], ALU.mult, ALU.subtract)
                    yield
            t = last("v")
            for d in range(2):
                s_ = seg[d]
                A(q_w[s_, :], q_w[s_, :], ACT.Exp, w=[t])
                A(q_a[s_, 0:256], q_a[s_, 0:256], ACT.Exp)
                A(q_f[s_, 0:256], q_f[s_, 0:256], ACT.Exp)
                t2 = A(small[s_, 8:12], small[s_, 8:12], ACT.Exp)
            yield
            dd = li[:, 0:32]
            t = V(tt, dd.rearrange("p (i n) -> p i n", i=8), small[:, None, 8:12].to_broadcast([36, 8, 4]),
                  k("m8")[0:36, :, None].to_broadcast([36, 8, 4]), ALU.mult, w=[t2])
            e1 = mm(PB[2][:, 0:32], ones[0:36, :], dd, w=[t, bank[2]], inc=True)
            for d in range(2):
                for qi, ap in enumerate((rr, q_w, q_a, q_f)):
                    for blk in range(4 if qi == 1 else 2):
                        e2 = mm(PB[3 + d][:, (qi * 4 + blk) * 4:(qi * 4 + blk) * 4 + 4], ap[seg[d], 128 * blk:128 * blk + 128],
                                ident[seg[d], seg[d]], w=[t, bank[3 + d]], inc=True)
            yield
            bank[2] = V(cp, dec.rearrange("p i n -> p (i n)"), PB[2][:, 0:32], w=[e1])
            for qi in range(4):
                nb = 4 if qi == 1 else 2
                for d in range(2):
                    t = V(cp, gc[:, qi, 0:nb, 4 * d:4 * d + 4],
                          PB[3 + d][:, qi * 16:qi * 16 + 4 * nb].rearrange("p (b i) -> p b i", i=4), w=[e2])
            bank[3] = bank[4] = t
            sc1.free = sc2.free = [t, e2, t2]

        def fourier():
            zf = sc3.ap[:, 0:1024].rearrange("p (a b) -> p a b", a=2)
            m12 = sc3.ap[:, 1024:2048].rearrange("p (a b) -> p a b", a=2)
            for q in range(2):
                w_ = S.get(1 + q)
                for a in range(4):
                    for i in range(2):
                        e = mm3(PB[6 + i][:, :], XT(4 * q + a, 128 * i), (w_.H[:, a, :], w_.L[:, a, :]),
                                q + a == 0, 4 * q + a == 7, w=[*w_.toks[a // 2], bank[6 + i]], inc=True)
                S.done(1 + q, e)
                yield
            fr = load(I["four"], 1280)
            f1 = fr.ap[:, 0:1024].rearrange("p (i n) -> p i n", i=2)
            cc, ns = fr.ap[:, 1024:1152], fr.ap[:, 1152:1280]
            for i in range(2):
                t = V(tt, zf[:, i, :], PB[6 + i][:, :], hg.ap[:, 1024:1536], ALU.add, w=[e, hg.tok])
                bank[6 + i] = t
            for g in range(4):
                b = 6 + g % 2
                for i in range(2):
                    e = mm(PB[b][:, :], zf[:, i, 128 * g:128 * g + 128], f1[:, i, :], i == 0, i == 1, w=[t, fr.tok, bank[b]], inc=i == 1)
                ta = A(m12[:, g % 2, :], PB[b][:, :], ACT.Copy, w=[e, last("t")])
                yield
                mm(PB[b][:, 0:256], cc, m12[:, g % 2, 0:256], True, False, w=[ta])
                e = mm(PB[b][:, 0:256], ns, m12[:, g % 2, 256:512], False, True, inc=True)
                bank[b] = V(cp, yfT[:, g, :], PB[b][:, 0:256], w=[e])
                yield
            fr.free = [e]
            sc3.free = [e, last("v"), last("a")]

        tri = k("tri").rearrange("p (d t) -> p d t", d=2)
        ready = {}
        npad = [0]

        def conv(dst, src, e, ci, T):
            cw = lambda j: col("conv_w_2", 16 * j + ci)
            bname, bi = ("b_q", ci) if ci < 8 else ("b_k", ci - 8)
            P_ = pads[1][:, 0:T // 256, :] if npad[0] % 2 == 0 else pads[0][:, 0:T // 256, :]
            npad[0] += 1
            V(ts, P_[:, :, 1:257], src[:, 0:T].rearrange("p (z t) -> p z t", t=256), col(bname, bi), None, ALU.add, w=[e])
            t = last("v")
            O = dst.rearrange("p (z t) -> p z t", t=256)
            V(ts, O, P_[:, :, 0:256], cw(0), col("conv_b_2", ci), ALU.mult, ALU.add, w=[last("t")])
            V(stt, O, P_[:, :, 1:257], cw(1), O, ALU.mult, ALU.add)
            V(stt, O, P_[:, :, 2:258], cw(2), O, ALU.mult, ALU.add)
            return t

        def proj(h):
            z = h % 2
            if h < 4:
                for c0, dst, T, cb in ((CQ, qT[z], 256, 0), (CK, kT[z], 512, 8)):
                    w_ = S.get(at[(c0, h)])
                    for f in range(2):
                        for kk in range(8):
                            e = mm3(PB[f][:, 0:T], (w_.H[:, kk, 128 * f:128 * f + 128], w_.L[:, kk, 128 * f:128 * f + 128]),
                                    XT(kk, 0, T), kk == 0, kk == 7, w=[*w_.toks[kk // 4], bank[f]], inc=kk == 7)
                            if kk % 4 == 3 and kk < 7:
                                yield
                        bank[f] = conv(dst[:, f, :], PB[f], e, cb + 2 * h + f, T)
                        yield
                    S.done(at[(c0, h)], e)
                w_ = S.get(at[(CV, h)])
                for i in range(4):
                    b = i % 2
                    for kk in range(8):
                        e = mm3(PB[b][:, 0:256], XT(kk, 128 * i), (w_.H[:, kk, :], w_.L[:, kk, :]), kk == 0, kk == 7,
                                w=[*w_.toks[kk // 4], bank[b]], inc=kk == 7)
                    bank[b] = V(tt, va[z][:, i, 0:256], PB[b][:, 0:256], bo.ap[:, 256 * h:256 * h + 256], ALU.add, w=[e, bo.tok])
                    yield
                S.done(at[(CV, h)], e)
            if h:
                w_ = S.get(at[(CO_, h - 1)])
                for i in range(2):
                    for kk in range(8):
                        e = mm3(PB[i][:, 0:256], XT(kk, 128 * i), (w_.H[:, kk, :], w_.L[:, kk, :]), kk == 0, kk == 7,
                                w=[*w_.toks[kk // 4], bank[i]], inc=kk == 7)
                    bank[i] = V(tt, so[:, i, :], PB[i][:, 0:256], bo.ap[:, 768 + 256 * h:1024 + 256 * h], ALU.add, w=[e])
                    yield
                S.done(at[(CO_, h - 1)], e)
            if h < 4:
                t = last("v")
                A(qT[z].rearrange("p a b -> p (a b)"), qT[z].rearrange("p a b -> p (a b)"), ACT.Silu, w=[t])
                ready[h] = [A(kT[z].rearrange("p a b -> p (a b)"), kT[z].rearrange("p a b -> p (a b)"), ACT.Silu), t]

        def finish(h):
            for i in range(2):
                t = A(inter[i][:, 0:256], hs[:, i, :], ACT.Square, accum_out=st[:, 52 + i:53 + i], w=[last("v")])
            rstd_of(52, 2, 256, t)
            A(so[:, 0, :], so[:, 0, :], ACT.Sigmoid, w=[last("v")])
            t_so = A(so[:, 1, :], so[:, 1, :], ACT.Sigmoid)
            for i in range(2):
                V(stt, hs[:, i, :], hs[:, i, :], st[:, 52 + i:53 + i], hg.ap[:, 256 * h:256 * h + 256], ALU.mult, ALU.mult, w=[hg.tok])
                t = V(tt, hs[:, i, :], hs[:, i, :], so[:, i, :], ALU.mult, w=[t_so])
                yield
                for f in range(2):
                    e = tp(PB[6 + i][:, 128 * f:128 * f + 128], hs[:, i, 128 * f:128 * f + 128], w=[t, bank[6 + i]], inc=f == 1)
                bank[6 + i] = V(cp, hmT[:, 2 * h:2 * h + 2, 128 * i:128 * i + 128],
                                PB[6 + i][:, 0:256].rearrange("p (f t) -> p f t", f=2), w=[e])

        def mlstm(h):
            z = h % 2
            if h:
                yield from finish(h - 1)
            tq = ready[h]
            q_, k_, v_ = qT[z], kT[z], va[z]
            for n in range(4):
                bl = [order[d][n] for d in range(2)]
                tc_ = [slice(128 * b, 128 * b + 128) for b in bl]
                S_, M_ = (2, 4), (3, 5)
                es = [None] * 2
                if n >= 2:
                    for d in range(2):
                        mm(PB[S_[d]][:, 0:128], k_[:, 0, tc_[d]], q_[:, 0, tc_[d]], True, False, w=[*tq, bank[S_[d]]])
                        mm(PB[S_[d]][:, 0:128], k_[:, 1, tc_[d]], q_[:, 1, tc_[d]], False, True)
                        es[d] = mm(PB[M_[d]][:, 0:128], k("m8")[0:36, 4 * d + h:4 * d + h + 1].to_broadcast([36, 128]), MM[:, tc_[d]],
                                   w=[bank[M_[d]]], inc=True)
                    yield
                    for d in range(2):
                        x = 4 * d + h
                        t = bank[M_[d]] = V(tt, wT[d], tri[:, d, :], PB[M_[d]][:, 0:128], ALU.subtract, w=[es[d]])
                        t = A(wT[d], wT[d], ACT.Exp, bias=gc[:, 0, bl[d], x:x + 1], w=[t])
                        es[d] = bank[S_[d]] = V(stt, sT[d], PB[S_[d]][:, 0:128], 0.0625, wT[d], ALU.mult, ALU.mult, w=[t, last("t")])
                if n < 3:
                    ks = [None] * 2
                    for d in range(2):
                        for f in range(2):
                            e = tp(PB[6 + d][:, 128 * f:128 * f + 128], k_[:, f, tc_[d]], w=[*tq, bank[6 + d]], inc=f == 1)
                        ks[d] = bank[6 + d] = V(ts, kw[d], PB[6 + d][:, 0:256], gc[:, 1, bl[d], 4 * d + h:4 * d + h + 1], 0.0625,
                                                ALU.mult, ALU.mult, w=[e])
                yield
                if n >= 2:
                    for d in range(2):
                        mm(PB[S_[d]][:, 0:257], sT[d], v_[:, bl[d], :], w=[es[d], bank[S_[d]]])
                        mm(PB[M_[d]][:, 0:257], q_[:, 0, tc_[d]], C[d][:, 0, :], True, False, w=[t_C[d], bank[M_[d]]])
                        es[d] = mm(PB[M_[d]][:, 0:257], q_[:, 1, tc_[d]], C[d][:, 1, :], False, True, inc=True)
                if n < 3:
                    for d in range(2):
                        for f in range(2):
                            e = mm(PB[6 + f][:, 0:257], kw[d][:, 128 * f:128 * f + 128], v_[:, bl[d], :], w=[ks[d], bank[6 + f], ready[h][1]], inc=True)
                            if n == 0:
                                t_C[d] = V(cp, C[d][:, f, :], PB[6 + f][:, 0:257], w=[e])
                            else:
                                t_C[d] = V(stt, C[d][:, f, :], C[d][:, f, :], dec[:, 4 * d + h, n:n + 1], PB[6 + f][:, 0:257],
                                           ALU.mult, ALU.add, w=[e])
                            bank[6 + f] = t_C[d]
                        if d == 0:
                            yield
                yield
                if n >= 2:
                    for d in range(2):
                        x, I_ = 4 * d + h, inter[d]
                        bank[M_[d]] = V(ts, I_, PB[M_[d]][:, 0:257], gc[:, 2, bl[d], x:x + 1], None, ALU.mult, w=[es[d]])
                        bank[S_[d]] = V(tt, I_, I_, PB[S_[d]][:, 0:257], ALU.add)
                        dn = st[:, 50 + d:51 + d]
                        V(stt, dn, I_[:, 256:257], -1.0, I_[:, 256:257], ALU.mult, ALU.max)
                        V(ts, dn, dn, gc[:, 3, bl[d], x:x + 1], None, ALU.max)
                        V(ve.reciprocal, dn, dn)
                        if n == 2:
                            V(ts, hs[:, bl[d], :], I_[:, 0:256], dn, None, ALU.mult, w=[last("t")])
                        else:
                            V(stt, hs[:, bl[d], :], I_[:, 0:256], dn, hs[:, bl[d], :], ALU.mult, ALU.add)

        t_C = [None, None]
        both(gates(), fourier())
        run(proj(0))
        dump("yfT", yfT, [last("v")])
        for h in range(4):
            both(mlstm(h), proj(h + 1))
        run(finish(3))
        bo.free = hg.free = [last("v")]
        dump("hmT", hmT, [last("v")])
        barrier_all()
        take = arena(kept)
        yT = take(8, 256)
        tmp = [take(512), take(512)]
        Gr = take(D)
        s1, s2 = [take(256) for _ in range(2)], [take(256) for _ in range(2)]
        for p in range(4):
            for q in range(2):
                w_ = S.get(m0 + 4 * p + q)
                for f in range(2):
                    b = 4 * f + q
                    for kk in range(8):
                        e = mm3(PB[b][:, 0:256], (w_.H[:, kk, 128 * f:128 * f + 128], w_.L[:, kk, 128 * f:128 * f + 128]),
                                XT(kk, 0, 256), kk == 0, kk == 7, w=[*w_.toks[kk // 4], bank[b]], inc=kk == 7)
                    bank[b] = A((s1, s2)[q][f], PB[b][:, 0:256], ACT.Sigmoid, bias=col(("b_gf", "b_gm")[q], 2 * p + f), w=[e, last("v")])
                S.done(m0 + 4 * p + q, e)
            for q, (src, nk) in ((2, (yfT, 4)), (3, (hmT, 8))):
                w_ = S.get(m0 + 4 * p + q)
                nx = halves(src[:, 0, :], 256, [])
                for kk in range(nk):
                    cur = nx
                    if kk < nk - 1:
                        nx = halves(src[:, kk + 1, :], 256, [])
                    for f in range(2):
                        b = 4 * f + q
                        e = mm3(PB[b][:, 0:256], (w_.H[:, kk, 128 * f:128 * f + 128], w_.L[:, kk, 128 * f:128 * f + 128]),
                                cur[1], kk == 0, kk == nk - 1, w=[*w_.toks[kk // (nk // 2)], *cur[2], bank[b]], inc=f == 1)
                    rb_free[cur[0]] = e
                S.done(m0 + 4 * p + q, e)
                for f in range(2):
                    s_ = (s1, s2)[q - 2][f]
                    bank[4 * f + q] = V(tt, s_, s_, PB[4 * f + q][:, 0:256], ALU.mult, w=[e, last("a")])
            for f in range(2):
                t_y = V(tt, yT[:, 2 * p + f, :], s1[f], s2[f], ALU.add)
        tg = row_of(Gr, AB2[:, 56:64], tmp[0], [])
        nx = halves(yT[:, 0, :], 256, [t_y])
        for kk in range(8):
            w_ = S.get(o0 + kk // 2)
            cur, a = nx, kk % 2
            if kk < 7:
                nx = halves(yT[:, kk + 1, :], 256, [t_y])
            for i in range(2):
                for j in range(2):
                    b = 4 + 2 * i + j
                    e = mm3(PB[b][:, :], (cur[1][0][:, 128 * i:128 * i + 128], cur[1][1][:, 128 * i:128 * i + 128]),
                            (w_.H[:, a, 512 * j:512 * j + 512], w_.L[:, a, 512 * j:512 * j + 512]), kk == 0, kk == 7,
                            w=[*w_.toks[a], *cur[2], bank[b]], inc=i + j == 2)
            rb_free[cur[0]] = e
            if a:
                S.done(o0 + kk // 2, e)
        post(2, [Gr], [4, 5, 6, 7], tmp, e, tg)
        barrier_all()

    def log1p(z, w_, w2, o, wt):
        V(ts, w_, z, 2.0, None, ALU.add, w=wt)
        V(ve.reciprocal, w_, w_)
        V(tt, w_, w_, z, ALU.mult)
        yield
        V(tt, w2, w_, w_, ALU.mult)
        V(ts, o, w2, 1.0 / 17, None, ALU.mult)
        for n in (15, 13, 11, 9, 7, 5, 3):
            V(stt, o, o, 1.0 / n, w2, ALU.add, ALU.mult)
            if n % 4 == 3:
                yield
        V(stt, o, o, 1.0, w_, ALU.add, ALU.mult)
        V(ts, o, o, 2.0, None, ALU.mult)

    TL = [(0, 128, 16), (1, 128, 144), (2, 16, 0)]
    T3 = 272

    def third():
        wait("s", [last("v"), last("a"), last("t"), t_c])
        t_m = load_once(X[0:16, 2, :], I["meta_tokens_3"])
        for e in "va":
            wait(e, [t_m, t_x])
        S = Stream(rows2(I["a_w_in_3"][0], 0, 704) + [cols256(I["a_w_in_3"][0], 704 + 256 * p) for p in range(4)]
                   + rows2(I["a_w_out_3"][0])
                   + [x for p in range(4) for x in (cols256(I["b_w_in_3"][0], 256 * p), cols256(I["b_w_in_3"][0], D + 256 * p))]
                   + [(I[n][0].rearrange("g (a p) n -> p g a n", p=128), 2048, "p (g a n) -> p g a n", dict(g=4, a=2))
                      for n in ("b_w_rg_3", "b_w_ig_3")] + rows2(I["b_w_out_3"][0]))

        def norm_T(gname, xnb):
            t = rstd([(X[0:n, i, :], n) for i, n, c in TL], 0, D, junk=xnb)
            return modulated_T([(X[0:n, i, :], n, i, c) for i, n, c in TL],
                               [(0, T3, lambda q: col(gname, q), None)], lambda i: xnb[:, D * i:D * i + D], [t])

        def project(yT, s0, tls):
            w = [last("v"), last("a")]
            nx = halves(yT[:, 0, :], T3, w)
            for kk in range(8):
                w_ = S.get(s0 + kk // 2)
                cur, a = nx, kk % 2
                if kk < 7:
                    nx = halves(yT[:, kk + 1, :], T3, w)
                for i, n, c in tls:
                    for j in range(2):
                        b = 2 * i + j
                        e = mm3(PB[b][:, :], (cur[1][0][:, c:c + 128], cur[1][1][:, c:c + 128]),
                                (w_.H[:, a, 512 * j:512 * j + 512], w_.L[:, a, 512 * j:512 * j + 512]), kk == 0, kk == 7,
                                w=[*w_.toks[a], *cur[2], bank[b]], inc=True)
                rb_free[cur[0]] = e
                if a:
                    S.done(s0 + kk // 2, e)
            for i, n, c in tls:
                for j in range(2):
                    b = 2 * i + j
                    bank[b] = V(tt, X[0:n, i, 512 * j:512 * j + 512], X[0:n, i, 512 * j:512 * j + 512], PB[b][0:n, :], ALU.add, w=[e])
            barrier_all()

        norm_T("a_norm", big[:, 0:3 * D])
        S.ahead()
        barrier_all()
        take = arena()
        pj = take(3, 704)
        qr = take(3, 512)
        kr = take(128)
        qlT = take(3, T3)
        kvT = take(2, T3)
        qrT = take(4, T3)
        krT = take(T3)
        vt = take(3, D)
        yT = take(8, T3)
        scr = take(2, 256)
        kn1 = take(T3)
        wu, wk = I["a_w_uq_3"][0], I["a_w_ukv_3"][0]
        wait("s", barrier())
        t_mask = load_once(tmp_row[:, 0:816], I["mask3"])
        mask = tmp_row[:, 0:816].rearrange("p (i t) -> p i t", i=3)
        for q in range(4):
            w_ = S.get(q)
            for a in range(2):
                kk = 2 * q + a
                for i, n, c in TL:
                    for j, (c0, c1) in enumerate(((0, 384), (384, 704))):
                        e = mm3(PB[2 * i + j][:, 0:c1 - c0], XT(kk, c), (w_.H[:, a, c0:c1], w_.L[:, a, c0:c1]),
                                kk == 0, kk == 7, w=[*w_.toks[a], bank[2 * i + j]], inc=True)
            S.done(q, e)
        for i, n, c in TL:
            bank[2 * i] = V(cp, pj[0:n, i, 0:384], PB[2 * i][0:n, 0:384], w=[e])
            bank[2 * i + 1] = A(pj[0:n, i, 384:704], PB[2 * i + 1][0:n, 0:320], ACT.Copy, w=[e])
        t_pj = [last("v"), last("a")]

        def gate():
            for p in range(4):
                w_ = S.get(4 + p)
                for f in range(2):
                    b = 6 + f
                    for kk in range(8):
                        e = mm3(PB[b][:, 0:T3], (w_.H[:, kk, 128 * f:128 * f + 128], w_.L[:, kk, 128 * f:128 * f + 128]),
                                XT(kk, 0, T3), kk == 0, kk == 7, w=[*w_.toks[kk // 4], bank[b]], inc=kk == 7)
                    bank[b] = A(yT[:, 2 * p + f, :], PB[b][:, 0:T3], ACT.Silu, w=[e])
                    yield
                S.done(4 + p, e)

        r3 = k("rope3").rearrange("p (i c d) -> p i c d", i=3, c=2)

        def latents():
            junk = qr.rearrange("p a b -> p (a b)")
            for i, n, c in TL:
                V(tt, junk[0:n, 0:640], pj[0:n, i, 0:640], pj[0:n, i, 0:640], ALU.mult, w=t_pj)
                V(ve.tensor_reduce, st[0:n, 2 * i:2 * i + 1], junk[0:n, 0:384], AX, ALU.add)
                V(ve.tensor_reduce, st[0:n, 2 * i + 1:2 * i + 2], junk[0:n, 384:640], AX, ALU.add)
            s6 = st[:, 0:6].rearrange("p (i c) -> p i c", c=2)
            V(ts, s6[:, :, 0], s6[:, :, 0], 1.0 / 384, 1e-6, ALU.mult, ALU.add)
            t = V(ts, s6[:, :, 1], s6[:, :, 1], 1.0 / 256, 1e-6, ALU.mult, ALU.add)
            t = A(st[:, 0:6], st[:, 0:6], ACT.Sqrt, w=[t])
            V(ve.reciprocal, st[:, 0:6], st[:, 0:6], w=[t])
            for i, n, c in TL:
                V(ts, pj[0:n, i, 0:384], pj[0:n, i, 0:384], st[0:n, 2 * i:2 * i + 1], None, ALU.mult)
                V(ts, pj[0:n, i, 384:640], pj[0:n, i, 384:640], st[0:n, 2 * i + 1:2 * i + 2], None, ALU.mult)
            yield
            t = last("v")
            for q in range(5):
                b = q % 2
                for i, n, c in TL:
                    e = tp(PB[b][:, c:c + n], pj[0:n, i, 128 * q:128 * q + 128], w=[t, bank[b]], inc=True)
                dst, g = (qlT[:, q, :], col("a_qn", q)) if q < 3 else (kvT[:, q - 3, :], col("a_kvn", q - 3))
                bank[b] = V(ts, dst, PB[b][:, 0:T3], g, None, ALU.mult, w=[e])
                if q % 2:
                    yield
            for i, n, c in TL:
                for z in range(2):
                    t = rope(kr[0:n, 64 * z:64 * z + 32], kr[0:n, 64 * z + 32:64 * z + 64], pj[0:n, i, 640:672],
                             pj[0:n, i, 672:704], r3[0:n, i, 0, :], r3[0:n, i, 1, :], [scr[0:n, 0, 0:32], scr[0:n, 1, 0:32]],
                             [last("t")] if z == 0 else [])
                e = tp(PB[2][:, c:c + n], kr[0:n, :], w=[t, bank[2]], inc=True)
                yield
            bank[2] = V(cp, krT, PB[2][:, 0:T3], w=[e])
            for i, n, c in TL:
                b = 3 + i
                for q in range(3):
                    e = mm(PB[b][0:n, :].rearrange("p (h d) -> p h d", h=8), qlT[:, q, c:c + n],
                           uq[q].ap.rearrange("p (h d) -> p h d", h=8)[:, :, 128:192], q == 0, q == 2,
                           w=[uq[q].tok, last("v"), bank[b]], inc=q == 2)
                yield
                bank[b] = V(cp, qr[0:n, i, :], PB[b][0:n, :], w=[e])
                a = qr[0:n, i, :].rearrange("p (h c d) -> p c h d", c=2, d=32)
                o = pj[0:n, i, 0:512].rearrange("p (h c d) -> p c h d", c=2, d=32)
                t = rope(o[:, 0], o[:, 1], a[:, 0], a[:, 1], r3[0:n, i, 0, None, :].to_broadcast([n, 8, 32]),
                         r3[0:n, i, 1, None, :].to_broadcast([n, 8, 32]),
                         [scr[0:n, 0, :].rearrange("p (h d) -> p h d", h=8), scr[0:n, 1, :].rearrange("p (h d) -> p h d", h=8)], [])
                yield
            for q in range(4):
                b = q % 2
                for i, n, c in TL:
                    e = tp(PB[b][:, c:c + n], pj[0:n, i, 128 * q:128 * q + 128], w=[t, bank[b]], inc=True)
                bank[b] = V(cp, qrT[:, q, :], PB[b][:, 0:T3], w=[e])
                yield

        uq = [load(wu[128 * q:128 * q + 128, :], 1536) for q in range(3)]
        both(latents(), gate())
        uk = [load(wk[128 * q:128 * q + 128, :], 2048) for q in range(2)]
        for i, n, c in TL:
            for j in range(2):
                b = 4 + (2 * i + j) % 4
                for q in range(2):
                    e = mm(PB[b][0:n, :].rearrange("p (h d) -> p h d", h=4), kvT[:, q, c:c + n],
                           uk[q].ap.rearrange("p (h z d) -> p h z d", h=8, z=2)[:, 4 * j:4 * j + 4, 1, :], q == 0, q == 1,
                           w=[uk[q].tok, last("v"), bank[b]], inc=q == 1)
                bank[b] = A(vt[0:n, i, 512 * j:512 * j + 512], PB[b][0:n, :], ACT.Copy, w=[e])
        wait("v", [last("t"), last("a"), t_mask])
        wait("a", [last("t"), last("v")])
        qf, pf = qr.rearrange("p a b -> p (a b)"), pj.rearrange("p a b -> p (a b)")
        prob = [qf[:, 0:816].rearrange("p (i t) -> p i t", i=3), pf[:, 0:816].rearrange("p (i t) -> p i t", i=3)]
        pT = pf[:, 816:1632].rearrange("p (i t) -> p i t", i=3)
        qn = [qf[:, 816:1088], scr.rearrange("p a b -> p (a b)")[:, 0:T3]]
        kn = [qf[:, 1088:1360], kn1]
        SC = float(192) ** -0.5
        t_B = [None] * 8

        def scores(h):
            z = h % 2
            for (dst, src, nk, b) in ((qn[z], qlT, 3, 0), (kn[z], kvT, 2, 1)):
                for q in range(nk):
                    wa = uq[q].ap[:, 192 * h:192 * h + 128] if b == 0 else uk[q].ap[:, 256 * h:256 * h + 128]
                    e = mm(PB[b][:, 0:T3], wa, src[:, q, :], q == 0, q == nk - 1, w=[bank[b]], inc=q == nk - 1)
                bank[b] = A(dst, PB[b][:, 0:T3], ACT.Copy, w=[e])
            r = 64 * (h % 2)
            es = []
            for i, n, c in TL:
                b = 2 + i
                mm(PB[b][0:n, 0:T3], qn[z][:, c:c + n], kn[z], True, False, w=[bank[0], bank[1], bank[b]])
                es.append(mm(PB[b][0:n, 0:T3], qrT[r:r + 64, h // 2, c:c + n], krT[r:r + 64, :], False, True, inc=True))
            for (i, n, c), e in zip(TL, es):
                b, p = 2 + i, prob[z][0:n, i, :]
                bank[b] = V(stt, p, PB[b][0:n, 0:T3], SC, mask[0:n, i, :], ALU.mult, ALU.add, w=[e, t_B[h - 2] if h > 1 else None])
                mx = st[0:n, 40 + i:41 + i]
                V(ve.tensor_reduce, mx, p, AX, ALU.max)
                t = V(ts, mx, mx, -1.0, None, ALU.mult)
                A(p, p, ACT.Exp, bias=mx, accum_out=st[0:n, 44 + i:45 + i], w=[t])
            ta = last("a")
            for i, n, c in TL:
                p = prob[z][0:n, i, :]
                V(ve.reciprocal, st[0:n, 44 + i:45 + i], st[0:n, 44 + i:45 + i], w=[ta])
                t = V(ts, p, p, st[0:n, 44 + i:45 + i], None, ALU.mult)
            return t

        def values(h, t):
            z = h % 2
            tk = []
            for ki, kn_, kc in TL:
                b = 5 + ki
                for i, n, c in TL:
                    if c >= kc:
                        e = tp(PB[b][0:kn_, c:c + n], prob[z][0:n, i, kc:kc + kn_], w=[t, bank[b]], inc=True)
                bank[b] = A(pT[0:kn_, ki, kc:T3], PB[b][0:kn_, kc:T3], ACT.Copy, w=[e])
            t_B[h] = e
            t = last("a")
            b = 0
            for y, (ki, kn_, kc) in enumerate((TL[2], TL[0], TL[1])):
                e = mm(PB[b][:, kc:T3], vt[0:kn_, ki, 128 * h:128 * h + 128], pT[0:kn_, ki, kc:T3], y == 0, y == 2,
                       w=[t, bank[b]], inc=y == 2)
            bank[b] = V(tt, yT[:, h, :], PB[b][:, 0:T3], yT[:, h, :], ALU.mult, w=[e])

        t = scores(0)
        for h in range(8):
            t2 = scores(h + 1) if h < 7 else None
            values(h, t)
            t = t2
        for s in uq + uk:
            s.free = [last("t")]
        dump("yT3", yT, [last("v")])
        project(yT, 8, TL)
        dump("mla", X[:, 0:2, :], [last("v")])

        norm_T("b_norm", big[:, 0:3 * D])
        S.ahead()
        barrier_all()
        take = arena()
        uT = take(8, T3)
        gT = take(8, T3)
        pad = [take(T3 + 3) for _ in range(2)]
        al = take(8, T3)
        ml = take(8, T3)
        bl = take(8, T3)
        sp = take(8)
        z8 = take(3, 8)
        l8 = take(8)
        lam = col("lam", 0, 8)
        V(ts, sp, lam, 0.0, None, ALU.min)
        t = V(stt, z8[:, 0, :], sp, 2.0, lam, ALU.mult, ALU.subtract)
        t = A(z8[:, 0, :], z8[:, 0, :], ACT.Exp, w=[t])
        run(log1p(z8[:, 0, :], z8[:, 1, :], z8[:, 2, :], l8, [t]))
        V(tt, sp, l8, sp, ALU.subtract)
        V(ts, sp, sp, -8.0, None, ALU.mult)
        V(ve.memset, pad[0][:, 0:3], 0.0)
        V(ve.memset, pad[1][:, 0:3], 0.0)
        for p in range(4):
            for q in range(2):
                w_ = S.get(12 + 2 * p + q)
                for f in range(2):
                    o = 2 * p + f
                    b = 4 * (p % 2) + 2 * q + f
                    for kk in range(8):
                        e = mm3(PB[b][:, 0:T3], (w_.H[:, kk, 128 * f:128 * f + 128], w_.L[:, kk, 128 * f:128 * f + 128]),
                                XT(kk, 0, T3), kk == 0, kk == 7, w=[*w_.toks[kk // 4], bank[b]], inc=kk == 7)
                    if q == 0:
                        P_ = pad[f]
                        bank[b] = V(cp, P_[:, 3:3 + T3], PB[b][:, 0:T3], w=[e])
                        V(ts, uT[:, o, :], P_[:, 0:T3], col("conv_w_3", o), col("conv_b_3", o), ALU.mult, ALU.add)
                        for j in range(1, 4):
                            V(stt, uT[:, o, :], P_[:, j:j + T3], col("conv_w_3", 8 * j + o), uT[:, o, :], ALU.mult, ALU.add)
                    else:
                        bank[b] = A(gT[:, o, :], PB[b][:, 0:T3], ACT.Silu, w=[e])
                S.done(12 + 2 * p + q, e)
        t_u = last("v")
        ws = [S.get(20, False), S.get(21, False)]
        for g in range(4):
            hv = [halves(uT[:, 2 * g + kk, :], T3, [t_u]) for kk in range(2)]
            for f in range(2):
                o = 2 * g + f
                for q in range(2):
                    b = 4 * (g % 2) + 2 * f + q
                    for kk in range(2):
                        e = mm3(PB[b][:, 0:T3], (ws[q].H[:, g, kk, 128 * f:128 * f + 128], ws[q].L[:, g, kk, 128 * f:128 * f + 128]),
                                hv[kk][1], kk == 0, kk == 1, w=[*ws[q].toks[0], *ws[q].toks[1], *hv[kk][2], bank[b]], inc=kk == 1)
                    bank[b] = A((al, bl)[q][:, o, :], PB[b][:, 0:T3], ACT.Sigmoid, bias=col(("b_rg", "b_ig")[q], o), w=[e])
            for kk in range(2):
                rb_free[hv[kk][0]] = e
        for q in range(2):
            S.done(20 + q, e)
        S.ahead()
        for o in range(8):
            t = V(ts, al[:, o, :], al[:, o, :], sp[:, o:o + 1], None, ALU.mult, w=[last("a")] if o == 0 else [])
        V(tt, bl[:, :, :], bl[:, :, :], uT[:, :, :], ALU.mult)
        for o in range(0, 8, 4):
            A(ml[:, o:o + 4, :], al[:, o:o + 4, :], ACT.Tanh, w=[t])
            t1 = A(al[:, o:o + 4, :], al[:, o:o + 4, :], ACT.Exp)
            V(tt, uT[:, o:o + 4, :], al[:, o:o + 4, :], al[:, o:o + 4, :], ALU.mult, w=[t1])
            t2 = V(stt, uT[:, o:o + 4, :], uT[:, o:o + 4, :], 1.0, ml[:, o:o + 4, :], ALU.add, ALU.mult)
        for o in range(0, 8, 4):
            A(ml[:, o:o + 4, :], uT[:, o:o + 4, :], ACT.Sqrt, scale=-1.0, w=[t2])
        t = last("a")
        V(ve.memset, ml[:, :, 0:1], 1.0, w=[t])
        V(tt, bl[:, :, :], bl[:, :, :], ml[:, :, :], ALU.mult)
        for o in range(8):
            V(ve.tensor_tensor_scan, ml[:, o, :], al[:, o, :], bl[:, o, :], 0.0, ALU.mult, ALU.add)
            V(tt, gT[:, o, :], gT[:, o, :], ml[:, o, :], ALU.mult)
        dump("gT3", gT, [last("v")])
        project(gT, 22, TL[0:2])
        fg = load(I["rows"][:, RO["final_g"]:RO["final_g"] + 1024], 1024)
        t = rstd([(X[:, i, :], 128) for i in range(2)], 0, D, junk=uT.rearrange("p a b -> p (a b)"))
        for i in range(2):
            t = V(stt, X[:, i, :], X[:, i, :], st[:, i:i + 1], fg.ap, ALU.mult, ALU.mult, w=[fg.tok])
        fg.free = [t]
        store(out.rearrange("a (t p) d -> p (a t) d", p=128), X[:, 0:2, :], [t])

    for nm, fn in (("first", first), ("second", second), ("third", third)):
        if only is None or nm in only:
            fn()
    for s in stores:
        nc.sync.wait_ge(s, 16)


WEIGHTS = ["x", "ctx", "w_mod", "w_in", "w_out", "w_router", "w1", "w3", "w2", "ctx_2", "w_ada_2", "w13_a_2", "w2_a_2",
           "w_in_2", "w_four_2", "w_mproj_2", "w_out_2", "w13_b_2", "w2_b_2", "meta_tokens_3", "a_w_in_3", "a_w_uq_3",
           "a_w_ukv_3", "a_w_out_3", "b_w_in_3", "b_w_rg_3", "b_w_ig_3", "b_w_out_3"]


def constants():
    f = np.float32
    K = {n: np.zeros((128, w), f) for n, w in CONSTS}
    K["ident"][:] = np.eye(128)
    K["ones"][:] = 1
    inv = (f(10000.0) ** (-np.arange(16, dtype=f) / f(16))).astype(f)
    tok = np.arange(256)
    ang = np.concatenate([(tok // 64).astype(f)[:, None] * inv, (tok % 64).astype(f)[:, None] * inv], 1).astype(f)
    K["rope1"][:] = np.stack([np.cos(ang), np.sin(ang)], 1).reshape(2, 128, 64).transpose(1, 0, 2).reshape(128, 128)
    inv = (f(10000.0) ** (-np.arange(0, 64, 2, dtype=f) / f(64))).astype(f)
    r3 = np.zeros((128, 3, 2, 32), f)
    for i, n, c in ((0, 128, 16), (1, 128, 144), (2, 16, 0)):
        a = (np.arange(c, c + n, dtype=f)[:, None] * inv).astype(f)
        r3[:n, i, 0], r3[:n, i, 1] = np.cos(a), np.sin(a)
    K["rope3"][:] = r3.reshape(128, 192)
    K["slot"][:] = np.arange(1, 33)
    s, t = np.arange(128)[:, None], np.arange(128)[None, :]
    K["tri"][:] = np.concatenate([np.where(s <= t, 0, NEG), np.where(s >= t, 0, NEG)], 1)
    for i in range(8):
        p = 32 * (i // 4) + i % 4
        K["m8"][p, i] = 1
        K["sel_i"][8 * (i // 4) + i % 4, p] = 1
        K["sel_f"][8 * (i // 4) + 4 + i % 4, p] = 1
    consts = np.concatenate([K[n] for n, _ in CONSTS], 1)
    mask = np.full((128, 3, 272), NEG, f)
    for i, n, c in ((0, 128, 16), (1, 128, 144), (2, 16, 0)):
        mask[:n, i] = np.where(np.arange(272)[None, :] <= np.arange(c, c + n)[:, None], 0, NEG)
    r, w = np.arange(256) // 64, np.arange(256) % 64
    th = 2 * np.pi * (np.outer(r, r) / 4 + np.outer(w, w) / 64)
    ct = np.concatenate([np.cos(th), np.sin(th)], 1).reshape(2, 128, 512).transpose(1, 0, 2).reshape(128, 1024)
    pc = 2 * np.pi * np.outer(np.arange(128), np.arange(128)) / 128
    nrm = 1 / np.sqrt(256 * 128)
    four = np.concatenate([ct, np.cos(pc) * nrm, -np.sin(pc) * nrm], 1).astype(f)
    return {"consts": consts, "mask3": mask.reshape(128, 816), "four": four}


def layout(I):
    def c(v):
        v = np.asarray(v).reshape(-1)
        return v.reshape(-1, 128).T
    b_in = np.asarray(I["b_in_2"])[0]
    gate = np.zeros((128, 2), b_in.dtype)
    for d in range(2):
        for q in range(2):
            gate[32 * d:32 * d + 4, q] = b_in[4608 + 8 * d + 4 * q:4612 + 8 * d + 4 * q]
    parts = {"c": c(I["c"]), "c_ctx": c(I["c_ctx"]), "b_mod": c(I["b_mod"]), "g_mix": c(I["g_mix"]),
             "g_ffn": c(I["g_ffn"]), "c_2": c(I["c_2"]), "c_ctx_2": c(I["c_ctx_2"]), "b_ada_2": c(I["b_ada_2"]),
             "norm_g_2": c(I["norm_g_2"]), "b_q": c(b_in[512:1536]), "b_k": c(b_in[1536:2560]),
             "b_gf": c(b_in[4624:5648]), "b_gm": c(b_in[5648:6672]), "conv_w_2": c(I["conv_w_2"]),
             "conv_b_2": c(I["conv_b_2"]), "b_s": np.asarray(I["b_s"])[0].T, "a_norm": c(I["a_norm_g_3"]),
             "a_qn": c(I["a_q_norm_g_3"]), "a_kvn": c(I["a_kv_norm_g_3"]), "b_norm": c(I["b_norm_g_3"]),
             "conv_w_3": c(I["b_conv_w_3"]), "conv_b_3": c(I["b_conv_b_3"]), "b_rg": c(I["b_b_rg_3"]),
             "b_ig": c(I["b_b_ig_3"]), "lam": c(I["b_lam_3"]), "b_gate": gate}
    cols = np.concatenate([parts[n] for n, _ in COLS], 1)
    rows = {"q_gain": np.tile(np.asarray(I["q_gain"])[0], 8), "k_gain": np.tile(np.asarray(I["k_gain"])[0], 2),
            "v_gain": np.asarray(I["v_gain"])[0], "g_final": I["g_final"], "b_f": b_in[0:512], "b_v": b_in[2560:3584],
            "b_o": b_in[3584:4608], "head_g": np.asarray(I["head_g_2"])[0], "final_g": I["final_norm_g_3"]}
    row = np.concatenate([np.asarray(rows[n]) for n, _ in ROWS])
    return {"cols": np.ascontiguousarray(cols), "rows": np.ascontiguousarray(np.broadcast_to(row, (128, NROW))),
            "w_sT": np.ascontiguousarray(np.asarray(I["w_s"])[0].transpose(2, 0, 1).reshape(128, 1024))}


def arrays_of(inputs):
    out = {n: np.ascontiguousarray(inputs[n]) for n in WEIGHTS}
    out.update(layout(inputs))
    out.update(constants())
    return out


def kernel(**inputs):
    import concourse.bacc as _bacc
    from concourse.bass_utils import run_bass_kernel_spmd as _run

    nc = _bacc.Bacc("TRN2", target_bir_lowering=False, num_devices=1)
    arrays, I = {}, {}
    for name, a in arrays_of(inputs).items():
        arrays[f"in_{name}"] = a
        I[name] = nc.dram_tensor(f"in_{name}", a.shape, mybir.dt.from_np(a.dtype), kind="ExternalInput").ap()
    o = nc.dram_tensor("out_0", (1, 256, D), F32, kind="ExternalOutput").ap()
    build(nc, I, o)
    r = _run(nc, [arrays], core_ids=[0])
    return r.results[0]["out_0"]
```

```python
from contextlib import ExitStack

import numpy as np
import concourse.bass as bass
from concourse import mybir

F32 = mybir.dt.float32
F32R = mybir.dt.float32r
ALU = mybir.AluOpType
ACT = mybir.ActivationFunctionType
AX = mybir.AxisListType.X
D = 1024
NSLOT = 7
BIG = 12544
NEG = -1e30

COLS = [("c", 8), ("c_ctx", 8), ("b_mod", 48), ("g_mix", 8), ("g_ffn", 8),
        ("c_2", 8), ("c_ctx_2", 8), ("b_ada_2", 72), ("norm_g_2", 48), ("b_q", 8), ("b_k", 8), ("b_gf", 8),
        ("b_gm", 8), ("conv_w_2", 48), ("conv_b_2", 16), ("b_s", 8),
        ("a_norm", 8), ("a_qn", 3), ("a_kvn", 2), ("b_norm", 8), ("conv_w_3", 32), ("conv_b_3", 8),
        ("b_rg", 8), ("b_ig", 8), ("lam", 8), ("b_gate", 2)]
CO, _n = {}, 0
for _name, _w in COLS:
    CO[_name] = _n
    _n += _w
NCOL = _n
ROWS = [("q_gain", 512), ("k_gain", 128), ("v_gain", 512), ("g_final", 1024), ("b_v", 1024),
        ("b_o", 1024), ("head_g", 1024), ("b_f", 512), ("final_g", 1024)]
RO, _n = {}, 0
for _name, _w in ROWS:
    RO[_name] = _n
    _n += _w
NROW = _n
CONSTS = [("ident", 128), ("ones", 128), ("rope1", 128), ("rope3", 192), ("slot", 32), ("tri", 256),
          ("m8", 8), ("sel_i", 36), ("sel_f", 36)]
KO, _n = {}, 0
for _name, _w in CONSTS:
    KO[_name] = _n
    _n += _w
NCONST = _n


def build(nc, I, out, dbg=None):
    ctx = ExitStack()
    with ctx:
        _build(nc, I, out, ctx, dbg)


def _build(nc, I, out, ctx, dbg):
    def sb(name, shape, dt=F32):
        return ctx.enter_context(nc.sbuf_tensor(name, shape, dt))

    def sem(name):
        return ctx.enter_context(nc.semaphore(name))

    ring = sb("ring", [128, NSLOT, 2048])
    X = sb("X", [128, 4, D])
    HH = sb("HH", [128, 8, 512], F32R)
    HL = sb("HL", [128, 8, 512], F32R)
    WB = sb("WB", [128, 2, 2, 2048], F32R)
    RB = sb("RB", [128, 2, 2, 512], F32R)
    big = sb("big", [128, BIG])
    cols = sb("cols", [128, NCOL])
    K = sb("K", [128, NCONST])
    cs = sb("cs", [128, 2, 8, 2])
    mraw = sb("mraw", [128, 512])
    mcol1 = sb("mcol1", [128, 48, 2])
    mcol2 = sb("mcol2", [128, 72, 2])
    AB = sb("AB", [128, 64])
    BO = sb("BO", [128, 36])
    st = sb("st", [128, 64])
    PB = [ctx.enter_context(nc.psum_tensor(f"pb{i}", [128, 512], F32)) for i in range(8)]

    eng = {"v": nc.vector, "a": nc.scalar, "g": nc.gpsimd, "t": nc.tensor, "s": nc.sync}
    esem = {e: sem("s_" + e) for e in "vagt"}
    count = {e: 0 for e in "vagt"}
    waited = {e: {} for e in "vagts"}

    def wait(e, toks):
        for t in toks:
            if t is None:
                continue
            s, n, key = t
            if waited[e].get(key, 0) < n:
                eng[e].wait_ge(s, n)
                waited[e][key] = n

    def done(e, ins):
        count[e] += 1
        ins.then_inc(esem[e], 1)
        return (esem[e], count[e], e)

    def last(e):
        return (esem[e], count[e], e) if count[e] else None

    def V(name, *args, w=(), **kw):
        wait("v", [last("v"), *w])
        return done("v", name(*args, **kw))

    def A(out_, in_, func, w=(), **kw):
        wait("a", [last("a"), *w])
        return done("a", nc.scalar.activation(out_, in_, func, **kw))

    def G(name, *args, w=(), **kw):
        wait("g", [last("g"), *w])
        return done("g", name(*args, **kw))

    def mm(o, l, r, start=True, stop=True, w=(), inc=False):
        wait("t", w)
        i = nc.tensor.matmul(o, l, r, start=start, stop=stop)
        return done("t", i) if inc else None

    def tp(o, in_, w=(), inc=False):
        n = in_.shape[0]
        wait("t", w)
        i = nc.tensor.transpose(o, in_, ident[0:n, 0:n])
        return done("t", i) if inc else None

    ve = nc.vector
    tt, ts, stt, cp = ve.tensor_tensor, ve.tensor_scalar, ve.scalar_tensor_tensor, ve.tensor_copy

    nload = [0]
    stores = []

    def store(dst, src, w):
        wait("s", w)
        s = sem(f"st{len(stores)}")
        nc.sync.dma_start(dst, src).then_inc(s, 16)
        stores.append(s)
        return (s, 16, f"st{len(stores)}")

    def dump(name, ap, w):
        if dbg is not None and name in dbg:
            t = store(dbg[name], ap, [*w, last("g")])
            wait("v", [t])
            wait("a", [t])

    def load_once(dst, src):
        nload[0] += 1
        s = sem(f"ld{nload[0]}")
        nc.sync.dma_start(dst, src).then_inc(s, 16)
        return (s, 16, f"ld{nload[0]}")

    class Slot:
        pass

    slot_sem = [sem(f"rs{i}") for i in range(NSLOT)]
    slot_use = [0] * NSLOT
    slot_last = [None] * NSLOT
    nslot = [0]

    def load(src, n, pat=None, parts=128, **dims):
        while slot_last[nslot[0] % NSLOT] is not None and slot_last[nslot[0] % NSLOT].free is None:
            nslot[0] += 1
        i = nslot[0] % NSLOT
        nslot[0] += 1
        if slot_last[i] is not None:
            wait("s", slot_last[i].free)
        s = Slot()
        s.i = i
        ap = ring[0:parts, i, 0:n]
        s.ap = ap.rearrange(pat, **dims) if pat else ap
        nc.sync.dma_start(s.ap, src).then_inc(slot_sem[i], 16)
        slot_use[i] += 16
        s.tok = (slot_sem[i], slot_use[i], f"rs{i}")
        s.free = None
        slot_last[i] = s
        return s

    def scratch():
        while slot_last[nslot[0] % NSLOT] is not None and slot_last[nslot[0] % NSLOT].free is None:
            nslot[0] += 1
        i = nslot[0] % NSLOT
        nslot[0] += 1
        s = Slot()
        s.ap = ring[:, i, :]
        s.tok = None
        if slot_last[i] is not None:
            for e in "va":
                wait(e, [*slot_last[i].free, slot_last[i].tok])
        s.free = None
        slot_last[i] = s
        return s

    class Halves:
        pass

    wb_free = [None, None]

    class Stream:

        def __init__(self):
            self.specs, self.n, self.out = [], 0, {}

        def add(self, specs):
            self.specs += specs
            return len(self.specs) - len(specs)

        def ahead(self):
            if self.n == len(self.specs):
                return
            src, n, pat, dims = self.specs[self.n]
            s = load(src, n, pat, **dims)
            b = wbn[0] % 2
            wbn[0] += 1
            assert wb_free[b] != "held"
            h = Halves()
            h.b = b
            flat = ring[:, s.i, :]
            h.toks = []
            m = (n // 2 + 1) // 2 * 2
            for (x, y) in ((0, m), (m, n)):
                ta = A(WB[:, b, 0, x:y], flat[:, x:y], ACT.Copy, w=[s.tok, wb_free[b]])
                tv = V(tt, WB[:, b, 1, x:y], flat[:, x:y], WB[:, b, 0, x:y].bitcast(F32), ALU.subtract,
                       w=[ta, s.tok, wb_free[b]])
                h.toks.append((ta, tv))
            s.free = [ta, tv]
            h.H, h.L = WB[:, b, 0, 0:n], WB[:, b, 1, 0:n]
            if pat:
                h.H, h.L = h.H.rearrange(pat, **dims), h.L.rearrange(pat, **dims)
            wb_free[b] = "held"
            self.out[self.n] = h
            self.n += 1

        def get(self, i, ahead=True):
            if not self.out:
                self.n = i
            while self.n <= i:
                self.ahead()
            if self.n == i + 1 and ahead:
                self.ahead()
            return self.out[i]

        def done(self, i, t):
            wb_free[self.out[i].b] = t

    wbn = [0]

    def mm3(o, l, r, start, stop, w=(), inc=False):
        mm(o, l[0], r[0], start, False, w=w)
        mm(o, l[0], r[1], False, False)
        return mm(o, l[1], r[0], False, stop, inc=inc)

    rbn = [0]
    rb_free = [None, None]

    def halves(x, n, w):
        b = rbn[0] % 2
        rbn[0] += 1
        ta = A(RB[:, b, 0, 0:n], x, ACT.Copy, w=[*w, rb_free[b]])
        tv = V(tt, RB[:, b, 1, 0:n], x, RB[:, b, 0, 0:n].bitcast(F32), ALU.subtract, w=[ta, *w, rb_free[b]])
        return b, (RB[:, b, 0, 0:n], RB[:, b, 1, 0:n]), [ta, tv]

    bank = [None] * 8

    def barrier():
        return [last(e) for e in "vagt"]

    def join():
        a, v, t = last("a"), last("v"), last("t")
        wait("v", [a, t])
        wait("a", [v, t])

    def barrier_all():
        b = barrier()
        for e in "vagt":
            wait(e, b)

    t_k = load_once(K[:], I["consts"])
    t_cols = load_once(cols[:], I["cols"])
    xv = I["x"].rearrange("a (t p) d -> p (a t) d", p=128)
    xc = I["ctx"].rearrange("a (t p) d -> p (a t) d", p=128)

    def load_x():
        return load_once(X[:, 0:2, :], xv), load_once(X[:, 2:4, :], xc)

    def k(name, n=None):
        w = dict(CONSTS)[name]
        return K[:, KO[name]:KO[name] + (n or w)]

    ident = k("ident")
    ones = k("ones")

    def col(name, i=0, n=1):
        return cols[:, CO[name] + i:CO[name] + i + n]

    def arena(start=0):
        at = [start]

        def take(*shape, parts=128):
            n = 1
            for s in shape:
                n *= s
            ap = big[0:parts, at[0]:at[0] + n]
            at[0] += n
            assert at[0] <= BIG, at[0]
            if len(shape) == 2:
                ap = ap.rearrange("p (a b) -> p a b", a=shape[0])
            elif len(shape) == 3:
                ap = ap.rearrange("p (a b c) -> p a b c", a=shape[0], b=shape[1])
            return ap
        return take

    for e in "vagt":
        wait(e, [t_k, t_cols])
    V(ve.memset, mraw[:], 0.0)
    wait("a", [V(ve.memset, st[:], 1.0)])

    def rstd(tiles, base, d, w=(), junk=None, eps=1e-6):
        t = None
        for i, (ap, n) in enumerate(tiles):
            t = A(junk[0:n, 0:d], ap, ACT.Square, accum_out=st[0:n, base + i:base + i + 1], w=w)
        return rstd_of(base, len(tiles), d, t, eps)

    x_tok = {}

    def rstd_x(tiles, junk):
        for i, (ap, n) in enumerate(tiles):
            t = A(junk[0:n, 0:D], ap, ACT.Square, accum_out=st[0:n, 16 + i:17 + i], w=[x_tok.get(i)])
        return rstd_of(16, len(tiles), D, t)

    def rstd_of(base, n, d, t, eps=1e-6, src=None, dst=None, parts=128):
        s = st[0:parts, base:base + n] if src is None else src
        t = V(ts, s, s, 1.0 / d, eps, ALU.mult, ALU.add, w=[t])
        t = A(s, s, ACT.Sqrt, w=[t])
        return V(ve.reciprocal, s, s, w=[t])

    def transposed(tiles, regions, xn, w, ready, f32=None, both=True, use=None):
        c0, c1 = regions[0][0], regions[-1][1]
        late = None
        for kk in range(8):
            b = kk % 4
            for i, (ap, n, r, c) in enumerate(tiles):
                q = b if c < regions[0][1] else 4 + b
                te = tp(PB[q][:, c:c + n], xn(i)[0:n, kk * 128:kk * 128 + 128], w=[ready[i], bank[q]], inc=True)
                if q == b:
                    t = te
            v = tmpT[:, kk % 2, :] if f32 is None else f32[:, kk, :]
            x, y, a, s = regions[0]
            if s is None:
                t2 = V(ts, v[:, x:y], PB[b][:, x:y], a(kk), None, ALU.mult, w=[t, ta_T[kk % 2]])
            else:
                t2 = V(ts, v[:, x:y], PB[b][:, x:y], a(kk), s(kk), ALU.mult, ALU.add, w=[t, ta_T[kk % 2]])
            bank[b] = t2
            if use:
                if kk:
                    use(kk - 1, t_use)
                t_use = t2
            if len(regions) == 2:
                x, y, a, s = regions[1]
                bank[4 + b] = A(v[:, x:y], PB[4 + b][:, x:y], ACT.Identity, bias=s(kk), scale=a(kk), w=[te, *tv_T[kk % 2]])
            if both:
                ta = A(HH[:, kk, c0:c1], v[:, c0:c1], ACT.Copy, w=[t2, *w])
                ta_T[kk % 2] = ta
                if late:
                    late()

                def late(kk=kk, v=v, ta=ta):
                    tv = V(tt, HL[:, kk, c0:c1], v[:, c0:c1], HH[:, kk, c0:c1].bitcast(F32), ALU.subtract, w=[ta, *w])
                    xt_tok[kk] = [*xt_tok[kk], ta, tv]
                    tv_T[kk % 2] = [tv]
                    return tv
        if both:
            t2 = late()
        return use(7, t_use) if use else t2

    tmpT = sb("tmpT", [128, 2, 512])
    xt_tok = [[]] * 8
    ta_T = [None, None]
    tv_T = [[], []]

    def scaled(tiles, xn, w):
        ready = []
        for i, (ap, n, r, c) in enumerate(tiles):
            if i % 2 == 0:
                ready.append(V(ts, xn(i)[0:n, :], ap, st[0:n, r:r + 1], None, ALU.mult, w=w))
            else:
                ready.append(A(xn(i)[0:n, :], ap, ACT.Copy, scale=st[0:n, r:r + 1], w=w))
        return ready

    def modulated_T(tiles, regions, xn, w, f32=None, both=True):
        ready = scaled(tiles, xn, w)
        return transposed(tiles, regions, xn, [last("t")], ready, f32, both)

    def gemv(w_dram, which, bname, nchunk, mcol, acc):
        for nb in range((nchunk + 3) // 4):
            q = min(4, nchunk - 4 * nb)
            for kk in range(8):
                s = load(w_dram[kk * 128:kk * 128 + 128, nb * 2048:nb * 2048 + q * 512], q * 512)
                for j in range(q):
                    e = mm(PB[acc][32 * j:32 * j + 2, :], cs[:, which, kk, :], s.ap[:, 512 * j:512 * j + 512],
                           kk == 0, kk == 7, w=[s.tok, bank[acc]], inc=j == q - 1)
                s.free = [e]
                yield
            for j in range(q):
                f = A(mraw[32 * j:32 * j + 2, :], PB[acc][32 * j:32 * j + 2, :], ACT.Copy, w=[e, last("t")])
            bank[acc] = f
            yield
            pick = ident.rearrange("p (j c) -> p j c", j=4)[:, 0:q, 0:2]
            for i in range(4):
                e = mm(PB[acc][:, 8 * i:8 * i + 2 * q].rearrange("p (j c) -> p j c", c=2), mraw[:, 128 * i:128 * i + 128], pick,
                       w=[f, bank[acc]], inc=i == 3)
            c = 16 * nb
            bank[acc] = V(tt, mcol[:, c:c + 4 * q, :].rearrange("p (j i) c -> p i j c", i=4),
                          PB[acc][:, 0:32].rearrange("p (i j c) -> p i j c", i=4, c=2)[:, :, 0:q, :],
                          col(bname, c, 4 * q).rearrange("p (j i) -> p i j", i=4)[:, :, :, None].to_broadcast([128, 4, q, 2]),
                          ALU.add, w=[e])
            yield

    def run(g):
        for _ in g:
            pass

    def steps(g, n):
        for _ in range(n):
            next(g, None)

    def row_steps(dst, c8, tmp, w, bank_=3):
        for z in range(2):
            t = V(tt, tmp.rearrange("p (k f) -> p k f", k=4), ident[:, None, :].to_broadcast([128, 4, 128]),
                  c8[:, 4 * z:4 * z + 4, None].to_broadcast([128, 4, 128]), ALU.mult, w=[*w, last("t")])
            yield
            e = mm(PB[bank_][:, :], ones, tmp, w=[t, bank[bank_]], inc=True)
            bank[bank_] = A(dst[:, 512 * z:512 * z + 512], PB[bank_][:, :], ACT.Copy, w=[e])

    def row_of(dst, c8, tmp, w, bank_=3):
        run(row_steps(dst, c8, tmp, w, bank_))
        return bank[bank_]

    def rope(dst1, dst2, x1, x2, cos, sin, t1, w):
        V(tt, t1[0], x1, cos, ALU.mult, w=w)
        V(tt, t1[1], x2, sin, ALU.mult)
        V(tt, dst1, t1[0], t1[1], ALU.subtract)
        V(tt, t1[0], x1, sin, ALU.mult)
        V(tt, t1[1], x2, cos, ALU.mult)
        return V(tt, dst2, t1[0], t1[1], ALU.add)

    only = dbg.get("only") if dbg else None

    def XT(kk, c, n=128):
        wait("t", xt_tok[kk])
        return HH[:, kk, c:c + n], HL[:, kk, c:c + n]

    def both(a, b, n=1):
        end = object()
        while True:
            x = next(a, end)
            for _ in range(n):
                y = next(b, end)
            if x is end and y is end:
                return

    def rows2(w, c0=0, n=D):
        return [(w[q * 256:q * 256 + 256, c0:c0 + n].rearrange("(a p) n -> p a n", p=128), 2 * n, "p (a n) -> p a n",
                 dict(a=2)) for q in range(w.shape[0] // 256)]

    def cols256(w, c0, a=8, n=256):
        return (w[:, c0:c0 + n].rearrange("(a p) n -> p a n", p=128), a * n, "p (a n) -> p a n", dict(a=a))

    def ffn_specs(w13, w2):
        return [x for p in range(11) for x in (cols256(w13, 256 * p), cols256(w13, 2816 + 256 * p))] + rows2(w2)

    CF, CQ, CK, CV, CO_, CG, CB = 0, 512, 1536, 2560, 3584, 4608, 4624
    at = {}

    def mixer_specs(base):
        w_in = I["w_in_2"][0]
        specs = [cols256(w_in, CG, 8, 128)]
        specs += [(w_in[512 * q:512 * q + 512, CF:CF + 512].rearrange("(a p) n -> p a n", p=128), 2048, "p (a n) -> p a n",
                   dict(a=4)) for q in range(2)]
        for h in range(5):
            for c0 in ((CQ, CK, CV) if h < 4 else ()):
                at[(c0, h)] = base + len(specs)
                specs.append(cols256(w_in, c0 + 256 * h))
            if h:
                at[(CO_, h - 1)] = base + len(specs)
                specs.append(cols256(w_in, CO_ + 256 * (h - 1)))
        at["merge"] = base + len(specs)
        for p in range(4):
            specs += [cols256(w_in, CB + 256 * p), cols256(w_in, CB + D + 256 * p), cols256(I["w_four_2"][0], 256 * p, 4),
                      cols256(I["w_mproj_2"][0], 256 * p)]
        at["out"] = base + len(specs)
        return specs + rows2(I["w_out_2"][0])

    S = Stream()
    S.add(rows2(I["w_in"][0], 0, 768) + rows2(I["w_in"][0], 768, 1024) + rows2(I["w_out"][0]))
    s_ffa = S.add(ffn_specs(I["w13_a_2"][0], I["w2_a_2"][0]))
    s_mix = S.add(mixer_specs(len(S.specs)))
    s_ffb = S.add(ffn_specs(I["w13_b_2"][0], I["w2_b_2"][0]))
    s_3 = S.add(rows2(I["a_w_in_3"][0], 0, 704) + [cols256(I["a_w_in_3"][0], 704 + 256 * p) for p in range(4)]
                + rows2(I["a_w_out_3"][0])
                + [x for p in range(4) for x in (cols256(I["b_w_in_3"][0], 256 * p), cols256(I["b_w_in_3"][0], D + 256 * p))]
                + [(I[n][0].rearrange("g (a p) n -> p g a n", p=128), 2048, "p (g a n) -> p g a n", dict(g=4, a=2))
                   for n in ("b_w_rg_3", "b_w_ig_3")] + rows2(I["b_w_out_3"][0]))

    def first():
        for i, (l, c) in enumerate((("c", "c_ctx"), ("c_2", "c_ctx_2"))):
            A(cs[:, i, :, 0], col(l, 0, 8), ACT.Silu)
            t = A(cs[:, i, :, 1], col(c, 0, 8), ACT.Silu)
        wait("t", [t])
        take = arena()
        xn = take(4, D)
        tl = [(X[:, i, :], 128, i, 128 * i) for i in range(4)]
        g1 = gemv(I["w_mod"][0], 0, "b_mod", 12, mcol1, 7)
        steps(g1, 3)
        t_x, t_c = load_x()
        t = rstd([(X[:, i, :], 128) for i in range(4)], 0, D, w=[t_x, t_c], junk=xn[:, 0, :])
        ready = scaled(tl, lambda i: xn[:, i, :], [t])
        steps(g1, 7)
        S.ahead()
        for i, which in enumerate((0, 1)):
            V(stt, AB[:, 8 * i:8 * i + 8], mcol1[:, 8:16, which], 1.0, col("g_mix", 0, 8), ALU.add, ALU.mult)
        wait("a", [last("v")])
        t_h = transposed(tl, [(0, 256, lambda q: AB[:, q:q + 1], lambda q: mcol1[:, q, 0:1]),
                              (256, 512, lambda q: AB[:, 8 + q:9 + q], lambda q: mcol1[:, q, 1:2])],
                         lambda i: xn[:, i, :], [], ready)
        join()

        def vectors():
            yield from g1
            yield from gemv(I["w_ada_2"][0], 1, "b_ada_2", 18, mcol2, 7)

        g2 = vectors()
        take = arena()
        qkv = take(4, 768)
        gm = take(2, D)
        w_in = I["w_in"][0]
        for q in range(4):
            if q == 1:
                wait("s", ready)
                t_c2 = load_once(X[:, 2:4, :], I["ctx_2"].rearrange("a (t p) d -> p (a t) d", p=128))
            w_ = S.get(q)
            for a in range(2):
                kk = 2 * q + a
                for i in range(2):
                    mm3(PB[i][:, :], XT(kk, 128 * i), (w_.H[:, a, 0:512], w_.L[:, a, 0:512]), kk == 0, kk == 7,
                        w=[*w_.toks[a], bank[i]])
                for i in range(4):
                    e = mm3(PB[2 + i][:, 0:256], XT(kk, 128 * i), (w_.H[:, a, 512:768], w_.L[:, a, 512:768]),
                            kk == 0, kk == 7, w=[bank[2 + i]], inc=i == 3)
            S.done(q, e)
            steps(g2, 2)
        for i in range(2):
            bank[i] = A(qkv[:, i, 0:512], PB[i][:, :], ACT.Copy, w=[e])
        for i in range(4):
            bank[2 + i] = V(cp, qkv[:, i, 512:768], PB[2 + i][:, 0:256], w=[e])
        t_qkv = [bank[1], bank[5]]
        GB = (6, 0, 1, 2)
        for q in range(4):
            w_ = S.get(4 + q)
            for a in range(2):
                kk = 2 * q + a
                for i in range(2):
                    for j in range(2):
                        b = GB[2 * i + j]
                        e = mm3(PB[b][:, :], XT(kk, 128 * i), (w_.H[:, a, 512 * j:512 * j + 512], w_.L[:, a, 512 * j:512 * j + 512]),
                                kk == 0, kk == 7, w=[*w_.toks[a], bank[b]], inc=i + j == 2)
            S.done(4 + q, e)
            steps(g2, 2)
        t_proj = e
        for i in range(2):
            for j in range(2):
                b = GB[2 * i + j]
                bank[b] = A(gm[:, i, 512 * j:512 * j + 512], PB[b][:, :], ACT.Gelu, w=[e])
        t_gm = bank[GB[3]]
        nrm = take(640)
        cos = [k("rope1")[:, 64 * i:64 * i + 32] for i in range(2)]
        sin = [k("rope1")[:, 64 * i + 32:64 * i + 64] for i in range(2)]
        qT = take(4, 256)
        kT = take(512)
        qp = take(512)
        kp = take(128)
        gains = load(I["rows"][:, 0:1152], 1152)
        s1, s2 = take(256), take(256)
        pr = [[take(512), take(512)] for _ in range(2)]
        pT = [take(4, 256), take(4, 256)]
        junk = pT[0].rearrange("p a b -> p (a b)")
        for i in range(4):
            n0 = 0 if i < 2 else 512
            nh = 10 if i < 2 else 2
            src = qkv[:, i, n0:640]
            dst = nrm[:, n0:640]
            ss = st[:, 16:16 + nh]
            V(tt, junk[:, 0:nh * 64], src, src, ALU.mult, w=t_qkv)
            t = V(ve.tensor_reduce, ss, junk[:, 0:nh * 64].rearrange("p (h d) -> p h d", d=64), AX, ALU.add)
            t = rstd_of(0, 0, 64, t, src=ss)
            V(tt, dst.rearrange("p (h d) -> p h d", d=64), src.rearrange("p (h d) -> p h d", d=64),
              ss[:, :, None].to_broadcast([128, nh, 64]), ALU.mult)
            t = V(tt, dst, dst, gains.ap[:, n0:640], ALU.mult, w=[gains.tok])
            steps(g2, 6 if i < 2 else 4)
            if i < 2:
                for (src, dst, hn) in ((nrm[:, 0:512], qp, 8), (nrm[:, 512:640], kp, 2)):
                    a = src.rearrange("p (h c d) -> p c h d", c=2, d=32)
                    for j in range(2 if hn == 8 else 1):
                        o = (dst.rearrange("p (i j c d) -> p c j i d", j=2, c=2, d=32)[:, :, j] if hn == 8 else
                             dst.rearrange("p (h c d) -> p c h d", c=2, d=32))
                        m = hn // 2 if hn == 8 else hn
                        cc = cos[i][:, None, :].to_broadcast([128, m, 32])
                        si = sin[i][:, None, :].to_broadcast([128, m, 32])
                        sc = [z[:, 0:32 * m].rearrange("p (h d) -> p h d", h=m) for z in (s1, s2)]
                        t = rope(o[:, 0], o[:, 1], a[:, 0, 4 * j:4 * j + m], a[:, 1, 4 * j:4 * j + m], cc, si, sc, [last("t")])
                for c in range(4):
                    e = tp(PB[2][:, 128 * c:128 * c + 128], qp[:, 128 * c:128 * c + 128], w=[t, bank[2]], inc=True)
                bank[2] = A(qT[:, :, 128 * i:128 * i + 128], PB[2][:, :].rearrange("p (c t) -> p c t", c=4), ACT.Copy, w=[e])
                e = tp(PB[3][:, 0:128], kp, w=[t, bank[3]], inc=True)
            else:
                e = tp(PB[3][:, 0:128], nrm[:, 512:640], w=[t, bank[3]], inc=True)
                wait("v", [e])
            bank[3] = A(kT[:, 128 * i:128 * i + 128], PB[3][:, 0:128], ACT.Copy, w=[e])
        t_q = last("a")
        dump("kT1", kT, [t_q])
        soft = [None] * 8

        def scores(h):
            pl, r = h % 4, 64 * (h // 4)
            for i in range(2):
                e = mm(PB[i][:, :], qT[r:r + 64, pl, 128 * i:128 * i + 128], kT[r:r + 64, :], w=[t_q, bank[i]], inc=True)
                mx, p = st[:, 32 + i:33 + i], pr[h % 2][i]
                V(ve.tensor_reduce, mx, PB[i][:, :], AX, ALU.max, w=[e])
                t = V(ts, mx, mx, -0.125, None, ALU.mult)
                bank[i] = A(p, PB[i][:, :], ACT.Exp, bias=mx, scale=0.125, accum_out=st[:, 34 + i:35 + i], w=[t, soft[h - 2] if h > 1 else None])
                V(ve.reciprocal, st[:, 36 + i:37 + i], st[:, 34 + i:35 + i], w=[bank[i]])
                t = V(ts, p, p, st[:, 36 + i:37 + i], None, ALU.mult)
            return t

        def values(h, t):
            for i in range(2):
                for s_ in range(4):
                    e = tp(PB[2 + i][:, 128 * s_:128 * s_ + 128], pr[h % 2][i][:, 128 * s_:128 * s_ + 128], w=[t, bank[2 + i]], inc=True)
                bank[2 + i] = A(pT[h % 2][:, :, 128 * i:128 * i + 128], PB[2 + i][:, :].rearrange("p (s t) -> p s t", s=4),
                                ACT.Copy, w=[e])
            soft[h] = e
            steps(g2, 5)
            b = 4 + h % 2
            ro = 64 * (h % 2)
            for s_ in range(4):
                e = mm(PB[b][ro:ro + 64, 0:256], qkv[:, s_, 640 + 64 * (h // 4):704 + 64 * (h // 4)], pT[h % 2][:, s_, :],
                       s_ == 0, s_ == 3, w=[bank[3], bank[b]], inc=s_ == 3)
            ta = A(HH[ro:ro + 64, h // 2, 0:256], PB[b][ro:ro + 64, 0:256], ACT.Copy, w=[e, t_proj])
            bank[b] = V(tt, HL[ro:ro + 64, h // 2, 0:256], PB[b][ro:ro + 64, 0:256], HH[ro:ro + 64, h // 2, 0:256].bitcast(F32),
                        ALU.subtract, w=[ta])

        ws = load(I["w_sT"], 1024, "p (g i) -> p g i", g=8)

        def gating():
            t = None
            for i in range(2):
                t = A(s12, gm[:, i, 512:1024], ACT.Square, accum_out=st[:, 40 + i:41 + i], w=[last("v")])
            t = rstd_of(40, 2, 512, t)
            for i in range(2):
                vv = gm[:, i, 512:1024]
                t = V(stt, vv, vv, st[:, 40 + i:41 + i], gains.ap[:, 640:1152], ALU.mult, ALU.mult)
                for g in range(8):
                    e = mm(PB[6][:, 64 * g:64 * g + 64], ws.ap[:, g, :], vv[:, 64 * g:64 * g + 64], w=[t, ws.tok, bank[6]], inc=g == 7)
                yield
                V(tt, vv.rearrange("p (g d) -> p g d", g=8), PB[6][:, :].rearrange("p (g d) -> p g d", g=8),
                  col("b_s", 0, 8)[:, :, None].to_broadcast([128, 8, 64]), ALU.add, w=[e])
                t = V(tt, vv, vv, gm[:, i, 0:512], ALU.mult)
                yield
                for c in range(4):
                    e = tp(PB[6][:, 128 * c:128 * c + 128], vv[:, 128 * c:128 * c + 128], w=[t, bank[6]], inc=c == 3)
                bank[6] = halves_of(PB[6][:, :].rearrange("p (c t) -> p c t", c=4), HH[:, 4:8, 128 * i:128 * i + 128],
                                    HL[:, 4:8, 128 * i:128 * i + 128], [e, t_proj])
                yield

        s12 = tmp_row[:, 0:512]
        gg = gating()
        t = scores(0)
        for h in range(8):
            t2 = scores(h + 1) if h < 7 else None
            values(h, t)
            t = t2
            steps(gg, 1)
        run(gg)
        run(g2)
        ws.free = [last("t")]
        gains.free = [last("v")]
        t_mix = [last("v"), last("a")]
        V(stt, AB[:, 16:24], mcol1[:, 32:40, 0], 1.0, col("g_ffn", 0, 8), ALU.add, ALU.mult)
        sc = scratch()
        gt = sc.ap[:, 0:1024]
        t_g = row_of(gt, mcol1[:, 16:24, 0], pr[0][0], [])
        es = rows_product(2, 8, 8, [4, 6], lambda kk: (None, XT(kk, 0, 256), t_mix), lambda i: 128 * i)
        tmp = pr[0][0]
        for i in range(2):
            for j in range(2):
                b = 2 * i + j + 4
                V(tt, tmp, PB[b][:, :], gt[:, 512 * j:512 * j + 512], ALU.mult, w=[es[i], t_g])
                x_tok[i] = bank[b] = V(tt, X[:, i, 512 * j:512 * j + 512], X[:, i, 512 * j:512 * j + 512], tmp, ALU.add)
        sc.free = [last("v")]
        dump("x1", X[:, 0:2, :], [last("v")])

        gT = big[:, 0:4096].rearrange("p (e t) -> p e t", e=16)
        take = arena()
        xn = take(2, D)
        rT = take(256, parts=16)
        rW = take(256, parts=16)
        rM = take(256, parts=16)
        m8 = take(8, parts=16)
        take = arena(4096)
        posr = RB[:, 0]
        pos = posr.bitcast(F32)
        xh, xl = (h_[:, 0:4, :].rearrange("p a b -> p (a b)").rearrange("p (i d) -> p i d", i=2) for h_ in (HH, HL))
        sil = [take(512), take(512)]
        act = take(3072)
        xeT = take(8, 512)
        aff = take(2, 16)
        slotT = take(2, 16)
        hTf = act[:, 0:2048].rearrange("p (a b) -> p a b", a=8)
        wait("v", [last("t"), last("a")])
        t = rstd_x([(X[:, i, :], 128) for i in range(2)], act[:, 0:D])
        ready = scaled([(X[:, i, :], 128, 16 + i, 128 * i) for i in range(2)], lambda i: xn[:, i, :], [t])
        s = load(I["w_router"][0].rearrange("(a p) n -> p a n", p=128), 128, "p (a n) -> p a n", a=8)

        def route(kk, t):
            e = None
            for i in range(2):
                e = mm(PB[4 + i][:, 0:16], hTf[:, kk, 128 * i:128 * i + 128], s.ap[:, kk, :], kk == 0, kk == 7,
                       w=[t, s.tok, bank[4 + i]], inc=kk == 7)
            return e

        e = transposed([(X[:, i, :], 128, i, 128 * i) for i in range(2)],
                          [(0, 256, lambda q: AB[:, 16 + q:17 + q], lambda q: mcol1[:, 24 + q, 0:1])],
                          lambda i: xn[:, i, :], [], ready, f32=hTf, both=False, use=route)
        s.free = [e]
        t_xh = halves_of(xn, xh, xl, ready)
        mx = st[:, 8:10]
        for i in range(2):
            V(ve.tensor_reduce, mx[:, i:i + 1], PB[4 + i][:, 0:16], AX, ALU.max, w=[e])
            t = bank[4 + i] = V(ts, aff[:, i, :], PB[4 + i][:, 0:16], mx[:, i:i + 1], None, ALU.subtract)
        t = A(aff, aff, ACT.Exp, w=[t])
        V(ve.tensor_reduce, mx, aff, AX, ALU.add, w=[t])
        V(ve.reciprocal, mx, mx)
        t_aff = V(tt, aff, aff, mx[:, :, None].to_broadcast([128, 2, 16]), ALU.mult)
        dump("aff", aff, [t_aff])
        for i in range(2):
            e = tp(PB[4][0:16, 128 * i:128 * i + 128], aff[:, i, :], w=[t_aff, bank[4]], inc=True)
        bank[4] = V(cp, rT, PB[4][0:16, 0:256], w=[e])
        cur = rT
        for r in range(4):
            V(ve.max, m8, cur)
            V(ve.match_replace, rW, m8, cur, -1.0)
            cur = rW
        V(ts, rM, rW, 0.0, None, ALU.is_lt)
        V(ve.memset, rT, 0.0)
        V(ve.tensor_tensor_scan, rW, rM, rT, 0.0, ALU.add, ALU.add)
        t = V(tt, rW, rW, rM, ALU.mult)
        for i in range(2):
            e = tp(PB[4][:, 16 * i:16 * i + 16], rW[:, 128 * i:128 * i + 128], w=[t, bank[4]], inc=True)
        bank[4] = V(cp, slotT, PB[4][:, 0:32].rearrange("p (i e) -> p i e", i=2), w=[e])
        for i in range(2):
            t_pos = V(tt, posr[:, i, :].rearrange("p (e s) -> p e s", e=16), slotT[:, i, :, None].to_broadcast([128, 16, 32]),
                      k("slot")[:, None, :].to_broadcast([128, 16, 32]), ALU.is_equal)
        wait("t", [t_pos])
        for kk in range(8):
            b = kk % 4
            for i in range(2):
                mm(PB[b][:, :], xh[:, i, kk * 128:kk * 128 + 128], posr[:, i, :], i == 0, False, w=[t_xh, bank[b]])
                e = mm(PB[b][:, :], xl[:, i, kk * 128:kk * 128 + 128], posr[:, i, :], False, i == 1, inc=i == 1)
            if kk % 2:
                bank[b] = V(ts, xeT[:, kk, :], PB[b][:, :], AB[:, 16 + kk:17 + kk], mcol1[:, 24 + kk, 0:1], ALU.mult, ALU.add, w=[e])
            else:
                bank[b] = A(xeT[:, kk, :], PB[b][:, :], ACT.Identity, bias=mcol1[:, 24 + kk, 0:1], scale=AB[:, 16 + kk:17 + kk], w=[e])
        t_xe = [last("v"), last("a")]
        gs = scratch()
        gg = gs.ap.rearrange("p (e c s) -> p e c s", e=16, c=4)

        def scatter_weights(i):
            for c in range(4):
                t = V(tt, gg[:, :, c, :], pos[:, i, :].rearrange("p (e s) -> p e s", e=16),
                      aff[:, i, :, None].to_broadcast([128, 16, 32]), ALU.mult, w=[last("t")])
            yield
            for q in range(4):
                b = 2 + q % 2
                for r in range(4):
                    e = tp(PB[b][:, 128 * r:128 * r + 128], gg[:, 4 * q + r].rearrange("p c s -> p (c s)"),
                           w=[t, bank[b]], inc=r == 3)
                bank[b] = A(gT[:, 4 * q:4 * q + 4, 128 * i:128 * i + 128], PB[b][:, :].rearrange("p (r t) -> p r t", r=4), ACT.Copy, w=[e])

        sw = [scatter_weights(0), scatter_weights(1)]
        steps(sw[0], 1)
        join()
        wait("t", t_xe)
        hidT = [act[:, 512 * z:512 * z + 512].rearrange("p (c m) -> p c m", c=4) for z in range(2)]
        ye = [act[:, 1024 + 1024 * z:2048 + 1024 * z] for z in range(2)]
        sil_free = [None, None]
        ye_free = [None, None]
        w1, w3, w2 = I["w1"][0], I["w3"][0], I["w2"][0]

        def scatter(x, t):
            for i in range(2):
                for j in range(2):
                    e = mm(PB[4 + 2 * i + j][:, :], gT[:, x, 128 * i:128 * i + 128], ye[x % 2][:, 512 * j:512 * j + 512],
                           x == 0, x == 15, w=[t, bank[4 + 2 * i + j]], inc=True)
            ye_free[x % 2] = e
            return e

        t_ye = None
        for x in range(16):
            z = x % 2
            for half, w_ in ((0, w1), (1, w3)):
                for kk in range(8):
                    s = load(w_[x, kk * 128:kk * 128 + 128, :], 2048)
                    for j in range(4):
                        e = mm(PB[half][32 * j:32 * j + 32, :], xeT[:, kk, 32 * x:32 * x + 32], s.ap[:, 512 * j:512 * j + 512],
                               kk == 0, kk == 7, w=[s.tok, bank[half]], inc=j == 3)
                    s.free = [e]
                if x == 0:
                    run(sw[half])
                    if half == 0:
                        steps(sw[1], 1)
                    else:
                        gs.free = [last("t")]
                if half == 0:
                    t_s = A(sil[z], PB[0][:, :], ACT.Silu, w=[e, sil_free[z]])
                    bank[0] = t_s
                    if x:
                        scatter(x - 1, t_ye)
            t = V(tt, sil[z], sil[z], PB[1][:, :], ALU.mult, w=[e, t_s])
            bank[1] = t
            for c in range(4):
                e = tp(PB[2][:, 128 * c:128 * c + 128], sil[z][:, 128 * c:128 * c + 128], w=[t, bank[2]], inc=c == 3)
            sil_free[z] = e
            t = V(cp, hidT[z], PB[2][:, :].rearrange("p (c m) -> p c m", c=4), w=[e])
            bank[2] = t
            for c in range(4):
                sl_ = [load(w2[x].rearrange("(j c p) n -> c p j n", j=4, c=4)[c][:, 2 * hf:2 * hf + 2, :], 2048,
                            "p (j n) -> p j n", j=2) for hf in range(2)]
                for n in range(2):
                    for j in range(4):
                        s = sl_[j // 2]
                        e = mm(PB[2 + n][32 * j:32 * j + 32, :], hidT[z][:, c, 32 * j:32 * j + 32],
                               s.ap[:, j % 2, 512 * n:512 * n + 512], c == 0, c == 3, w=[s.tok, t, bank[2 + n]], inc=j % 2 == 1)
                        if n == 1:
                            s.free = [e]
            A(ye[z][:, 0:512], PB[2][:, :], ACT.Copy, w=[e, ye_free[z]])
            t_ye = A(ye[z][:, 512:1024], PB[3][:, :], ACT.Copy)
            bank[2] = bank[3] = t_ye
            if x == 2 and t_c2:
                ctx_ahead(t_c2)
            if x == 4:
                t_g = row_of(tmp_row, mcol1[:, 40:48, 0], sil[1], [last("t"), last("a")])
                sil_free[1] = last("t")
        e = scatter(15, t_ye)
        r = [None] * 2
        gf = load(I["rows"][:, RO["g_final"]:RO["g_final"] + 1024], 1024)
        for i in range(2):
            for j in range(2):
                b = 4 + 2 * i + j
                V(tt, sil[1], PB[b][:, :], tmpT[:, j, :], ALU.mult, w=[e, t_g])
                t = bank[b] = V(tt, X[:, i, 512 * j:512 * j + 512], X[:, i, 512 * j:512 * j + 512], sil[1], ALU.add)
            r[i] = A(ye[0], X[:, i, :], ACT.Square, accum_out=st[:, i:i + 1], w=[t])
        dump("x2", X[:, 0:2, :], [last("v")])
        rstd_of(0, 2, D, r[1])
        for i in range(2):
            t = x_tok[i] = V(stt, X[:, i, :], X[:, i, :], st[:, i:i + 1], gf.ap, ALU.mult, ALU.mult, w=[gf.tok])
        gf.free = [t]
        dump("xf", X[:, 0:2, :], [t])

    tmp_row = tmpT[:, :, :].rearrange("p a b -> p (a b)")

    def halves_of(x, h, l, w):
        ta = A(h, x, ACT.Copy, w=w)
        return V(tt, l, x, h.bitcast(F32), ALU.subtract, w=[ta, *w])

    def ng(i):
        return col("norm_g_2", 8 * i, 8)

    def ada_scales():
        for i, (g, ch, which) in enumerate(((0, 1, 0), (0, 1, 1), (2, 4, 0), (2, 4, 1), (4, 7, 0))):
            V(stt, AB2[:, 8 * i:8 * i + 8], mcol2[:, 8 * ch:8 * ch + 8, which], 1.0, ng(g), ALU.add, ALU.mult)
        V(stt, AB2[:, 40:48], mcol2[:, 16:24, 0], 0.5, ng(1), ALU.mult, ALU.mult)
        V(stt, AB2[:, 48:56], mcol2[:, 16:24, 1], 0.5, ng(1), ALU.mult, ALU.mult)
        V(tt, AB2[:, 56:64], mcol2[:, 40:48, 0], ng(3), ALU.mult)
        return V(stt, AB2[:, 64:72], mcol2[:, 64:72, 0], 0.5, ng(5), ALU.mult, ALU.mult)

    def ctx_ahead(t_c2):
        ada_scales()
        sc = scratch()
        t = rstd([(X[:, 2 + i, :], 128) for i in range(2)], 2, D, w=[t_c2], junk=sc.ap[:, 0:D])
        modulated_T([(X[:, 2 + i, :], 128, 2 + i, 256 + 128 * i) for i in range(2)],
                    [(256, 512, lambda q: AB2[:, 8 + q:9 + q], lambda q: mcol2[:, q, 1:2])],
                    lambda i: sc.ap[:, D * i:D * i + D], [t])
        sc.free = [last("t"), last("v"), last("a")]

    AB2 = sb("AB2", [128, 72])

    def post(nt, G_, banks, tmp, es, t_g):
        r = [None] * nt
        t_x_ = [None, None]

        def squares(i):
            for j in range(2):
                e = es[i]
                r[i] = A(tmp_row[:, 0:512], PB[banks[2 * i + j]][:, :], ACT.Square, accum_out=st[:, 8 + 2 * i + j:9 + 2 * i + j], w=[e])

        def root(i):
            V(tt, st[:, i:i + 1], st[:, 8 + 2 * i:9 + 2 * i], st[:, 9 + 2 * i:10 + 2 * i], ALU.add, w=[r[i]])
            rstd_of(i, 1, D, None)

        squares(0)
        for i in range(nt):
            if i + 1 < nt:
                squares(i + 1)
            root(i)
            for j in range(2):
                b = banks[2 * i + j]
                bank[b] = V(stt, tmp[j], PB[b][:, :], st[:, i:i + 1], G_[i // 2][:, 512 * j:512 * j + 512], ALU.mult, ALU.mult,
                            w=[t_g, t_x_[j]])
                x_tok[i] = t_x_[j] = G(nc.gpsimd.tensor_tensor, X[:, i, 512 * j:512 * j + 512], X[:, i, 512 * j:512 * j + 512],
                                       tmp[j], ALU.add, w=[bank[b]])

    def rows_product(tiles, nk, s0, b0, operand, col0):
        nx = operand(0)
        es = [None] * tiles
        held = []
        for n in range(nk):
            w_ = S.get(s0 + n // 2, False)
            cur = nx
            if n < nk - 1:
                nx = operand(n + 1)
            S.get(s0 + n // 2)
            held.append((n, cur))
            if n == nk - 2:
                continue
            for i in range(tiles):
                for m, (b_, (h_, l_), tk) in held:
                    a, c = m % 2, col0(i)
                    for j in range(2):
                        b = b0[i] + j
                        es[i] = mm3(PB[b][:, :], (h_[:, c:c + 128], l_[:, c:c + 128]),
                                    (w_.H[:, a, 512 * j:512 * j + 512], w_.L[:, a, 512 * j:512 * j + 512]), m == 0, m == nk - 1,
                                    w=[*w_.toks[a], *tk, bank[b]], inc=j == 1)
            for m, (b_, hl, tk) in held:
                if b_ is not None:
                    rb_free[b_] = es[-1]
            held = []
            if n % 2 == 1:
                S.done(s0 + n // 2, es[-1])
        return es

    def row_all(dsts, c8s, tmp):
        for d, c8 in zip(dsts, c8s):
            yield from row_steps(d, c8, tmp, [], 3)

    def half_ffn(nt, done_ctx, pre, sh, gates, s0):
        take = arena()
        T = 128 * nt
        hid = take(22, T)
        xn = hid.rearrange("p a b -> p (a b)")
        tmp = [take(512), take(512)]
        sl = [tmp_row[:, 0:T], tmp[1]]
        sc = scratch()
        Gr = [sc.ap[:, D * z:D * z + D] for z in range(len(gates))]
        nn = 2 if done_ctx else nt
        wait("v", [last("a")])
        t = rstd_x([(X[:, i, :], 128) for i in range(nn)], xn[:, 0:D])
        reg = []
        for z, p in enumerate(pre[:nn // 2]):
            reg.append((256 * z, 256 * z + 256, (lambda q, p=p: AB2[:, 8 * p + q:8 * p + q + 1]),
                        (lambda q, z=z: mcol2[:, sh * 8 + q, z:z + 1])))
        modulated_T([(X[:, i, :], 128, 16 + i, 128 * i) for i in range(nn)], reg, lambda i: xn[:, D * i:D * i + D], [t])
        join()
        sfree = [last("v")] * 2
        rows = row_all(Gr, gates, tmp[0])
        for p in range(11):
            bs = 4 * (p % 2)
            for q in range(2):
                w_ = S.get(s0 + 2 * p + q)
                for f in range(2):
                    b = bs + 2 * q + f
                    for kk in range(8):
                        e = mm3(PB[b][:, 0:T], (w_.H[:, kk, 128 * f:128 * f + 128], w_.L[:, kk, 128 * f:128 * f + 128]),
                                XT(kk, 0, T), kk == 0, kk == 7, w=[*w_.toks[kk // 4], bank[b]], inc=kk == 7)
                    if q == 0:
                        bank[b] = A(sl[f][:, 0:T], PB[b][:, 0:T], ACT.Silu, w=[e, sfree[f]])
                    else:
                        sfree[f] = bank[b] = V(tt, hid[:, 2 * p + f, :], sl[f][:, 0:T], PB[b][:, 0:T], ALU.mult,
                                               w=[e, bank[bs + f]])
                S.done(s0 + 2 * p + q, e)
            steps(rows, 1)
        t_g = last("a")
        es = rows_product(nt, 22, s0 + 22, [2 * i for i in range(nt)], lambda n: halves(hid[:, n, :], T, sfree), lambda i: 128 * i)
        post(nt, Gr, list(range(8)), tmp, es, t_g)
        sc.free = [last("v")]

    def second():
        if only and "first" not in only:
            for i, (l, c) in enumerate((("c", "c_ctx"), ("c_2", "c_ctx_2"))):
                A(cs[:, i, :, 0], col(l, 0, 8), ACT.Silu)
                A(cs[:, i, :, 1], col(c, 0, 8), ACT.Silu)
            wait("t", [last("a")])
            run(gemv(I["w_ada_2"][0], 1, "b_ada_2", 18, mcol2, 7))
            t_c2 = load_once(X[:, 2:4, :], I["ctx_2"].rearrange("a (t p) d -> p (a t) d", p=128))
            wait("v", [t_c2])
            wait("a", [t_c2])
            ctx_ahead(t_c2)
            barrier_all()
        half_ffn(4, True, (0, 1), 0, (AB2[:, 40:48], AB2[:, 48:56]), s_ffa)
        dump("ffa", X[:], [last("v")])
        mixer()
        dump("mix2", X[:, 0:2, :], [last("v")])
        half_ffn(2, False, (4,), 6, (AB2[:, 64:72],), s_ffb)
        dump("ffb", X[:, 0:2, :], [last("v")])

    def mixer():
        xn = big[:, 0:4096].rearrange("p (a b) -> p a b", a=4)
        m0, o0 = at["merge"], at["out"]
        t = rstd_x([(X[:, i, :], 128) for i in range(4)], xn[:, 0, :])
        modulated_T([(X[:, i, :], 128, 16 + i, 128 * i) for i in range(4)],
                    [(0, 256, lambda q: AB2[:, 16 + q:17 + q], lambda q: mcol2[:, 24 + q, 0:1]),
                     (256, 512, lambda q: AB2[:, 24 + q:25 + q], lambda q: mcol2[:, 24 + q, 1:2])],
                    lambda i: xn[:, i, :], [t])
        join()
        take = arena()
        yH, yL = (RB[:, z].rearrange("p a b -> p (a b)").rearrange("p (g t) -> p g t", g=4) for z in range(2))
        t_yf = [None]
        hmT = take(6, 256)
        gr = 512
        MM = take(gr, parts=36)
        dec = take(8, 4)
        gc = take(4, 4, 8)
        qT = [take(2, 256) for _ in range(2)]
        kT = [take(2, 512) for _ in range(2)]
        va = [take(4, 257) for _ in range(2)]
        sos = [take(2, 256) for _ in range(2)]
        hs = take(2, 256)
        C = [take(2, 257) for _ in range(2)]
        inter = [take(257) for _ in range(2)]
        pads = [take(2, 258) for _ in range(2)]
        tf = tmp_row
        kw = [tf[:, 0:256], tf[:, 256:512]]
        wT = [tf[:, 512:640], tf[:, 640:768]]
        sT = [tf[:, 768:896], tf[:, 896:1024]]
        bo = load(I["rows"][:, RO["b_v"]:RO["b_v"] + 2048], 2048)
        hg = load(I["rows"][:, RO["head_g"]:RO["head_g"] + 1536], 1536)
        for z in range(2):
            V(ve.memset, pads[z], 0.0)
            t_va = V(ve.memset, va[z], 1.0)
        order = [[2, 3, 0, 1], [3, 2, 1, 0]]
        seg = [slice(0, 4), slice(32, 36)]

        w_ = S.get(s_mix)
        for kk in range(8):
            e = mm3(PB[0][:, :], (w_.H[:, kk, :], w_.L[:, kk, :]), XT(kk, 0, 512), kk == 0, kk == 7,
                    w=[*w_.toks[kk // 4], bank[0]], inc=kk == 7)
        S.done(s_mix, e)
        sc1, sc2, sc3 = scratch(), scratch(), scratch()

        def row36(s, i):
            return s.ap[0:36, 512 * i:512 * i + 512]

        li, lf, bb, rr = (row36(sc1, i) for i in range(4))
        q_a, q_f, q_w, zz = (row36(sc2, i) for i in range(4))
        g16 = pads[0].rearrange("p a b -> p (a b)")[0:16, 0:512]
        small = BO[0:36, 0:32]
        t_pad = [None]
        first_head = []

        def gates():
            t = V(cp, g16, PB[0][0:16, :], w=[e])
            bank[0] = t
            mm(PB[2][0:36, :], k("sel_i")[0:16, :], g16, w=[t, bank[2]])
            e1 = mm(PB[3][0:36, :], k("sel_f")[0:16, :], g16, w=[t, bank[3]], inc=True)
            yield
            V(ts, li, PB[2][0:36, :], col("b_gate", 0)[0:36, :], None, ALU.add, w=[e1])
            bank[2] = bank[3] = V(ts, lf, PB[3][0:36, :], col("b_gate", 1)[0:36, :], None, ALU.add)
            t_pad[0] = V(ve.memset, pads[0], 0.0)
            V(ts, bb, lf, 0.0, None, ALU.min)
            t = V(stt, rr, bb, 2.0, lf, ALU.mult, ALU.subtract)
            V(ve.memset, sc2.ap[0:36, :], 0.0)
            t = A(rr, rr, ACT.Exp, w=[t])
            yield
            yield from log1p(rr, MM, q_a, q_f, [t])
            V(tt, lf, bb, q_f, ALU.subtract)

            def view(ap, d, blk):
                a = ap[seg[d], 128 * blk:128 * blk + 128]
                return a if d == 0 else a[:, ::-1]

            def endof(ap, d, blk):
                i = 128 * blk + (127 if d == 0 else 0)
                return ap[seg[d], i:i + 1]

            V(ve.memset, small, 0.0)
            for d in range(2):
                yield
                for blk in range(4):
                    V(ve.tensor_tensor_scan, view(bb, d, blk), view(lf, d, blk), view(zz, d, blk), 0.0, ALU.add, ALU.add)
            V(tt, rr, li, bb, ALU.subtract)
            for d in range(2):
                for n in range(4):
                    blk = order[d][n]
                    tc_ = slice(128 * blk, 128 * blk + 128)
                    m_0 = small[seg[d], n:n + 1]
                    V(ve.tensor_tensor_scan, view(MM, d, blk), view(rr, d, blk), view(rr, d, blk), m_0, ALU.max, ALU.max)
                    V(tt, small[seg[d], n + 1:n + 2], endof(bb, d, blk), endof(MM, d, blk), ALU.add)
                    V(tt, small[seg[d], 8 + n:9 + n], m_0, endof(MM, d, blk), ALU.subtract)
                    V(ts, q_w[seg[d], tc_], rr[seg[d], tc_], endof(MM, d, blk), None, ALU.subtract)
                    if n >= 2:
                        V(ts, q_a[seg[d], tc_], MM[seg[d], tc_], -1.0, m_0, ALU.mult, ALU.add)
                        V(stt, q_f[seg[d], tc_], bb[seg[d], tc_], -1.0, MM[seg[d], tc_], ALU.mult, ALU.subtract)
                    yield
            t = last("v")
            for d in range(2):
                s_ = seg[d]
                A(q_w[s_, :], q_w[s_, :], ACT.Exp, w=[t])
                A(q_a[s_, 0:256], q_a[s_, 0:256], ACT.Exp)
                A(q_f[s_, 0:256], q_f[s_, 0:256], ACT.Exp)
                t2 = A(small[s_, 8:12], small[s_, 8:12], ACT.Exp)
            while not first_head:
                yield
            dd = li[:, 0:32]
            t = V(tt, dd.rearrange("p (i n) -> p i n", i=8), small[:, None, 8:12].to_broadcast([36, 8, 4]),
                  k("m8")[0:36, :, None].to_broadcast([36, 8, 4]), ALU.mult, w=[t2])
            e1 = mm(PB[2][:, 0:32], ones[0:36, :], dd, w=[t, bank[2]], inc=True)
            at_ = 0
            place = []
            for qi, ap in enumerate((rr, q_w, q_a, q_f)):
                for blk in range(4 if qi == 1 else 2):
                    place.append((qi, blk, at_))
                    e2 = mm(PB[3][:, at_:at_ + 36], ap[:, 128 * blk:128 * blk + 128], ident[0:36, 0:36],
                            w=[t, bank[3]], inc=blk > 0)
                    at_ += 36
            bank[2] = V(cp, dec.rearrange("p i n -> p (i n)"), PB[2][:, 0:32], w=[e1])
            for qi, blk, x in place:
                t = V(cp, gc[:, qi, blk, :].rearrange("p (d i) -> p d i", d=2),
                      PB[3][:, x:x + 64].rearrange("p (d i) -> p d i", d=2)[:, :, 0:4], w=[e2])
            bank[3] = t
            sc1.free = sc2.free = [t, e2, t2]

        def fourier():
            zf = sc3.ap[:, 0:1024].rearrange("p (a b) -> p a b", a=2)
            m12 = sc3.ap[:, 1024:2048].rearrange("p (a b) -> p a b", a=2)
            for q in range(2):
                w_ = S.get(s_mix + 1 + q)
                for a in range(4):
                    for i in range(2):
                        e = mm3(PB[6 + i][:, :], XT(4 * q + a, 128 * i), (w_.H[:, a, :], w_.L[:, a, :]),
                                q + a == 0, 4 * q + a == 7, w=[*w_.toks[a // 2], bank[6 + i]], inc=True)
                S.done(s_mix + 1 + q, e)
                yield
            fr = load(I["four"], 1280)
            f1 = fr.ap[:, 0:1024].rearrange("p (i n) -> p i n", i=2)
            cc, ns = fr.ap[:, 1024:1152], fr.ap[:, 1152:1280]
            for i in range(2):
                t = V(tt, zf[:, i, :], PB[6 + i][:, :], hg.ap[:, 1024:1536], ALU.add, w=[e, hg.tok])
                bank[6 + i] = t
            for g in range(4):
                b = 6 + g % 2
                for i in range(2):
                    e = mm(PB[b][:, :], zf[:, i, 128 * g:128 * g + 128], f1[:, i, :], i == 0, i == 1, w=[t, fr.tok, bank[b]], inc=i == 1)
                ta = A(m12[:, g % 2, :], PB[b][:, :], ACT.Copy, w=[e, last("t")])
                yield
                mm(PB[b][:, 0:256], cc, m12[:, g % 2, 0:256], True, False, w=[ta])
                e = mm(PB[b][:, 0:256], ns, m12[:, g % 2, 256:512], False, True, inc=True)
                t_yf[0] = bank[b] = halves_of(PB[b][:, 0:256], yH[:, g, :], yL[:, g, :], [e, *rb_free])
                yield
            fr.free = [e]
            sc3.free = [e, last("v"), last("a")]

        tri = k("tri").rearrange("p (d t) -> p d t", d=2)
        ready = {}
        npad = [0]

        def conv(dst, src, e, ci, T):
            cw = lambda j: col("conv_w_2", 16 * j + ci)
            bname, bi = ("b_q", ci) if ci < 8 else ("b_k", ci - 8)
            P_ = pads[1][:, 0:T // 256, :] if npad[0] % 2 == 0 else pads[0][:, 0:T // 256, :]
            npad[0] += 1
            V(ts, P_[:, :, 1:257], src[:, 0:T].rearrange("p (z t) -> p z t", t=256), col(bname, bi), None, ALU.add, w=[e])
            t = last("v")
            O = dst.rearrange("p (z t) -> p z t", t=256)
            V(ts, O, P_[:, :, 0:256], cw(0), col("conv_b_2", ci), ALU.mult, ALU.add, w=[last("t")])
            V(stt, O, P_[:, :, 1:257], cw(1), O, ALU.mult, ALU.add)
            V(stt, O, P_[:, :, 2:258], cw(2), O, ALU.mult, ALU.add)
            return t

        def proj(h):
            z = h % 2
            if h < 4:
                for c0, dst, T, cb in ((CQ, qT[z], 256, 0), (CK, kT[z], 512, 8)):
                    w_ = S.get(at[(c0, h)])
                    for f in range(2):
                        for kk in range(8):
                            e = mm3(PB[f][:, 0:T], (w_.H[:, kk, 128 * f:128 * f + 128], w_.L[:, kk, 128 * f:128 * f + 128]),
                                    XT(kk, 0, T), kk == 0, kk == 7, w=[*w_.toks[kk // 4], bank[f]], inc=kk == 7)
                            if kk % 2 and kk < 7:
                                yield
                        bank[f] = conv(dst[:, f, :], PB[f], e, cb + 2 * h + f, T)
                        yield
                    S.done(at[(c0, h)], e)
                w_ = S.get(at[(CV, h)])
                for i in range(4):
                    b = i % 2
                    for kk in range(8):
                        e = mm3(PB[b][:, 0:256], XT(kk, 128 * i), (w_.H[:, kk, :], w_.L[:, kk, :]), kk == 0, kk == 7,
                                w=[*w_.toks[kk // 4], bank[b]], inc=kk == 7)
                        if kk == 3:
                            yield
                    bank[b] = V(tt, va[z][:, i, 0:256], PB[b][:, 0:256], bo.ap[:, 256 * h:256 * h + 256], ALU.add, w=[e, bo.tok])
                    yield
                S.done(at[(CV, h)], e)
            if h:
                so = sos[(h - 1) % 2]
                w_ = S.get(at[(CO_, h - 1)])
                for i in range(2):
                    for kk in range(8):
                        e = mm3(PB[i][:, 0:256], XT(kk, 128 * i), (w_.H[:, kk, :], w_.L[:, kk, :]), kk == 0, kk == 7,
                                w=[*w_.toks[kk // 4], bank[i]], inc=kk == 7)
                        if kk == 3:
                            yield
                    bank[i] = V(tt, so[:, i, :], PB[i][:, 0:256], bo.ap[:, 768 + 256 * h:1024 + 256 * h], ALU.add, w=[e])
                    yield
                S.done(at[(CO_, h - 1)], e)
            if h < 4:
                t = last("v")
                A(qT[z].rearrange("p a b -> p (a b)"), qT[z].rearrange("p a b -> p (a b)"), ACT.Silu, w=[t])
                ready[h] = [A(kT[z].rearrange("p a b -> p (a b)"), kT[z].rearrange("p a b -> p (a b)"), ACT.Silu), t]

        def finish(h):
            so = sos[h % 2]
            for i in range(2):
                t = A(inter[i][:, 0:256], hs[:, i, :], ACT.Square, accum_out=st[:, 52 + i:53 + i], w=[last("v")])
            yield
            rstd_of(52, 2, 256, t)
            yield
            A(so[:, 0, :], so[:, 0, :], ACT.Sigmoid, w=[last("v")])
            t_so = A(so[:, 1, :], so[:, 1, :], ACT.Sigmoid)
            yield
            for i in range(2):
                V(stt, hs[:, i, :], hs[:, i, :], st[:, 52 + i:53 + i], hg.ap[:, 256 * h:256 * h + 256], ALU.mult, ALU.mult, w=[hg.tok])
                t = V(tt, hs[:, i, :], hs[:, i, :], so[:, i, :], ALU.mult, w=[t_so])
                yield
                for f in range(2):
                    e = tp(PB[6 + i][:, 128 * f:128 * f + 128], hs[:, i, 128 * f:128 * f + 128], w=[t, bank[6 + i]], inc=f == 1)
                src = PB[6 + i][:, 0:256].rearrange("p (f t) -> p f t", f=2)
                c = 128 * i
                if h < 3:
                    bank[6 + i] = V(cp, hmT[:, 2 * h:2 * h + 2, c:c + 128], src, w=[e])
                else:
                    bank[6 + i] = halves_of(src, HH[:, 6:8, 256 + c:384 + c], HL[:, 6:8, 256 + c:384 + c], [e])

        def mlstm(h):
            z = h % 2
            fin = finish(h - 1) if h else iter(())
            tq = ready[h]
            q_, k_, v_ = qT[z], kT[z], va[z]
            for n in range(4):
                bl = [order[d][n] for d in range(2)]
                tc_ = [slice(128 * b, 128 * b + 128) for b in bl]
                S_, M_ = (2, 4), (3, 5)
                es = [None] * 2
                if n >= 2:
                    for d in range(2):
                        mm(PB[S_[d]][:, 0:128], k_[:, 0, tc_[d]], q_[:, 0, tc_[d]], True, False, w=[*tq, bank[S_[d]]])
                        mm(PB[S_[d]][:, 0:128], k_[:, 1, tc_[d]], q_[:, 1, tc_[d]], False, True)
                        es[d] = mm(PB[M_[d]][:, 0:128], k("m8")[0:36, 4 * d + h:4 * d + h + 1].to_broadcast([36, 128]), MM[:, tc_[d]],
                                   w=[bank[M_[d]]], inc=True)
                    steps(fin, 9)
                    yield
                    for d in range(2):
                        x = 4 * d + h
                        t = bank[M_[d]] = V(tt, wT[d], tri[:, d, :], PB[M_[d]][:, 0:128], ALU.subtract, w=[es[d]])
                        t = A(wT[d], wT[d], ACT.Exp, bias=gc[:, 0, bl[d], x:x + 1], w=[t])
                        es[d] = bank[S_[d]] = V(stt, sT[d], PB[S_[d]][:, 0:128], 0.0625, wT[d], ALU.mult, ALU.mult, w=[t, last("t")])
                if n < 3:
                    ks = [None] * 2
                    for d in range(2):
                        for f in range(2):
                            e = tp(PB[6 + d][:, 128 * f:128 * f + 128], k_[:, f, tc_[d]], w=[*tq, bank[6 + d]], inc=f == 1)
                        ks[d] = bank[6 + d] = V(ts, kw[d], PB[6 + d][:, 0:256], gc[:, 1, bl[d], 4 * d + h:4 * d + h + 1], 0.0625,
                                                ALU.mult, ALU.mult, w=[e])
                steps(fin, 1)
                yield
                if n >= 2:
                    for d in range(2):
                        mm(PB[S_[d]][:, 0:257], sT[d], v_[:, bl[d], :], w=[es[d], bank[S_[d]]])
                        mm(PB[M_[d]][:, 0:257], q_[:, 0, tc_[d]], C[d][:, 0, :], True, False, w=[t_C[d], bank[M_[d]]])
                        es[d] = mm(PB[M_[d]][:, 0:257], q_[:, 1, tc_[d]], C[d][:, 1, :], False, True, inc=True)
                if n < 3:
                    for d in range(2):
                        for f in range(2):
                            e = mm(PB[6 + f][:, 0:257], kw[d][:, 128 * f:128 * f + 128], v_[:, bl[d], :], w=[ks[d], bank[6 + f], ready[h][1]], inc=True)
                            if n == 0:
                                t_C[d] = V(cp, C[d][:, f, :], PB[6 + f][:, 0:257], w=[e])
                            else:
                                t_C[d] = V(stt, C[d][:, f, :], C[d][:, f, :], dec[:, 4 * d + h, n:n + 1], PB[6 + f][:, 0:257],
                                           ALU.mult, ALU.add, w=[e])
                            bank[6 + f] = t_C[d]
                        if d == 0:
                            steps(fin, 1)
                            yield
                steps(fin, 1)
                yield
                if n >= 2:
                    for d in range(2):
                        x, I_ = 4 * d + h, inter[d]
                        bank[M_[d]] = V(ts, I_, PB[M_[d]][:, 0:257], gc[:, 2, bl[d], x:x + 1], None, ALU.mult, w=[es[d]])
                        bank[S_[d]] = V(tt, I_, I_, PB[S_[d]][:, 0:257], ALU.add)
                        dn = st[:, 50 + d:51 + d]
                        V(stt, dn, I_[:, 256:257], -1.0, I_[:, 256:257], ALU.mult, ALU.max)
                        V(ts, dn, dn, gc[:, 3, bl[d], x:x + 1], None, ALU.max)
                        V(ve.reciprocal, dn, dn)
                        if n == 2:
                            V(ts, hs[:, bl[d], :], I_[:, 0:256], dn, None, ALU.mult, w=[last("t")])
                        else:
                            V(stt, hs[:, bl[d], :], I_[:, 0:256], dn, hs[:, bl[d], :], ALU.mult, ALU.add)

        t_C = [None, None]
        def others():
            yield from fourier()
            yield from proj(0)
            first_head.append(True)

        both(gates(), others())
        for h in range(4):
            both(mlstm(h), proj(h + 1), 3)
        halves_of(hmT[:, :, :], HH[:, 0:6, 256:512], HL[:, 0:6, 256:512], [last("v"), last("t")])
        take = arena(BIG - 1024)
        s1, s2 = [take(256) for _ in range(2)], [take(256) for _ in range(2)]

        def branches(p):
            for q in range(2):
                w_ = S.get(m0 + 4 * p + q)
                for f in range(2):
                    b = 4 * f + q
                    for kk in range(8):
                        e = mm3(PB[b][:, 0:256], (w_.H[:, kk, 128 * f:128 * f + 128], w_.L[:, kk, 128 * f:128 * f + 128]),
                                XT(kk, 0, 256), kk == 0, kk == 7, w=[*w_.toks[kk // 4], bank[b]], inc=kk == 7)
                        if kk == 3:
                            yield
                    bank[b] = A((s1, s2)[q][f], PB[b][:, 0:256], ACT.Sigmoid, bias=col(("b_gf", "b_gm")[q], 2 * p + f), w=[e, last("v")])
                    yield
                S.done(m0 + 4 * p + q, e)

        both(finish(3), branches(0))
        join()
        bo.free = hg.free = [last("v")]
        take = arena()
        yT = take(8, 256)
        tmp = [take(512), take(512)]
        Gr = take(D)
        rows = row_steps(Gr, AB2[:, 56:64], tmp[0], [], 2)
        for p in range(4):
            if p:
                run(branches(p))
            steps(rows, 1)
            for q, nk in ((2, 4), (3, 8)):
                w_ = S.get(m0 + 4 * p + q)
                for kk in range(nk):
                    src = (yH[:, kk, :], yL[:, kk, :]) if q == 2 else (HH[:, kk, 256:512], HL[:, kk, 256:512])
                    for f in range(2):
                        b = 4 * f + q
                        e = mm3(PB[b][:, 0:256], (w_.H[:, kk, 128 * f:128 * f + 128], w_.L[:, kk, 128 * f:128 * f + 128]),
                                src, kk == 0, kk == nk - 1, w=[*w_.toks[kk // (nk // 2)], bank[b]], inc=True)
                S.done(m0 + 4 * p + q, e)
                for f in range(2):
                    s_ = (s1, s2)[q - 2][f]
                    bank[4 * f + q] = V(tt, s_, s_, PB[4 * f + q][:, 0:256], ALU.mult, w=[e, last("a")])
            for f in range(2):
                t_y = V(tt, yT[:, 2 * p + f, :], s1[f], s2[f], ALU.add)
        rb_free[0] = rb_free[1] = e
        tg = last("a")
        es = rows_product(2, 8, o0, [4, 6], lambda kk: halves(yT[:, kk, :], 256, [t_y]), lambda i: 128 * i)
        post(2, [Gr], [4, 5, 6, 7], tmp, es, tg)

    def log1p(z, w_, w2, o, wt):
        V(ts, w_, z, 2.0, None, ALU.add, w=wt)
        V(ve.reciprocal, w_, w_)
        V(tt, w_, w_, z, ALU.mult)
        yield
        V(tt, w2, w_, w_, ALU.mult)
        V(ts, o, w2, 1.0 / 17, None, ALU.mult)
        for n in (15, 13, 11, 9, 7, 5, 3):
            V(stt, o, o, 1.0 / n, w2, ALU.add, ALU.mult)
            if n % 4 == 3:
                yield
        V(stt, o, o, 1.0, w_, ALU.add, ALU.mult)
        V(ts, o, o, 2.0, None, ALU.mult)

    TL = [(0, 128, 16), (1, 128, 144), (2, 16, 0)]
    T3 = 272

    def third():
        wait("s", [last("v"), last("a"), last("t"), last("g")])
        t_m = load_once(X[0:16, 2, :], I["meta_tokens_3"])
        for e in "va":
            wait(e, [t_m])
        def norm_T(gname, xnb):
            t = rstd_x([(X[0:n, i, :], n) for i, n, c in TL], xnb)
            modulated_T([(X[0:n, i, :], n, 16 + i, c) for i, n, c in TL],
                        [(0, T3, lambda q: col(gname, q), None)], lambda i: xnb[:, D * i:D * i + D], [t])
            join()

        def project(yT, s0, tls, prepare=lambda kk: None):
            w = [last("v"), last("a")]
            es = rows_product(len(tls), 8, s0, [2 * i for i, n, c in tls],
                              lambda kk: halves(yT[:, kk, :], T3, [*w, prepare(kk)]), lambda i: TL[i][2])
            for i, n, c in tls:
                for j in range(2):
                    b = 2 * i + j
                    x_tok[i] = bank[b] = V(tt, X[0:n, i, 512 * j:512 * j + 512], X[0:n, i, 512 * j:512 * j + 512], PB[b][0:n, :],
                                           ALU.add, w=[es[i]])

        x_tok[2] = None
        norm_T("a_norm", big[:, 0:3 * D])
        take = arena()
        pj = take(3, 704)
        qr = take(3, 512)
        kr = take(128)
        qlT = take(3, T3)
        kvT = take(2, T3)
        qrT = take(4, T3)
        krT = take(T3)
        vt = take(3, D)
        yT = take(8, T3)
        scr = take(2, 256)
        kn1 = take(T3)
        wu, wk = I["a_w_uq_3"][0], I["a_w_ukv_3"][0]
        wait("s", barrier())
        t_mask = load_once(tmp_row[:, 0:816], I["mask3"])
        mask = tmp_row[:, 0:816].rearrange("p (i t) -> p i t", i=3)
        for q in range(4):
            w_ = S.get(s_3 + q)
            for a in range(2):
                kk = 2 * q + a
                for i, n, c in TL:
                    for j, (c0, c1) in enumerate(((0, 384), (384, 704))):
                        e = mm3(PB[2 * i + j][:, 0:c1 - c0], XT(kk, c), (w_.H[:, a, c0:c1], w_.L[:, a, c0:c1]),
                                kk == 0, kk == 7, w=[*w_.toks[a], bank[2 * i + j]], inc=True)
            S.done(s_3 + q, e)
        for i, n, c in TL:
            bank[2 * i] = V(cp, pj[0:n, i, 0:384], PB[2 * i][0:n, 0:384], w=[e])
            bank[2 * i + 1] = A(pj[0:n, i, 384:704], PB[2 * i + 1][0:n, 0:320], ACT.Copy, w=[e])
        t_pj = [last("v"), last("a")]

        def gate():
            for p in range(4):
                w_ = S.get(s_3 + 4 + p)
                for f in range(2):
                    b = 6 + f
                    for kk in range(8):
                        e = mm3(PB[b][:, 0:T3], (w_.H[:, kk, 128 * f:128 * f + 128], w_.L[:, kk, 128 * f:128 * f + 128]),
                                XT(kk, 0, T3), kk == 0, kk == 7, w=[*w_.toks[kk // 4], bank[b]], inc=kk == 7)
                    bank[b] = A(yT[:, 2 * p + f, :], PB[b][:, 0:T3], ACT.Silu, w=[e])
                    yield
                S.done(s_3 + 4 + p, e)

        r3 = k("rope3").rearrange("p (i c d) -> p i c d", i=3, c=2)

        def latents():
            junk = qr.rearrange("p a b -> p (a b)")
            for i, n, c in TL:
                for z, (c0, c1) in enumerate(((0, 384), (384, 640))):
                    t = A(junk[0:n, c0:c1], pj[0:n, i, c0:c1], ACT.Square, accum_out=st[0:n, 2 * i + z:2 * i + z + 1], w=t_pj)
            s6 = st[:, 0:6].rearrange("p (i c) -> p i c", c=2)
            V(ts, s6[:, :, 0], s6[:, :, 0], 1.0 / 384, 1e-6, ALU.mult, ALU.add, w=[t])
            t = V(ts, s6[:, :, 1], s6[:, :, 1], 1.0 / 256, 1e-6, ALU.mult, ALU.add)
            t = A(st[:, 0:6], st[:, 0:6], ACT.Sqrt, w=[t])
            V(ve.reciprocal, st[:, 0:6], st[:, 0:6], w=[t])
            for i, n, c in TL:
                V(ts, pj[0:n, i, 0:384], pj[0:n, i, 0:384], st[0:n, 2 * i:2 * i + 1], None, ALU.mult)
                V(ts, pj[0:n, i, 384:640], pj[0:n, i, 384:640], st[0:n, 2 * i + 1:2 * i + 2], None, ALU.mult)
            yield
            t = last("v")
            for q in range(5):
                b = q % 2
                for i, n, c in TL:
                    e = tp(PB[b][:, c:c + n], pj[0:n, i, 128 * q:128 * q + 128], w=[t, bank[b]], inc=True)
                dst, g = (qlT[:, q, :], col("a_qn", q)) if q < 3 else (kvT[:, q - 3, :], col("a_kvn", q - 3))
                bank[b] = V(ts, dst, PB[b][:, 0:T3], g, None, ALU.mult, w=[e])
                if q % 2:
                    yield
            for i, n, c in TL:
                for z in range(2):
                    t = rope(kr[0:n, 64 * z:64 * z + 32], kr[0:n, 64 * z + 32:64 * z + 64], pj[0:n, i, 640:672],
                             pj[0:n, i, 672:704], r3[0:n, i, 0, :], r3[0:n, i, 1, :], [scr[0:n, 0, 0:32], scr[0:n, 1, 0:32]],
                             [last("t")] if z == 0 else [])
                e = tp(PB[2][:, c:c + n], kr[0:n, :], w=[t, bank[2]], inc=True)
                yield
            bank[2] = V(cp, krT, PB[2][:, 0:T3], w=[e])
            for i, n, c in TL:
                b = 3 + i
                for q in range(3):
                    e = mm(PB[b][0:n, :].rearrange("p (h d) -> p h d", h=8), qlT[:, q, c:c + n],
                           uq[q].ap.rearrange("p (h d) -> p h d", h=8)[:, :, 128:192], q == 0, q == 2,
                           w=[uq[q].tok, last("v"), bank[b]], inc=q == 2)
                yield
                bank[b] = V(cp, qr[0:n, i, :], PB[b][0:n, :], w=[e])
                a = qr[0:n, i, :].rearrange("p (h c d) -> p c h d", c=2, d=32)
                o = pj[0:n, i, 0:512].rearrange("p (h c d) -> p c h d", c=2, d=32)
                t = rope(o[:, 0], o[:, 1], a[:, 0], a[:, 1], r3[0:n, i, 0, None, :].to_broadcast([n, 8, 32]),
                         r3[0:n, i, 1, None, :].to_broadcast([n, 8, 32]),
                         [scr[0:n, 0, :].rearrange("p (h d) -> p h d", h=8), scr[0:n, 1, :].rearrange("p (h d) -> p h d", h=8)], [])
                yield
            for q in range(4):
                b = q % 2
                for i, n, c in TL:
                    e = tp(PB[b][:, c:c + n], pj[0:n, i, 128 * q:128 * q + 128], w=[t, bank[b]], inc=True)
                bank[b] = V(cp, qrT[:, q, :], PB[b][:, 0:T3], w=[e])
                yield

        uq = [load(wu[128 * q:128 * q + 128, :], 1536) for q in range(3)]
        lat, gat = latents(), gate()
        steps(lat, 1)
        steps(gat, 2)
        both(gat, lat, 2)
        uk = [load(wk[128 * q:128 * q + 128, :], 2048) for q in range(2)]
        for i, n, c in TL:
            for j in range(2):
                b = 4 + (2 * i + j) % 4
                for q in range(2):
                    e = mm(PB[b][0:n, :].rearrange("p (h d) -> p h d", h=4), kvT[:, q, c:c + n],
                           uk[q].ap.rearrange("p (h z d) -> p h z d", h=8, z=2)[:, 4 * j:4 * j + 4, 1, :], q == 0, q == 1,
                           w=[uk[q].tok, last("v"), bank[b]], inc=q == 1)
                bank[b] = A(vt[0:n, i, 512 * j:512 * j + 512], PB[b][0:n, :], ACT.Copy, w=[e])
        wait("v", [last("t"), last("a"), t_mask])
        wait("a", [last("t"), last("v")])
        qf, pf = qr.rearrange("p a b -> p (a b)"), pj.rearrange("p a b -> p (a b)")
        prob = [qf[:, 0:816].rearrange("p (i t) -> p i t", i=3), pf[:, 0:816].rearrange("p (i t) -> p i t", i=3)]
        pT = pf[:, 816:1632].rearrange("p (i t) -> p i t", i=3)
        qn = [qf[:, 816:1088], scr.rearrange("p a b -> p (a b)")[:, 0:T3]]
        kn = [qf[:, 1088:1360], kn1]
        SC = float(192) ** -0.5
        t_B = [None] * 8

        def keys(h):
            z = h % 2
            for (dst, src, nk, b) in ((qn[z], qlT, 3, 0), (kn[z], kvT, 2, 1)):
                for q in range(nk):
                    wa = uq[q].ap[:, 192 * h:192 * h + 128] if b == 0 else uk[q].ap[:, 256 * h:256 * h + 128]
                    e = mm(PB[b][:, 0:T3], wa, src[:, q, :], q == 0, q == nk - 1, w=[bank[b]], inc=q == nk - 1)
                bank[b] = A(dst, PB[b][:, 0:T3], ACT.Copy, w=[e])

        def scores(h):
            z = h % 2
            r = 64 * (h % 2)
            es = []
            for i, n, c in TL:
                b = 2 + i
                mm(PB[b][0:n, 0:T3], qn[z][:, c:c + n], kn[z], True, False, w=[bank[0], bank[1], bank[b]])
                es.append(mm(PB[b][0:n, 0:T3], qrT[r:r + 64, h // 2, c:c + n], krT[r:r + 64, :], False, True, inc=True))
            for (i, n, c), e in zip(TL, es):
                b, p = 2 + i, prob[z][0:n, i, :]
                bank[b] = V(stt, p, PB[b][0:n, 0:T3], SC, mask[0:n, i, :], ALU.mult, ALU.add, w=[e, t_B[h - 2] if h > 1 else None])
                mx = st[0:n, 40 + i:41 + i]
                V(ve.tensor_reduce, mx, p, AX, ALU.max)
                t = V(ts, mx, mx, -1.0, None, ALU.mult)
                ta = A(p, p, ACT.Exp, bias=mx, accum_out=st[0:n, 44 + i:45 + i], w=[t])
            for i, n, c in TL:
                p = prob[z][0:n, i, :]
                V(ve.reciprocal, st[0:n, 44 + i:45 + i], st[0:n, 44 + i:45 + i], w=[ta])
                t = V(ts, p, p, st[0:n, 44 + i:45 + i], None, ALU.mult)
            return t

        PL = {0: (5, 0), 1: (5, 256), 2: (6, 0)}

        def turned(h, t):
            z = h % 2
            for ki, kn_, kc in TL:
                b, o = PL[ki]
                for i, n, c in TL:
                    if c >= kc:
                        e = tp(PB[b][0:kn_, o + c - kc:o + c - kc + n], prob[z][0:n, i, kc:kc + kn_], w=[t, bank[b]], inc=True)
            for ki, kn_, kc in TL:
                b, o = PL[ki]
                bank[b] = ta = A(pT[0:kn_, ki, kc:T3], PB[b][0:kn_, o:o + T3 - kc], ACT.Copy, w=[e])
            t_B[h] = e
            return ta

        def values(h, t):
            for y, (ki, kn_, kc) in enumerate((TL[2], TL[0], TL[1])):
                e = mm(PB[7][:, kc:T3], vt[0:kn_, ki, 128 * h:128 * h + 128], pT[0:kn_, ki, kc:T3], y == 0, y == 2,
                       w=[t, bank[7]], inc=y == 2)
            bank[7] = V(tt, yT[:, h, :], PB[7][:, 0:T3], yT[:, h, :], ALU.mult, w=[e])
            wait("a", [e])

        keys(0)
        t = scores(0)
        for h in range(8):
            if h < 7:
                keys(h + 1)
            ta = turned(h, t)
            if h < 7:
                t = scores(h + 1)
            values(h, ta)
        for s in uq + uk:
            s.free = [last("t")]
        dump("yT3", yT, [last("v")])
        project(yT, s_3 + 8, TL)
        dump("mla", X[:, 0:2, :], [last("v")])

        norm_T("b_norm", big[:, 0:3 * D])
        take = arena()
        uT = take(8, T3)
        gT = take(8, T3)
        pad = [take(T3 + 3) for _ in range(2)]
        al = take(8, T3)
        ml = take(8, T3)
        bl = take(8, T3)
        sp = take(8)
        z8 = take(3, 8)
        l8 = take(8)
        lam = col("lam", 0, 8)
        V(ts, sp, lam, 0.0, None, ALU.min)
        t = V(stt, z8[:, 0, :], sp, 2.0, lam, ALU.mult, ALU.subtract)
        t = A(z8[:, 0, :], z8[:, 0, :], ACT.Exp, w=[t])
        run(log1p(z8[:, 0, :], z8[:, 1, :], z8[:, 2, :], l8, [t]))
        V(tt, sp, l8, sp, ALU.subtract)
        V(ts, sp, sp, -8.0, None, ALU.mult)
        V(ve.memset, pad[0][:, 0:3], 0.0)
        V(ve.memset, pad[1][:, 0:3], 0.0)
        for p in range(4):
            for q in range(2):
                w_ = S.get(s_3 + 12 + 2 * p + q)
                for f in range(2):
                    o = 2 * p + f
                    b = 4 * (p % 2) + 2 * q + f
                    for kk in range(8):
                        e = mm3(PB[b][:, 0:T3], (w_.H[:, kk, 128 * f:128 * f + 128], w_.L[:, kk, 128 * f:128 * f + 128]),
                                XT(kk, 0, T3), kk == 0, kk == 7, w=[*w_.toks[kk // 4], bank[b]], inc=kk == 7)
                    if q == 0:
                        P_ = pad[f]
                        bank[b] = V(cp, P_[:, 3:3 + T3], PB[b][:, 0:T3], w=[e])
                        V(ts, uT[:, o, :], P_[:, 0:T3], col("conv_w_3", o), col("conv_b_3", o), ALU.mult, ALU.add)
                        for j in range(1, 4):
                            V(stt, uT[:, o, :], P_[:, j:j + T3], col("conv_w_3", 8 * j + o), uT[:, o, :], ALU.mult, ALU.add)
                    else:
                        bank[b] = A(gT[:, o, :], PB[b][:, 0:T3], ACT.Silu, w=[e])
                S.done(s_3 + 12 + 2 * p + q, e)
        t_u = last("v")
        tq = [None] * 4
        ws = [S.get(s_3 + 20, False), S.get(s_3 + 21, False)]
        uh = [(HH[:, o, 0:T3], HL[:, o, 0:T3]) for o in range(8)]
        t_uh = [halves_of(uT[:, o:o + 2, :], HH[:, o:o + 2, 0:T3], HL[:, o:o + 2, 0:T3], [t_u, e]) for o in range(0, 8, 2)]
        for g in range(4):
            for f in range(2):
                o = 2 * g + f
                for q in range(2):
                    b = 4 * (g % 2) + 2 * f + q
                    for kk in range(2):
                        e = mm3(PB[b][:, 0:T3], (ws[q].H[:, g, kk, 128 * f:128 * f + 128], ws[q].L[:, g, kk, 128 * f:128 * f + 128]),
                                uh[2 * g + kk], kk == 0, kk == 1, w=[*ws[q].toks[0], *ws[q].toks[1], t_uh[g], bank[b]], inc=kk == 1)
                    bank[b] = A((al, bl)[q][:, o, :], PB[b][:, 0:T3], ACT.Sigmoid, bias=col(("b_rg", "b_ig")[q], o), w=[e])
            t = last("a")
            g2_ = slice(2 * g, 2 * g + 2)
            for o in (2 * g, 2 * g + 1):
                t = V(ts, al[:, o, :], al[:, o, :], sp[:, o:o + 1], None, ALU.mult, w=[t])
            A(ml[:, g2_, :], al[:, g2_, :], ACT.Tanh, w=[t])
            V(tt, bl[:, g2_, :], bl[:, g2_, :], uT[:, g2_, :], ALU.mult)
        for q in range(2):
            S.done(s_3 + 20 + q, e)
        pairs = [slice(o, o + 2) for o in range(0, 8, 2)]
        t = last("v")
        for g, p in enumerate(pairs):
            t = A(uT[:, p, :], al[:, p, :], ACT.Exp, scale=2.0, w=[t])
            tq[g] = V(stt, uT[:, p, :], uT[:, p, :], 1.0, ml[:, p, :], ALU.add, ALU.mult, w=[t])
        te = [A(al[:, p, :], al[:, p, :], ACT.Exp) for p in pairs]
        S.ahead()
        for g, p in enumerate(pairs):
            tq[g] = A(ml[:, p, :], uT[:, p, :], ACT.Sqrt, scale=-1.0, w=[tq[g]])

        def recur(o):
            if o % 2 == 0:
                V(ve.memset, ml[:, o:o + 2, 0:1], 1.0, w=[tq[o // 2]])
                V(tt, bl[:, o:o + 2, :], bl[:, o:o + 2, :], ml[:, o:o + 2, :], ALU.mult)
            V(ve.tensor_tensor_scan, ml[:, o, :], al[:, o, :], bl[:, o, :], 0.0, ALU.mult, ALU.add, w=[te[o // 2]])
            return V(tt, gT[:, o, :], gT[:, o, :], ml[:, o, :], ALU.mult)

        project(gT, s_3 + 22, TL[0:2], recur)
        fg = load(I["rows"][:, RO["final_g"]:RO["final_g"] + 1024], 1024)
        t = rstd_x([(X[:, i, :], 128) for i in range(2)], uT.rearrange("p a b -> p (a b)"))
        for i in range(2):
            t = V(stt, X[:, i, :], X[:, i, :], st[:, 16 + i:17 + i], fg.ap, ALU.mult, ALU.mult, w=[fg.tok])
        fg.free = [t]
        store(out.rearrange("a (t p) d -> p (a t) d", p=128), X[:, 0:2, :], [t])

    if only and "first" not in only:
        for t in load_x():
            for e in "vas":
                wait(e, [t])
    for nm, fn in (("first", first), ("second", second), ("third", third)):
        if only is None or nm in only:
            fn()
    for s in stores:
        nc.sync.wait_ge(s, 16)


WEIGHTS = ["x", "ctx", "w_mod", "w_in", "w_out", "w_router", "w1", "w3", "w2", "ctx_2", "w_ada_2", "w13_a_2", "w2_a_2",
           "w_in_2", "w_four_2", "w_mproj_2", "w_out_2", "w13_b_2", "w2_b_2", "meta_tokens_3", "a_w_in_3", "a_w_uq_3",
           "a_w_ukv_3", "a_w_out_3", "b_w_in_3", "b_w_rg_3", "b_w_ig_3", "b_w_out_3"]


def constants():
    f = np.float32
    K = {n: np.zeros((128, w), f) for n, w in CONSTS}
    K["ident"][:] = np.eye(128)
    K["ones"][:] = 1
    inv = (f(10000.0) ** (-np.arange(16, dtype=f) / f(16))).astype(f)
    tok = np.arange(256)
    ang = np.concatenate([(tok // 64).astype(f)[:, None] * inv, (tok % 64).astype(f)[:, None] * inv], 1).astype(f)
    K["rope1"][:] = np.stack([np.cos(ang), np.sin(ang)], 1).reshape(2, 128, 64).transpose(1, 0, 2).reshape(128, 128)
    inv = (f(10000.0) ** (-np.arange(0, 64, 2, dtype=f) / f(64))).astype(f)
    r3 = np.zeros((128, 3, 2, 32), f)
    for i, n, c in ((0, 128, 16), (1, 128, 144), (2, 16, 0)):
        a = (np.arange(c, c + n, dtype=f)[:, None] * inv).astype(f)
        r3[:n, i, 0], r3[:n, i, 1] = np.cos(a), np.sin(a)
    K["rope3"][:] = r3.reshape(128, 192)
    K["slot"][:] = np.arange(1, 33)
    s, t = np.arange(128)[:, None], np.arange(128)[None, :]
    K["tri"][:] = np.concatenate([np.where(s <= t, 0, NEG), np.where(s >= t, 0, NEG)], 1)
    for i in range(8):
        p = 32 * (i // 4) + i % 4
        K["m8"][p, i] = 1
        K["sel_i"][8 * (i // 4) + i % 4, p] = 1
        K["sel_f"][8 * (i // 4) + 4 + i % 4, p] = 1
    consts = np.concatenate([K[n] for n, _ in CONSTS], 1)
    mask = np.full((128, 3, 272), NEG, f)
    for i, n, c in ((0, 128, 16), (1, 128, 144), (2, 16, 0)):
        mask[:n, i] = np.where(np.arange(272)[None, :] <= np.arange(c, c + n)[:, None], 0, NEG)
    r, w = np.arange(256) // 64, np.arange(256) % 64
    th = 2 * np.pi * (np.outer(r, r) / 4 + np.outer(w, w) / 64)
    ct = np.concatenate([np.cos(th), np.sin(th)], 1).reshape(2, 128, 512).transpose(1, 0, 2).reshape(128, 1024)
    pc = 2 * np.pi * np.outer(np.arange(128), np.arange(128)) / 128
    nrm = 1 / np.sqrt(256 * 128)
    four = np.concatenate([ct, np.cos(pc) * nrm, -np.sin(pc) * nrm], 1).astype(f)
    return {"consts": consts, "mask3": mask.reshape(128, 816), "four": four}


def layout(I):
    def c(v):
        v = np.asarray(v).reshape(-1)
        return v.reshape(-1, 128).T
    b_in = np.asarray(I["b_in_2"])[0]
    gate = np.zeros((128, 2), b_in.dtype)
    for d in range(2):
        for q in range(2):
            gate[32 * d:32 * d + 4, q] = b_in[4608 + 8 * d + 4 * q:4612 + 8 * d + 4 * q]
    parts = {"c": c(I["c"]), "c_ctx": c(I["c_ctx"]), "b_mod": c(I["b_mod"]), "g_mix": c(I["g_mix"]),
             "g_ffn": c(I["g_ffn"]), "c_2": c(I["c_2"]), "c_ctx_2": c(I["c_ctx_2"]), "b_ada_2": c(I["b_ada_2"]),
             "norm_g_2": c(I["norm_g_2"]), "b_q": c(b_in[512:1536]), "b_k": c(b_in[1536:2560]),
             "b_gf": c(b_in[4624:5648]), "b_gm": c(b_in[5648:6672]), "conv_w_2": c(I["conv_w_2"]),
             "conv_b_2": c(I["conv_b_2"]), "b_s": np.asarray(I["b_s"])[0].T, "a_norm": c(I["a_norm_g_3"]),
             "a_qn": c(I["a_q_norm_g_3"]), "a_kvn": c(I["a_kv_norm_g_3"]), "b_norm": c(I["b_norm_g_3"]),
             "conv_w_3": c(I["b_conv_w_3"]), "conv_b_3": c(I["b_conv_b_3"]), "b_rg": c(I["b_b_rg_3"]),
             "b_ig": c(I["b_b_ig_3"]), "lam": c(I["b_lam_3"]), "b_gate": gate}
    cols = np.concatenate([parts[n] for n, _ in COLS], 1)
    rows = {"q_gain": np.tile(np.asarray(I["q_gain"])[0], 8), "k_gain": np.tile(np.asarray(I["k_gain"])[0], 2),
            "v_gain": np.asarray(I["v_gain"])[0], "g_final": I["g_final"], "b_f": b_in[0:512], "b_v": b_in[2560:3584],
            "b_o": b_in[3584:4608], "head_g": np.asarray(I["head_g_2"])[0], "final_g": I["final_norm_g_3"]}
    row = np.concatenate([np.asarray(rows[n]) for n, _ in ROWS])
    return {"cols": np.ascontiguousarray(cols), "rows": np.ascontiguousarray(np.broadcast_to(row, (128, NROW))),
            "w_sT": np.ascontiguousarray(np.asarray(I["w_s"])[0].transpose(2, 0, 1).reshape(128, 1024))}


def arrays_of(inputs):
    out = {n: np.ascontiguousarray(inputs[n]) for n in WEIGHTS}
    out.update(layout(inputs))
    out.update(constants())
    return out


def kernel(**inputs):
    import concourse.bacc as _bacc
    from concourse.bass_utils import run_bass_kernel_spmd as _run

    nc = _bacc.Bacc("TRN2", target_bir_lowering=False, num_devices=1)
    arrays, I = {}, {}
    for name, a in arrays_of(inputs).items():
        arrays[f"in_{name}"] = a
        I[name] = nc.dram_tensor(f"in_{name}", a.shape, mybir.dt.from_np(a.dtype), kind="ExternalInput").ap()
    o = nc.dram_tensor("out_0", (1, 256, D), F32, kind="ExternalOutput").ap()
    build(nc, I, o)
    r = _run(nc, [arrays], core_ids=[0])
    return r.results[0]["out_0"]
```
